# Optimizing a Trainium2 kernel written in Bass

```python
import functools
import jax
import jax.numpy as jnp
from jax import lax
import numpy as np

D_MODEL = 1024
BATCH = 1
SEQ = 512
DEPTH = 2
DEC_BATCH = 8
DEC_SEQ = 1
PAST_LEN = 1024
PAGE_SIZE = 128

N_PAGES = PAST_LEN // PAGE_SIZE

RG_WIDTH = D_MODEL
RG_BLOCKS = 8
RG_BLOCK_W = RG_WIDTH // RG_BLOCKS
RG_CONV_W = 4
RG_C = 8.0
GLA_HEADS = 4
GLA_DK = D_MODEL // (2 * GLA_HEADS)
GLA_DV = D_MODEL // GLA_HEADS
GLA_RANK = 16
GLA_TAU = 16.0
GLA_CHUNK = 64
NSA_HEADS = 16
NSA_KV_HEADS = 4
NSA_HPG = NSA_HEADS // NSA_KV_HEADS
NSA_DH = D_MODEL // NSA_HEADS
CMP_BLOCK = 32
CMP_STRIDE = 16
CMP_RATIO = CMP_BLOCK // CMP_STRIDE
SEL_BLOCK = 64
TOP_N = 16
WINDOW = 512
NSA_Q_BLOCK = 64
D_FF = ((8 * D_MODEL + 3 * 256 - 1) // (3 * 256)) * 256

KV_W = 2 * NSA_KV_HEADS * NSA_DH
IN_SIZES = (RG_WIDTH, RG_WIDTH,
            GLA_HEADS * GLA_DK, GLA_HEADS * GLA_DK, GLA_HEADS * GLA_DV, GLA_HEADS * GLA_DV, GLA_RANK,
            NSA_HEADS * NSA_DH, KV_W, KV_W, KV_W, 3 * NSA_HEADS,
            3 * D_MODEL)
D_IN = sum(IN_SIZES)

EPS = 1e-6
NEG = -1e30
TINY = 1e-30
FORCE_SCORE = 1e4

kernel_name = 'hybrid_rglru_gla_nsa_decoder_step'

def split_cols(z):
    outs, start = [], 0
    for n in IN_SIZES:
        outs.append(z[..., start:start + n])
        start += n
    return outs

def rms_norm(x, g):
    xf = x.astype(jnp.float32)
    y = xf * lax.rsqrt(jnp.mean(xf * xf, axis=-1, keepdims=True) + EPS)
    return (y * g.astype(jnp.float32)).astype(x.dtype)

def norm_keys(kv, g):
    return jnp.stack([rms_norm(kv[:, :, 0], g), kv[:, :, 1]], axis=2)

def masked_softmax(s, mask):
    s = jnp.where(mask, s.astype(jnp.float32), NEG)
    m = jnp.max(s, axis=-1, keepdims=True)
    e = jnp.where(mask, jnp.exp(s - m), 0.0)
    return e / jnp.maximum(jnp.sum(e, axis=-1, keepdims=True), TINY)

def alibi_slopes():
    h = jnp.arange(1, NSA_HEADS + 1, dtype=jnp.float32)
    return (2.0 ** (-8.0 * h / NSA_HEADS)).reshape(NSA_KV_HEADS, NSA_HPG)

def causal_conv(x, buf, w, b):
    T = x.shape[1]
    xp = jnp.concatenate([buf.astype(x.dtype), x], axis=1)
    y = b
    for j in range(RG_CONV_W):
        y = y + xp[:, j:j + T] * w[j]
    return y, xp[:, -(RG_CONV_W - 1):]

def rglru(x, h0, w_a, b_a, w_x, b_x, lam):
    B, T, C = x.shape
    f32 = jnp.float32
    xf = x.astype(f32)
    xb = xf.reshape(B, T, RG_BLOCKS, RG_BLOCK_W)
    rec = jax.nn.sigmoid(jnp.einsum('btnc,ncd->btnd', xb, w_a.astype(f32)).reshape(B, T, C) + b_a.astype(f32))
    inp = jax.nn.sigmoid(jnp.einsum('btnc,ncd->btnd', xb, w_x.astype(f32)).reshape(B, T, C) + b_x.astype(f32))
    log_a = -RG_C * rec * jax.nn.softplus(-lam.astype(f32))
    a = jnp.exp(log_a)
    u = jnp.sqrt(-jnp.expm1(2.0 * log_a)) * (inp * xf)
    u = u.at[:, 0].add(a[:, 0] * h0.astype(f32))

    def combine(left, right):
        a1, b1 = left
        a2, b2 = right
        return a1 * a2, a2 * b1 + b2

    _, h = lax.associative_scan(combine, (a, u), axis=1)
    return h.astype(x.dtype), h[:, -1]

def gla_recurrent(q, k, v, log_g, s0):
    B, T, H, DK = q.shape
    f32 = jnp.float32
    C = min(GLA_CHUNK, T)
    n_ch = -(-T // C)
    pad = n_ch * C - T

    def prep(a):
        a = jnp.pad(a.astype(f32), ((0, 0), (0, pad), (0, 0), (0, 0)))
        return a.reshape(B, n_ch, C, H, a.shape[-1]).transpose(1, 0, 3, 2, 4)

    causal = jnp.tril(jnp.ones((C, C), dtype=bool))

    def step(S, inp):
        qc, kc, vc, gc = inp
        b = jnp.cumsum(gc, axis=2)
        diff = b[:, :, :, None, :] - b[:, :, None, :, :]
        decay = jnp.exp(jnp.where(causal[:, :, None], diff, -jnp.inf))
        A = jnp.einsum('bhtd,bhsd,bhtsd->bhts', qc, kc, decay)
        o = jnp.einsum('bhts,bhsv->bhtv', A, vc) + jnp.einsum('bhtd,bhdv->bhtv', qc * jnp.exp(b), S)
        b_last = b[:, :, -1]
        S = jnp.exp(b_last)[..., None] * S + jnp.einsum(
            'bhsd,bhsv->bhdv', kc * jnp.exp(b_last[:, :, None] - b), vc)
        return S, o

    S, o = lax.scan(step, s0.astype(f32), (prep(q), prep(k), prep(v), prep(log_g)))
    o = o.transpose(1, 0, 3, 2, 4).reshape(B, n_ch * C, H, -1)[:, :T]
    return o, S

def compress(rows, phi, pe):
    B, L = rows.shape[:2]
    n_chunk = L // CMP_STRIDE
    n_cmp = n_chunk - CMP_RATIO + 1
    ch = rows[:, :n_chunk * CMP_STRIDE].reshape(B, n_chunk, CMP_STRIDE, NSA_KV_HEADS, NSA_DH)
    out = 0.0
    for r in range(CMP_RATIO):
        sl = slice(r * CMP_STRIDE, (r + 1) * CMP_STRIDE)
        part = jnp.einsum('bnsgd,sde->bnge', ch + pe[sl][:, None, :], phi[sl])
        out = out + part[:, r:r + n_cmp]
    return out

def compressed_keys(cmp_kv, lw):
    kc = rms_norm(compress(cmp_kv[:, :, 0], lw['phi_k'], lw['cmp_pe'][0]), lw['k_norm'][0])
    vc = compress(cmp_kv[:, :, 1], lw['phi_v'], lw['cmp_pe'][1])
    c_end = jnp.arange(kc.shape[1]) * CMP_STRIDE + (CMP_BLOCK - 1)
    return kc, vc, c_end

def cmp_to_sel(n_cmp, n_sel):
    start = jnp.arange(n_cmp)[:, None] * CMP_STRIDE
    sel = jnp.arange(n_sel)[None, :] * SEL_BLOCK
    return ((start < sel + SEL_BLOCK) & (start + CMP_BLOCK > sel)).astype(jnp.float32)

def nsa_attend(q, q_pos, kc, vc, c_end, n_sel, fetch, k_win, v_win, w_pos, gates, slopes):
    f32 = jnp.float32
    sl = slopes[None, :, :, None, None]
    s = jnp.einsum('bqgpd,bngd->bgpqn', q, kc).astype(f32)
    dist = (q_pos[:, None] - c_end[None, :]).astype(f32)
    p_cmp = masked_softmax(s - sl * dist, c_end[None, :] <= q_pos[:, None])
    o_cmp = jnp.einsum('bgpqn,bngd->bqgpd', p_cmp.astype(vc.dtype), vc)
    imp = jnp.einsum('bgpqn,nj->bgqj', p_cmp, cmp_to_sel(kc.shape[1], n_sel))
    j = jnp.arange(n_sel)[None, :]
    cur = (q_pos // SEL_BLOCK)[:, None]
    valid = j <= cur
    forced = (j == 0) | (j == cur) | (j == cur - 1)
    score = jnp.where(valid, jnp.where(forced, FORCE_SCORE, imp), NEG)
    _, idx = lax.top_k(score, min(TOP_N, n_sel))
    Bq, G, Q, n = idx.shape
    kg, vg = fetch(idx)
    kg = kg.reshape(Bq, G, Q, n * SEL_BLOCK, NSA_DH)
    vg = vg.reshape(Bq, G, Q, n * SEL_BLOCK, NSA_DH)
    k_pos = (idx[..., None] * SEL_BLOCK + jnp.arange(SEL_BLOCK)).reshape(Bq, G, Q, n * SEL_BLOCK)
    s = jnp.einsum('bqgpd,bgqkd->bgpqk', q, kg).astype(f32)
    dist = (q_pos[None, None, :, None] - k_pos)[:, :, None]
    p = masked_softmax(s - sl * dist.astype(f32), dist >= 0)
    o_slc = jnp.einsum('bgpqk,bgqkd->bqgpd', p.astype(vg.dtype), vg)
    s = jnp.einsum('bqgpd,bwgd->bgpqw', q, k_win).astype(f32)
    dist = q_pos[:, None] - w_pos[None, :]
    mask = (dist >= 0) & (dist <= WINDOW) & (w_pos[None, :] >= 0)
    p = masked_softmax(s - sl * dist.astype(f32), mask)
    o_win = jnp.einsum('bgpqw,bwgd->bqgpd', p.astype(v_win.dtype), v_win)
    return gates[..., 0:1] * o_cmp + gates[..., 1:2] * o_slc + gates[..., 2:3] * o_win

def nsa_prompt(q, cmp_kv, slc_kv, win_kv, gates, lw, slopes):
    B, T = q.shape[:2]
    G, DH = NSA_KV_HEADS, NSA_DH
    kc, vc, c_end = compressed_keys(cmp_kv, lw)
    n_sel = T // SEL_BLOCK
    blocks = slc_kv.reshape(B, n_sel, SEL_BLOCK, 2, G, DH)
    b_idx = jnp.arange(B)[:, None, None, None]
    g_idx = jnp.arange(G)[None, :, None, None]

    def fetch(idx):
        kv = blocks[b_idx, idx, :, :, g_idx]
        return kv[..., 0, :], kv[..., 1, :]

    win_pad = jnp.pad(win_kv, ((0, 0), (WINDOW, 0), (0, 0), (0, 0), (0, 0)))
    QB = min(NSA_Q_BLOCK, T)
    nqb = T // QB

    def blockify(a):
        return a.reshape(B, nqb, QB, *a.shape[2:]).swapaxes(0, 1)

    def one_block(inp):
        i, qb, gb = inp
        start = i * QB
        q_pos = start + jnp.arange(QB)
        band = lax.dynamic_slice_in_dim(win_pad, start, WINDOW + QB, axis=1)
        w_pos = start - WINDOW + jnp.arange(WINDOW + QB)
        return nsa_attend(qb, q_pos, kc, vc, c_end, n_sel, fetch,
                          band[:, :, 0], band[:, :, 1], w_pos, gb, slopes)

    o = lax.map(one_block, (jnp.arange(nqb), blockify(q), blockify(gates)))
    o = o.swapaxes(0, 1).reshape(B, T, NSA_HEADS * DH)
    return o, win_kv[:, -min(WINDOW, T):]

def nsa_sample(q, cmp_kv, slc_kv, win_kv, gates, lw, slopes, cmp_pool, slc_pool, win_buf, page_table):
    B, S = q.shape[:2]
    G, DH = NSA_KV_HEADS, NSA_DH
    past_len = page_table.shape[1] * PAGE_SIZE
    past_cmp = cmp_pool[page_table].reshape(B, past_len, 2, G, DH).astype(cmp_kv.dtype)
    kc, vc, c_end = compressed_keys(jnp.concatenate([past_cmp, cmp_kv], axis=1), lw)
    n_past = past_len // SEL_BLOCK
    n_tail = -(-S // SEL_BLOCK)
    tail = jnp.pad(slc_kv, ((0, 0), (0, n_tail * SEL_BLOCK - S), (0, 0), (0, 0), (0, 0)))
    tail = tail.reshape(B, n_tail, SEL_BLOCK, 2, G, DH)
    bpp = PAGE_SIZE // SEL_BLOCK
    pool_blocks = slc_pool.reshape(-1, SEL_BLOCK, 2, G, DH)
    b_idx = jnp.arange(B)[:, None, None, None]
    g_idx = jnp.arange(G)[None, :, None, None]

    def fetch(idx):
        jp = jnp.minimum(idx, n_past - 1)
        phys = page_table[b_idx, jp // bpp] * bpp + jp % bpp
        past = pool_blocks[phys, :, :, g_idx].astype(slc_kv.dtype)
        fresh = tail[b_idx, jnp.clip(idx - n_past, 0, n_tail - 1), :, :, g_idx]
        kv = jnp.where((idx < n_past)[..., None, None, None], past, fresh)
        return kv[..., 0, :], kv[..., 1, :]

    win_all = jnp.concatenate([win_buf.astype(win_kv.dtype), win_kv], axis=1)
    w_len = win_buf.shape[1]
    w_pos = past_len - w_len + jnp.arange(w_len + S)
    q_pos = past_len + jnp.arange(S)
    o = nsa_attend(q, q_pos, kc, vc, c_end, n_past + n_tail, fetch,
                   win_all[:, :, 0], win_all[:, :, 1], w_pos, gates, slopes)
    return o.reshape(B, S, NSA_HEADS * DH), win_all[:, -w_len:]

def layer_forward(x, lw, nsa_fn, conv_buf, h0, s0):
    B, T, _ = x.shape
    G, P, DH = NSA_KV_HEADS, NSA_HPG, NSA_DH
    h = rms_norm(x, lw['norm_mix'])
    (rg_y, rg_x, g_q, g_k, g_v, g_r, g_a,
     n_q, n_cmp, n_slc, n_win, n_gate, m_gate) = split_cols(h @ lw['w_in'])
    xc, conv_new = causal_conv(rg_x, conv_buf, lw['rg_conv_w'], lw['rg_conv_b'])
    hr, h_last = rglru(xc, h0, lw['rg_w_a'], lw['rg_b_a'], lw['rg_w_x'], lw['rg_b_x'], lw['rg_lambda'])
    o_a = jax.nn.gelu(rg_y) * hr
    q = g_q.reshape(B, T, GLA_HEADS, GLA_DK) * (GLA_DK ** -0.5)
    k = g_k.reshape(B, T, GLA_HEADS, GLA_DK)
    v = g_v.reshape(B, T, GLA_HEADS, GLA_DV)
    log_g = jax.nn.log_sigmoid((g_a @ lw['gla_w_a'] + lw['gla_b_a']).astype(jnp.float32)) / GLA_TAU
    o, s_new = gla_recurrent(q, k, v, log_g.reshape(B, T, GLA_HEADS, GLA_DK), s0)
    o_b = rms_norm(o, lw['gla_norm']).reshape(B, T, GLA_HEADS * GLA_DV).astype(x.dtype) * jax.nn.silu(g_r)
    kv_shape = (B, T, 2, G, DH)
    qn = rms_norm(n_q.reshape(B, T, G, P, DH), lw['q_norm']) * (DH ** -0.5)
    cmp_kv = n_cmp.reshape(kv_shape)
    slc_kv = norm_keys(n_slc.reshape(kv_shape), lw['k_norm'][1])
    win_kv = norm_keys(n_win.reshape(kv_shape), lw['k_norm'][2])
    gates = jax.nn.sigmoid(n_gate).reshape(B, T, G, P, 3)
    o_c, win_state = nsa_fn(qn, cmp_kv, slc_kv, win_kv, gates, lw)
    m_a, m_b, m_c = jnp.split(jax.nn.sigmoid(m_gate), 3, axis=-1)
    merged = (m_a * (o_a @ lw['w_rg_out']) + m_b * (o_b @ lw['w_gla_out'])
              + m_c * (o_c @ lw['w_nsa_out']))
    x = x + merged @ lw['w_out']
    h = rms_norm(x, lw['norm_ffn'])
    x = x + (jax.nn.silu(h @ lw['w_ffn_gate']) * (h @ lw['w_ffn_up'])) @ lw['w_ffn_down']
    return x, (cmp_kv, slc_kv, win_state, s_new.astype(x.dtype), h_last.astype(x.dtype), conv_new)

def setup_inputs(seed: int = 0) -> dict:
    key = jax.random.key(seed)
    keys = jax.random.split(key, 40)
    counter = iter(range(40))
    f32 = jnp.float32

    def nrm(shape, scale):
        return jax.random.normal(keys[next(counter)], shape, f32) * scale

    G, DH = NSA_KV_HEADS, NSA_DH
    n_used = DEC_BATCH * N_PAGES
    n_pool = n_used + max(1, n_used // 4)
    win_buf = min(WINDOW, PAST_LEN)
    perm = jax.random.permutation(keys[next(counter)], n_pool)
    page_table = perm[:n_used].reshape(DEC_BATCH, N_PAGES).astype(jnp.int32)
    u = jax.random.uniform(keys[next(counter)], (DEPTH, RG_WIDTH), f32, 0.9, 0.999)
    sg = u ** (1.0 / RG_C)
    rg_lambda = jnp.log(sg) - jnp.log1p(-sg)
    return {
        'x_prompt': nrm((BATCH, SEQ, D_MODEL), 1.0),
        'x_sample': nrm((DEC_BATCH, DEC_SEQ, D_MODEL), 1.0),
        'cache_cmp_kv': nrm((DEPTH, n_pool, PAGE_SIZE, 2, G, DH), 1.0),
        'cache_slc_kv': nrm((DEPTH, n_pool, PAGE_SIZE, 2, G, DH), 1.0),
        'cache_win_kv': nrm((DEPTH, DEC_BATCH, win_buf, 2, G, DH), 1.0),
        'state_gla': nrm((DEPTH, DEC_BATCH, GLA_HEADS, GLA_DK, GLA_DV), 0.5),
        'state_rglru': nrm((DEPTH, DEC_BATCH, RG_WIDTH), 0.5),
        'state_conv': nrm((DEPTH, DEC_BATCH, RG_CONV_W - 1, RG_WIDTH), 1.0),
        'page_table': page_table,
        'norm_mix_g': 1.0 + nrm((DEPTH, D_MODEL), 0.02),
        'w_in': nrm((DEPTH, D_MODEL, D_IN), D_MODEL ** -0.5),
        'rg_conv_w': nrm((DEPTH, RG_CONV_W, RG_WIDTH), RG_CONV_W ** -0.5),
        'rg_conv_b': nrm((DEPTH, RG_WIDTH), 0.02),
        'rg_w_a': nrm((DEPTH, RG_BLOCKS, RG_BLOCK_W, RG_BLOCK_W), RG_BLOCK_W ** -0.5),
        'rg_b_a': nrm((DEPTH, RG_WIDTH), 0.02),
        'rg_w_x': nrm((DEPTH, RG_BLOCKS, RG_BLOCK_W, RG_BLOCK_W), RG_BLOCK_W ** -0.5),
        'rg_b_x': nrm((DEPTH, RG_WIDTH), 0.02),
        'rg_lambda': rg_lambda,
        'gla_w_a': nrm((DEPTH, GLA_RANK, GLA_HEADS * GLA_DK), GLA_RANK ** -0.5),
        'gla_b_a': nrm((DEPTH, GLA_HEADS * GLA_DK), 0.02),
        'gla_norm_g': 1.0 + nrm((DEPTH, GLA_DV), 0.02),
        'nsa_q_norm_g': 1.0 + nrm((DEPTH, DH), 0.02),
        'nsa_k_norm_g': 1.0 + nrm((DEPTH, 3, DH), 0.02),
        'nsa_phi_k': nrm((DEPTH, CMP_BLOCK, DH, DH), (CMP_BLOCK * DH) ** -0.5),
        'nsa_phi_v': nrm((DEPTH, CMP_BLOCK, DH, DH), (CMP_BLOCK * DH) ** -0.5),
        'nsa_cmp_pe': nrm((DEPTH, 2, CMP_BLOCK, DH), 0.1),
        'w_rg_out': nrm((DEPTH, RG_WIDTH, D_MODEL), RG_WIDTH ** -0.5),
        'w_gla_out': nrm((DEPTH, GLA_HEADS * GLA_DV, D_MODEL), (GLA_HEADS * GLA_DV) ** -0.5),
        'w_nsa_out': nrm((DEPTH, NSA_HEADS * DH, D_MODEL), (NSA_HEADS * DH) ** -0.5),
        'w_out': nrm((DEPTH, D_MODEL, D_MODEL), D_MODEL ** -0.5),
        'norm_ffn_g': 1.0 + nrm((DEPTH, D_MODEL), 0.02),
        'w_ffn_gate': nrm((DEPTH, D_MODEL, D_FF), D_MODEL ** -0.5),
        'w_ffn_up': nrm((DEPTH, D_MODEL, D_FF), D_MODEL ** -0.5),
        'w_ffn_down': nrm((DEPTH, D_FF, D_MODEL), D_FF ** -0.5),
    }

def reference(x_prompt, x_sample, cache_cmp_kv, cache_slc_kv, cache_win_kv, state_gla, state_rglru,
              state_conv, page_table, norm_mix_g, w_in, rg_conv_w, rg_conv_b, rg_w_a, rg_b_a, rg_w_x,
              rg_b_x, rg_lambda, gla_w_a, gla_b_a, gla_norm_g, nsa_q_norm_g, nsa_k_norm_g, nsa_phi_k,
              nsa_phi_v, nsa_cmp_pe, w_rg_out, w_gla_out, w_nsa_out, w_out, norm_ffn_g, w_ffn_gate,
              w_ffn_up, w_ffn_down):
    slopes = alibi_slopes()
    Bp = x_prompt.shape[0]
    yp, ys = x_prompt, x_sample
    p_out = [[] for _ in range(6)]
    s_out = [[] for _ in range(6)]
    for l in range(DEPTH):
        lw = {'norm_mix': norm_mix_g[l], 'w_in': w_in[l], 'rg_conv_w': rg_conv_w[l], 'rg_conv_b': rg_conv_b[l],
              'rg_w_a': rg_w_a[l], 'rg_b_a': rg_b_a[l], 'rg_w_x': rg_w_x[l], 'rg_b_x': rg_b_x[l],
              'rg_lambda': rg_lambda[l], 'gla_w_a': gla_w_a[l], 'gla_b_a': gla_b_a[l], 'gla_norm': gla_norm_g[l],
              'q_norm': nsa_q_norm_g[l], 'k_norm': nsa_k_norm_g[l], 'phi_k': nsa_phi_k[l], 'phi_v': nsa_phi_v[l],
              'cmp_pe': nsa_cmp_pe[l], 'w_rg_out': w_rg_out[l], 'w_gla_out': w_gla_out[l],
              'w_nsa_out': w_nsa_out[l], 'w_out': w_out[l], 'norm_ffn': norm_ffn_g[l],
              'w_ffn_gate': w_ffn_gate[l], 'w_ffn_up': w_ffn_up[l], 'w_ffn_down': w_ffn_down[l]}
        yp, p_new = layer_forward(
            yp, lw, functools.partial(nsa_prompt, slopes=slopes),
            jnp.zeros((Bp, RG_CONV_W - 1, RG_WIDTH), yp.dtype),
            jnp.zeros((Bp, RG_WIDTH), jnp.float32),
            jnp.zeros((Bp, GLA_HEADS, GLA_DK, GLA_DV), jnp.float32))
        ys, s_new = layer_forward(
            ys, lw, functools.partial(nsa_sample, slopes=slopes, cmp_pool=cache_cmp_kv[l],
                                      slc_pool=cache_slc_kv[l], win_buf=cache_win_kv[l], page_table=page_table),
            state_conv[l], state_rglru[l], state_gla[l])
        for i in range(6):
            p_out[i].append(p_new[i])
            s_out[i].append(s_new[i])
    p_cmp_kv = jnp.stack(p_out[0])
    p_slc_kv = jnp.stack(p_out[1])
    p_win_kv = jnp.stack(p_out[2])
    p_gla = jnp.stack(p_out[3])
    p_rglru = jnp.stack(p_out[4])
    p_conv = jnp.stack(p_out[5])
    s_cmp_kv = jnp.stack(s_out[0])
    s_slc_kv = jnp.stack(s_out[1])
    s_win_kv = jnp.stack(s_out[2])
    s_gla = jnp.stack(s_out[3])
    s_rglru = jnp.stack(s_out[4])
    s_conv = jnp.stack(s_out[5])
    return (yp, ys, p_cmp_kv, p_slc_kv, p_win_kv, p_gla, p_rglru, p_conv,
            s_cmp_kv, s_slc_kv, s_win_kv, s_gla, s_rglru, s_conv)


_drawn_inputs = setup_inputs


def setup_inputs(seed=0):
    import zlib

    import numpy as np

    out = dict(_drawn_inputs(seed))
    spreads = {}
    factors = {'rg_b_a': 8.0,
     'rg_b_x': 7.085,
     'gla_b_a': 6.041,
     'gla_norm_g': 6.25,
     'nsa_q_norm_g': 8.0,
     'nsa_k_norm_g': 3.768,
     'norm_ffn_g': 2.725}
    for name, (base, spread) in spreads.items():
        noise = np.random.default_rng([zlib.crc32(name.encode()), seed]).standard_normal(out[name].shape)
        drawn = base * np.exp(spread * noise) if base else spread * noise
        out[name] = jnp.asarray(drawn.astype(out[name].dtype))
    for name, factor in factors.items():
        out[name] = (out[name] * factor).astype(out[name].dtype)
    return out
```

```python
import numpy as np

import concourse.bass as bass
from concourse import mybir

F32 = mybir.dt.float32
U8 = mybir.dt.uint8
I32 = mybir.dt.int32
U32 = mybir.dt.uint32
ALU = mybir.AluOpType
ACT = mybir.ActivationFunctionType
AX = mybir.AxisListType

P = 128
DM, T, NB, L = 1024, 512, 8, 2
TA = T + NB
KT = DM // P
NT = T // P
GH, DK, DV, RANK = 4, 128, 256, 16
NH, G, HPG, DH = 16, 4, 4, 64
KVW = 2 * G * DH
PAST, PAGE, WIN = 1024, 128, 512
NPG = PAST // PAGE
STR, SEL = 16, 64
NCP, NCS = T // STR, PAST // STR
NSEL = PAST // SEL + 1
FF = 2816
FT = FF // P
EPS, TINY = 1e-6, 1e-30
BIG = 2.56e32
SLOPE = [2.0 ** (-8.0 * h / NH) for h in range(1, NH + 1)]

IN = {}
_at = 0
for _n, _w in (("rgy", DM), ("rgx", DM), ("gq", 512), ("gk", 512), ("gv", 1024), ("gr", 1024), ("ga", RANK),
               ("nq", DM), ("cmp", KVW), ("slc", KVW), ("win", KVW), ("gate", 3 * NH), ("merge", 3 * DM)):
    IN[_n] = _at
    _at += _w

PR = {"mix": 0, "ffn": 8, "cw": 16, "cb": 48, "ba": 56, "bx": 64, "lam": 72, "gba": 80, "gno": 84, "qn": 86, "kn": 87}
NPR = 88

CC, _at = {}, 0
for _n, _w in (("ident", 128), ("ones", 128), ("blk", 128), ("grp", 128), ("bsel", 8), ("nsl", 16), ("nslr", 1),
               ("dist", 896), ("drow", PAST), ("dcmp", NT * NCP), ("mcmp", NT * NCP), ("dcs", NCS), ("c2s", 14),
               ("jj", 14), ("crow", 4), ("srow", 1)):
    CC[_n] = (_at, _w)
    _at += _w
NCC = _at
LEVELS = (64, 32, 16, 8, 4, 2, 1)


def constants():
    c = np.zeros((P, NCC), np.float32)
    p = np.arange(P)

    def put(name, a):
        c[:, CC[name][0]:CC[name][0] + CC[name][1]] = a

    put("ident", np.eye(P))
    put("ones", np.ones((P, P)))
    put("blk", (p[:, None] // DH) == (p[None, :] // DH))
    put("grp", (p[:, None] // HPG) == (p[None, :] // HPG))
    put("bsel", (p[:, None] // NH) == np.arange(NB)[None, :])
    put("nsl", -np.array(SLOPE)[None, :])
    put("nslr", -np.array(SLOPE)[p % NH][:, None])
    d = p[:, None] + 384 - np.arange(896)[None, :]
    put("dist", np.where(d >= 0, d, BIG))
    put("drow", PAST - np.arange(PAST)[None, :])
    q = (np.arange(NT)[None, :, None] * P + p[:, None, None])
    n = np.arange(NCP)[None, None, :]
    ok = (n * STR + 31 <= q) & (n < NCP - 1)
    put("dcmp", np.where(ok, q - (n * STR + 31), BIG).reshape(P, -1))
    put("mcmp", ok.reshape(P, -1))
    m = np.arange(NCS)
    put("dcs", np.where(m < NCS - 1, PAST - (m * STR + 31), BIG)[None, :])
    st = p[:, None] * STR
    sel = np.arange(1, 15)[None, :] * SEL
    put("c2s", (st < sel + SEL) & (st + 32 > sel) & (p[:, None] < NCS - 1))
    put("jj", np.arange(1, 15)[None, :])
    put("crow", (p % 8)[:, None] * 4 + np.arange(4)[None, :])
    put("srow", 2 * p[:, None])
    s, t = p[:, None], p[None, :]
    mask = np.zeros((P, len(LEVELS) + 1, P), np.int32)
    for i, h in enumerate(LEVELS):
        mask[:, i] = (s // (2 * h) == t // (2 * h)) & (s % (2 * h) < h) & (t % (2 * h) >= h)
    mask[:, len(LEVELS)] = s == t
    return c, mask.reshape(P, -1)


class Own:

    def __init__(self, eng, sem, count):
        self.eng, self.sem, self.count = eng, sem, count

    def tick(self, ins):
        ins.then_inc(self.sem, 1)
        self.count[0] += 1
        return self.count[0]

    def wait(self, n=None):
        self.eng.wait_ge(self.sem, self.count[0] if n is None else n)

    def __call__(self, ins):
        self.tick(ins)
        self.wait()


def slabs_of_layer():
    s = {}

    def add(name, tensor, r0, rt, c0, w):
        s[name] = (tensor, r0, rt, c0, w)

    for n in ("rgx", "rgy"):
        for i in range(2):
            add(f"{n}{i}", "w_in", 0, KT, IN[n] + 512 * i, 512)
    marks = [len(s)]
    add("ga", "w_in", 0, KT, IN["ga"], RANK)
    add("gk", "w_in", 0, KT, IN["gk"], 512)
    add("gq", "w_in", 0, KT, IN["gq"], 512)
    for n in ("gv", "gr"):
        for i in range(2):
            add(f"{n}{i}", "w_in", 0, KT, IN[n] + 512 * i, 512)
    marks.append(len(s))
    add("gate", "w_in", 0, KT, IN["gate"], 3 * NH)
    add("cmp", "w_in", 0, KT, IN["cmp"], 512)
    marks.append(len(s))
    for n in ("slc", "win"):
        add(n, "w_in", 0, KT, IN[n], 512)
    for i in range(2):
        add(f"nq{i}", "w_in", 0, KT, IN["nq"] + 512 * i, 512)
    marks.append(len(s))
    for hf in range(2):
        for br, t in enumerate(("w_rg_out", "w_gla_out", "w_nsa_out")):
            add(f"mg{hf}{br}", "w_in", 0, KT, IN["merge"] + br * DM + 512 * hf, 512)
            add(f"mo{hf}{br}", t, 0, KT, 512 * hf, 512)
    for hf in range(2):
        add(f"wo{hf}", "w_out", 0, KT, 512 * hf, 512)
    marks.append(len(s))
    for c in range((FT + 3) // 4):
        w = min(512, FF - 512 * c)
        add(f"fg{c}", "w_ffn_gate", 0, KT, 512 * c, w)
        add(f"fu{c}", "w_ffn_up", 0, KT, 512 * c, w)
    for hf in range(2):
        for r in range(0, FT, 8):
            add(f"fd{hf}{r}", "w_ffn_down", r, min(8, FT - r), 512 * hf, 512)
    marks.append(len(s))
    return s, marks


def tiles_of_layer():
    t = []
    t += [(("rgx", i), "act") for i in range(KT)] + [(("rgy", i), "act") for i in range(KT)]
    t += [(("ga", 0), "act")] + [(("gk", i), "act") for i in range(4)] + [(("gq", i), "act") for i in range(4)]
    t += [(("gv", i, tt), "act") for i in range(2) for tt in range(NT + 1)]
    t += [(("gr", i), "act") for i in range(KT)]
    t += [(("gate", tt), "act") for tt in range(NT + 1)]
    t += [(("cmp", tt), "act") for tt in range(NT + 1)]
    t += [((n, tt), "dve") for n in ("slc", "win") for tt in range(NT + 1)]
    t += [(("nq", i), "dve") for i in range(KT)]
    for hf in range(2):
        for br in range(3):
            for m in range(4):
                t += [(("mg", hf, br, m), "act"), (("mo", hf, br, m), "dve")]
    t += [(("wo", i), "dve") for i in range(KT)]
    for i in range(FT):
        t += [(("fg", i), "act"), (("fu", i), "dve")]
    t += [(("fd", i), "dve") for i in range(KT)]
    return t


NSLOT = 3


def build(nc, A, O, C):
    sems = {}

    def sem(name):
        if name not in sems:
            sems[name] = nc.alloc_semaphore(name)
        return sems[name]

    def sb(name, shape, dt=F32):
        return nc.alloc_sbuf_tensor(name, shape, dt)

    con = sb("con", [P, NCC])
    lmask = sb("lmask", [P, 8 * P], U8)
    xT, hT, oaT, obT, ocT = (sb(n, [P, KT, TA]) for n in ("xT", "hT", "oaT", "obT", "ocT"))
    ring = sb("ring", [P, NSLOT, KT * 512])
    par = sb("par", [P, P])
    kgain = sb("kgain", [P, 2, DH])
    gate_s = sb("gate_s", [P, 3])
    nqs = sb("nqs", [P, KT, NB])
    knewT = sb("knewT", [P, 2, 2, NB])
    vnew = sb("vnew", [NB, 2, 256])
    pages = sb("pages", [1, NB * NPG], I32)
    pg_rows = sb("pg_rows", [P, NB // 2 + NB * NPG])
    gather = sb("gather", [P, 16 + 2 * NB * NPG], U32)
    ARENA = 15744
    arena = sb("arena", [P, ARENA])
    pair = [nc.alloc_psum_tensor(f"pair{i}", [P, 2, 512], F32) for i in range(4)]
    bank = [pair[i // 2][:, i % 2, :] for i in range(8)]
    gate_rows = nc.dram_tensor("gate_rows", [NB, 3 * NH], F32, kind="Internal").ap()
    cmp_rows = nc.dram_tensor("cmp_rows", [2, P, 2 * NB * NCS], F32, kind="Internal").ap()
    HA = TA // 2

    def both(i):
        return pair[i][:, :, 0:HA]

    def two(ap):
        return ap.rearrange("p (a b) -> p a b", a=2)

    def c(name, rows=P):
        a, w = CC[name]
        return con[0:rows, a:a + w]

    ident, ones, blk = c("ident"), c("ones"), c("blk")

    class Space:

        def __init__(self, flat):
            self.flat, self.at, self.end = flat, 0, flat.shape[1]

        def take(self, *dims):
            n = int(np.prod(dims))
            assert self.at + n <= self.end, (self.at, n, self.end)
            v = self.flat[:, self.at:self.at + n]
            self.at += n
            if len(dims) == 2:
                v = v.rearrange("p (a b) -> p a b", a=dims[0])
            if len(dims) == 3:
                v = v.rearrange("p (a b c) -> p a b c", a=dims[0], b=dims[1])
            if len(dims) == 4:
                v = v.rearrange("p (a b c d) -> p a b c d", a=dims[0], b=dims[1], c=dims[2])
            return v

    def flat(t):
        return t[:, :, :].rearrange("p a b -> p (a b)")

    SLABS, MARKS = slabs_of_layer()
    names = list(SLABS)
    TILES = tiles_of_layer()
    TI = {k: i for i, (k, _) in enumerate(TILES)}
    own_counts = {"act": [0], "dve": [0], "pool": [0]}

    def pieces(name):
        return 4 if name.startswith("mo") and name.endswith("2") else 2 * KT if name.startswith("nq") else 1

    def slab_view(name):
        _, _, rt, _, w = SLABS[name]
        i = names.index(name)
        return ring[:, i % NSLOT, 0:rt * w].rearrange("p (k n) -> p k n", k=rt)

    def slab_ready(name):
        i = names.index(name)
        return sem(f"slab_in{i % NSLOT}"), 16 * sum(pieces(n) for n in names[i % NSLOT:i + 1:NSLOT])

    def slab_used(name):
        n, d = name.rstrip("0123456789"), name[len(name.rstrip("0123456789")):]
        if n == "fd" and int(d[1:]) != 16:
            return sem("ffn_down_slab"), int(d[0]) * 2 + int(d[1:]) // 8 + 1
        if n in ("mg", "mo"):
            key = (n, int(d[0]), int(d[1]), 3)
        elif n == "gv":
            key = (n, int(d), NT)
        elif n in ("gate", "slc", "win", "cmp"):
            key = (n, NT)
        elif n == "ga":
            key = (n, 0)
        elif n == "fd":
            key = (n, 4 * int(d[0]) + 3)
        else:
            key = (n, min(4 * int(d or 0) + 3, FT - 1))
        return sem("proj_done"), TI[key] + 1

    def load_slab(eng, name, l):
        t, r0, rt, c0, w = SLABS[name]
        i = names.index(name)
        if i >= NSLOT:
            eng.wait_ge(*slab_used(names[i - NSLOT]))
        got = sem(f"slab_in{i % NSLOT}")
        src = A[t][l][r0 * P:(r0 + rt) * P, c0:c0 + w]
        if pieces(name) == 1:
            eng.dma_start(slab_view(name), src.rearrange("(k p) n -> p k n", p=P)).then_inc(got, 16)
            return
        if name.startswith("nq"):
            for k in range(KT):
                v = src[k * P:(k + 1) * P].rearrange("p (a h c) -> p a h c", a=2, h=HPG)
                d = slab_view(name)[:, k, :].rearrange("p (h a c) -> p a h c", a=2, h=HPG)
                for a in range(2):
                    eng.dma_start(d[:, a], v[:, a]).then_inc(got, 16)
            return
        v = src.rearrange("(gp a h d) n -> gp a d h n", gp=2, a=2, h=HPG)
        for gp in range(2):
            for a in range(2):
                eng.dma_start(slab_view(name)[a * DH:(a + 1) * DH, gp * 4:gp * 4 + 4, :],
                              v[gp, a]).then_inc(got, 16)

    def loads_of_phase(eng, ph, l):
        ahead = [0] + [min(m + NSLOT - (j == 3), len(names)) for j, m in enumerate(MARKS)]
        for n in names[ahead[ph]:ahead[ph + 1]]:
            load_slab(eng, n, l)

    def proj_pair(key):
        return key[1] % 4 if key[0] == "fd" else TI[key] % 2

    def wait_proj_bank(pe, key):
        i = TI[key] - 2
        if key[0] == "fd":
            i = TI[("fd", 0)] - 1 if key[1] < 4 else TI[key] - 4
        if i < 0:
            return
        for e in ("act", "dve"):
            if key[0] == "fd" or TILES[i][1] == e:
                pe.wait_ge(sem(f"proj_read_{e}"), sum(1 for _, x in TILES[:i + 1] if x == e))

    def wait_proj(eng, key):
        eng.wait_ge(sem("proj_done"), TI[key] + 1)

    def proj_T(pe, key, lhs, rhs, nk=KT, m=P):
        wait_proj_bank(pe, key)
        o = proj_pair(key)
        for half in range(2):
            for k in range(nk):
                last = pe.matmul(pair[o][0:m, half, 0:HA], lhs(k), rhs[:, k, half * HA:(half + 1) * HA],
                                 start=(k == 0), stop=(k == nk - 1))
        last.then_inc(sem("proj_done"), 1)

    def proj_rows(pe, key, tt, slab, w):
        wait_proj_bank(pe, key)
        big = pair[proj_pair(key)][:, 0, :]
        rows = P if tt < NT else NB
        for k in range(KT):
            last = pe.matmul(big[0:rows, 0:w], hT[:, k, tt * P:tt * P + rows], slab[:, k, 0:w],
                             start=(k == 0), stop=(k == KT - 1))
        last.then_inc(sem("proj_done"), 1)

    def open_slab(pe, name):
        s, v = slab_ready(name)
        pe.wait_ge(s, v)
        return slab_view(name)

    def bc(ap, n):
        return ap.unsqueeze(len(ap.shape)).to_broadcast(list(ap.shape) + [n])

    def rep(ap, n):
        return ap.unsqueeze(1).to_broadcast([ap.shape[0], n, ap.shape[1]])

    xr = arena[:, 0:5 * DM].rearrange("p (t n) -> p t n", t=5)
    lmask_in = arena[:, 5 * DM:6 * DM].bitcast(I32)
    pg_in = arena[:, 6 * DM:6 * DM + NB // 2 + NB * NPG].bitcast(I32)
    page_rows = NB // 2
    with nc.Block() as block:
        @block.sync
        def _(sp):
            sp.dma_start(con[:, :], C["con"]).then_inc(sem("io_moved"), 16)
            sp.dma_start(lmask_in, C["lmask"]).then_inc(sem("io_moved"), 16)
            sp.dma_start(pages[:, :], A["page_table"].rearrange("(a b) t -> a (b t)", a=1)).then_inc(sem("io_moved"), 16)
            for ct in range(NB // 2):
                for b2 in range(2):
                    src = A["page_table"][2 * ct + b2].unsqueeze(1).to_broadcast([NPG, 8]).unsqueeze(2)
                    sp.dma_start(pg_in[b2 * 64:b2 * 64 + 64, ct:ct + 1], src,
                                 allow_slow_non_contiguous=True).then_inc(sem("pages_in"), 16)
            sp.dma_start(pg_in[:, NB // 2:], A["page_table"].rearrange("(a b) t -> a (b t)", a=1)
                         .to_broadcast([P, NB * NPG])).then_inc(sem("pages_in"), 16)
            sp.dma_start(xr[:, 0:NT, :], A["x_prompt"][0].rearrange("(t p) n -> p t n", p=P)).then_inc(sem("io_moved"), 16)
            sp.dma_start(xr[0:NB, NT, :], A["x_sample"][:, 0, :]).then_inc(sem("io_moved"), 16)

        @block.tensor
        def _(pe):
            pe.wait_ge(sem("io_moved"), 80)
            for k in range(KT):
                if k >= 4:
                    pe.wait_ge(sem("io_copied"), k - 3)
                for tt in range(NT):
                    pe.transpose(bank[k % 4][:, tt * P:(tt + 1) * P], xr[:, tt, k * P:(k + 1) * P], ident)
                pe.transpose(bank[4 + k % 4][:, 0:NB], xr[0:NB, NT, k * P:(k + 1) * P],
                             ident[0:NB, 0:NB]).then_inc(sem("io_turned"), 1)

        @block.vector
        def _(dve):
            for k in range(KT):
                dve.wait_ge(sem("io_turned"), k + 1)
                dve.tensor_copy(xT[:, k, 0:T], bank[k % 4][:, :])
                dve.tensor_copy(xT[:, k, T:TA], bank[4 + k % 4][:, 0:NB]).then_inc(sem("io_copied"), 1)
            dve.tensor_copy(lmask[:, :], lmask_in)
            dve.wait_ge(sem("pages_in"), 16 * (NB + 1))
            dve.tensor_copy(pg_rows[:, :], pg_in)

    def norm_pe(pe, tag, n=KT):
        for k in range(n):
            pe.wait_ge(sem(f"{tag}_sq"), k + 1)
            for half in range(2):
                last = pe.matmul(pair[2][:, half, 0:HA], ones, tag_sq[tag][k % 2][:, half * HA:(half + 1) * HA],
                                 start=(k == 0), stop=(k == n - 1))
            last.then_inc(sem(f"{tag}_sum"), 1)

    def norm_act(act, tag, ms):
        for k in range(KT):
            if k >= 2:
                act.wait_ge(sem(f"{tag}_sum"), k - 1)
            act.activation(tag_sq[tag][k % 2], xT[:, k, :], ACT.Square).then_inc(sem(f"{tag}_sq"), 1)
        act.wait_ge(sem(f"{tag}_ms"), 1)
        act.activation(ms, ms, ACT.Sqrt).then_inc(sem(f"{tag}_rt"), 1)

    def norm_dve(dve, own, tag, ms, gain):
        dve.wait_ge(sem(f"{tag}_sum"), KT)
        dve.tensor_scalar(two(ms), both(2), 1.0 / DM, EPS, ALU.mult, ALU.add).then_inc(sem(f"{tag}_ms"), 1)
        dve.wait_ge(sem(f"{tag}_rt"), 1)
        own(dve.reciprocal(ms, ms))
        for k in range(KT):
            dve.scalar_tensor_tensor(hT[:, k, :], xT[:, k, :], par[:, PR[gain] + k:PR[gain] + k + 1], ms,
                                     ALU.mult, ALU.mult).then_inc(sem(f"{tag}_h"), 1)

    tag_sq = {}
    OCF, OBF = flat(ocT), flat(obT)

    with nc.Fori(0, L) as l:
        for cnt in own_counts.values():
            cnt[0] = 0

        sp0 = Space(arena[:, :])
        prow = sp0.take(P)
        strow = sp0.take(DM)
        Mb = sp0.take(KT, TA)
        XP = [sp0.take(3 + TA) for _ in range(2)]
        XS = [sp0.take(NB, 4) for _ in range(2)]
        XC = [sp0.take(TA) for _ in range(2)]
        TR = [sp0.take(TA) for _ in range(2)]
        TX = [sp0.take(TA) for _ in range(2)]
        DN = [sp0.take(TA) for _ in range(2)]
        h0T = sp0.take(KT, 32)
        tag_sq["mix"] = [sp0.take(TA) for _ in range(2)]
        ms0 = sp0.take(TA)
        pk = sp0.take(8, KT)
        gw = sp0.take(2, 8, P)
        AC, VB = ocT, obT
        states = sp0.take(KT, 36)

        def conv_w(j, n):
            k = PR["cw"] + 8 * j + n
            return par[:, k:k + 1]

        def pcol(name, n):
            return par[:, PR[name] + n:PR[name] + n + 1]

        PAR_IN = 16 * 17

        with nc.Block() as block:
            @block.sync
            def _(sp):
                def rows(r, src):
                    sp.dma_start(prow[r:r + src.shape[0], 0:src.shape[1]], src).then_inc(sem("par_in"), 16)

                def as_rows(v):
                    return v.rearrange("(a n) -> a n", n=P)

                rows(PR["mix"], as_rows(A["norm_mix_g"][l]))
                rows(PR["ffn"], as_rows(A["norm_ffn_g"][l]))
                rows(PR["cw"], A["rg_conv_w"][l].rearrange("j (a n) -> (j a) n", n=P))
                rows(PR["cb"], as_rows(A["rg_conv_b"][l]))
                rows(PR["ba"], as_rows(A["rg_b_a"][l]))
                rows(PR["bx"], as_rows(A["rg_b_x"][l]))
                rows(PR["lam"], as_rows(A["rg_lambda"][l]))
                rows(PR["gba"], as_rows(A["gla_b_a"][l]))
                rows(PR["gno"], as_rows(A["gla_norm_g"][l]))
                for a in range(2):
                    sp.dma_start(prow[PR["qn"]:PR["qn"] + 1, a * DH:(a + 1) * DH],
                                 A["nsa_q_norm_g"][l].unsqueeze(0)).then_inc(sem("par_in"), 16)
                    sp.dma_start(prow[PR["kn"]:PR["kn"] + 1, a * DH:(a + 1) * DH],
                                 A["nsa_k_norm_g"][l][0:1, :]).then_inc(sem("par_in"), 16)
                sp.dma_start(strow[0:24, :], A["state_conv"][l].rearrange("b j n -> (b j) n")).then_inc(sem("par_in"), 16)
                sp.dma_start(strow[24:32, :], A["state_rglru"][l]).then_inc(sem("par_in"), 16)
                for r in range(2):
                    sp.dma_start(kgain[:, r, :], A["nsa_k_norm_g"][l][r + 1].unsqueeze(0).to_broadcast([P, DH])
                                 ).then_inc(sem("par_in"), 16)
                loads_of_phase(sp, 0, l)
                sp.dma_start(O["s_win_kv"][l][:, 0:WIN - 1].rearrange("b w k g d -> b (w k g d)"),
                             A["cache_win_kv"][l][:, 1:WIN].rearrange("b w k g d -> b (w k g d)")
                             ).then_inc(sem("win_moved"), 16)
                sp.wait_ge(sem("rg_out"), 1)
                sp.dma_start(O["p_rglru"][l], strow[0:1, :]).then_inc(sem("rg_st"), 16)
                sp.dma_start(O["s_rglru"][l], strow[1:9, :]).then_inc(sem("rg_st"), 16)
                sp.dma_start(O["p_conv"][l][0], strow[9:12, :]).then_inc(sem("rg_st"), 16)
                sp.dma_start(O["s_conv"][l].rearrange("b j n -> (b j) n"), strow[12:36, :]).then_inc(sem("rg_st"), 16)
                sp.wait_ge(sem("rg_st"), 64)


            @block.tensor
            def _(pe):
                norm_pe(pe, "mix")
                pe.wait_ge(sem("par_in"), PAR_IN)
                pe.transpose(bank[7][:, 0:NPR], prow[0:NPR, :], ident[0:NPR, 0:NPR])
                for k in range(KT):
                    last = pe.transpose(bank[7][:, 128 + 32 * k:160 + 32 * k], strow[0:32, k * P:(k + 1) * P],
                                        ident[0:32, 0:32])
                last.then_inc(sem("par_turned"), 1)
                pe.wait_ge(sem("mix_h"), KT)

                def gates(n):
                    pe.wait_ge(sem("gw_in"), 32)
                    pe.wait_ge(sem("conv"), n + 1)
                    if n >= 1:
                        pe.wait_ge(sem("rg_tanh"), 2 * n)
                    else:
                        pe.wait_ge(sem("mix_h"), 1)
                    for j in range(2):
                        for half in range(2):
                            last = pe.matmul(pair[2 + j][:, half, 0:HA], gw[:, j, n, :],
                                             XC[n % 2][:, half * HA:(half + 1) * HA], start=True, stop=True)
                    last.then_inc(sem("rg_gate"), 1)

                for nm in ("rgx", "rgy"):
                    for i in range(2):
                        w = open_slab(pe, f"{nm}{i}")
                        for m in range(4):
                            n = 4 * i + m
                            proj_T(pe, (nm, n), lambda k: w[:, k, m * P:(m + 1) * P], hT)
                            if nm == "rgx" and n >= 2:
                                gates(n - 2)
                            if nm == "rgy" and n < 2:
                                gates(6 + n)
                pe.wait_ge(sem("rg_states"), KT)
                for k in range(KT):
                    last = pe.transpose(bank[6 + k // 4][0:36, (k % 4) * P:(k % 4 + 1) * P], states[:, k, :], ident)
                last.then_inc(sem("rg_rows"), 1)

            @block.scalar
            def _(act):
                own = Own(act, sem("act_own"), own_counts["act"])
                act.dma_start(gw[:, 0, :, :], A["rg_w_a"][l].rearrange("n c d -> c n d")).then_inc(sem("gw_in"), 16)
                act.dma_start(gw[:, 1, :, :], A["rg_w_x"][l].rearrange("n c d -> c n d")).then_inc(sem("gw_in"), 16)
                norm_act(act, "mix", ms0)
                act.wait_ge(sem("par_set"), 1)
                own(act.activation(pk[:, 0, :], par[:, PR["lam"]:PR["lam"] + 8], ACT.Abs))
                own(act.activation(pk[:, 1, :], pk[:, 0, :], ACT.Exp, scale=-1.0))
                act.activation(pk[:, 2, :], pk[:, 1, :], ACT.Ln, bias=1.0).then_inc(sem("sp_ln"), 1)

                def evac_x(n):
                    wait_proj(act, ("rgx", n))
                    if n >= 2:
                        act.wait_ge(sem("conv"), n - 1)
                    act.activation(two(XP[n % 2][:, 3:3 + TA]), both(proj_pair(("rgx", n))),
                                   ACT.Copy).then_inc(sem("proj_read_act"), 1)

                def gate_tanh(n):
                    act.wait_ge(sem("rg_gate"), n + 1)
                    act.wait_ge(sem("sp_done"), 1)
                    if n >= 2:
                        act.wait_ge(sem("rg_v"), n - 1)
                    for j, (dst, b) in enumerate(((TR, 4), (TX, 5))):
                        act.activation(two(dst[n % 2]), both(2 + j), ACT.Tanh, scale=0.5,
                                       bias=pk[:, b, n:n + 1]).then_inc(sem("rg_tanh"), 1)
                    act.wait_ge(sem("rg_tanh"), 2 * n + 2)
                    own.tick(act.activation(DN[n % 2], TR[n % 2], ACT.Tanh, scale=pk[:, 3, n:n + 1],
                                            bias=pk[:, 3, n:n + 1]))
                    act.activation(AC[:, n, :], TR[n % 2], ACT.Exp, scale=pk[:, 6, n:n + 1],
                                   bias=pk[:, 6, n:n + 1]).then_inc(sem("rg_a"), 1)

                for n in range(KT):
                    evac_x(n)
                    if n >= 2:
                        gate_tanh(n - 2)
                gate_tanh(6)
                def gelu(n):
                    wait_proj(act, ("rgy", n))
                    act.activation(two(oaT[:, n, :]), both(proj_pair(("rgy", n))),
                                   ACT.Gelu_apprx_tanh).then_inc(sem("proj_read_act"), 1)
                gelu(0)
                gate_tanh(7)
                for n in range(1, KT):
                    gelu(n)
                for n in range(KT):
                    act.wait_ge(sem("rg_v"), n + 1)
                    act.activation(VB[:, n, :], VB[:, n, :], ACT.Sqrt).then_inc(sem("rg_sqrt"), 1)
                act.wait_ge(sem("rg_rows"), 1)
                own.tick(act.activation(strow[0:36, 0:512], bank[6][0:36, :], ACT.Copy))
                act.activation(strow[0:36, 512:1024], bank[7][0:36, :], ACT.Copy).then_inc(sem("rg_out"), 1)

            @block.vector
            def _(dve):
                own = Own(dve, sem("dve_own"), own_counts["dve"])
                dve.wait_ge(sem("par_turned"), 1)
                dve.tensor_copy(par[:, 0:NPR], bank[7][:, 0:NPR]).then_inc(sem("par_set"), 1)
                dve.wait_ge(sem("par_set"), 1)
                own(dve.tensor_copy(h0T, bank[7][:, 128:384].rearrange("p (k r) -> p k r", k=KT)))
                lam = par[:, PR["lam"]:PR["lam"] + 8]
                norm_dve(dve, own, "mix", ms0, "mix")
                dve.wait_ge(sem("sp_ln"), 1)
                own(dve.tensor_scalar(pk[:, 3, :], pk[:, 1, :], 1.0, 1.0, ALU.add, ALU.subtract))
                own(dve.tensor_scalar(pk[:, 4, :], pk[:, 3, :], 0.0, None, ALU.is_equal))
                own(dve.tensor_scalar(pk[:, 3, :], pk[:, 3, :], TINY, None, ALU.max))
                own(dve.reciprocal(pk[:, 3, :], pk[:, 3, :]))
                own(dve.tensor_tensor(pk[:, 2, :], pk[:, 2, :], pk[:, 3, :], ALU.mult))
                own(dve.tensor_tensor(pk[:, 2, :], pk[:, 2, :], pk[:, 4, :], ALU.add))
                own(dve.tensor_tensor(pk[:, 2, :], pk[:, 2, :], pk[:, 1, :], ALU.mult))
                own(dve.tensor_scalar(pk[:, 5, :], lam, -1.0, 0.0, ALU.mult, ALU.max))
                own(dve.tensor_tensor(pk[:, 2, :], pk[:, 2, :], pk[:, 5, :], ALU.add))
                own(dve.tensor_scalar(pk[:, 3, :], pk[:, 2, :], 4.0, None, ALU.mult))
                own(dve.tensor_scalar(pk[:, 6, :], pk[:, 2, :], -4.0, None, ALU.mult))
                own(dve.tensor_scalar(pk[:, 4, :], par[:, PR["ba"]:PR["ba"] + 8], 0.5, None, ALU.mult))
                dve.tensor_scalar(pk[:, 5, :], par[:, PR["bx"]:PR["bx"] + 8], 0.5, None,
                                  ALU.mult).then_inc(sem("sp_done"), 1)
                for i in range(2):
                    own(dve.memset(XP[i][:, 0:3], 0.0))

                def conv(n):
                    xp, xs, xc = XP[n % 2], XS[n % 2], XC[n % 2]
                    own.tick(dve.tensor_copy(xs[:, :, 0:3], h0T[:, n, 0:24].rearrange("p (b j) -> p b j", b=NB)))
                    dve.wait_ge(sem("proj_read_act"), n + 1)
                    if n >= 2:
                        dve.wait_ge(sem("rg_gate"), n - 1)
                    own.tick(dve.tensor_copy(xs[:, :, 3], xp[:, 3 + T:3 + TA]))
                    own(dve.tensor_scalar(xc[:, 0:T], xp[:, 0:T], conv_w(0, n), pcol("cb", n), ALU.mult, ALU.add))
                    own(dve.tensor_scalar(xc[:, T:TA], xs[:, :, 0], conv_w(0, n), pcol("cb", n), ALU.mult, ALU.add))
                    for j in range(1, 4):
                        own.tick(dve.scalar_tensor_tensor(xc[:, 0:T], xp[:, j:j + T], conv_w(j, n), xc[:, 0:T],
                                                          ALU.mult, ALU.add))
                        own(dve.scalar_tensor_tensor(xc[:, T:TA], xs[:, :, j], conv_w(j, n), xc[:, T:TA],
                                                     ALU.mult, ALU.add))
                    own.tick(dve.tensor_copy(states[:, n, 9:12], xp[:, T:T + 3]))
                    dve.tensor_copy(states[:, n, 12:36].rearrange("p (b j) -> p b j", b=NB),
                                    xs[:, :, 1:4]).then_inc(sem("conv"), 1)

                def scale(n):
                    dve.wait_ge(sem("rg_a"), n + 1)
                    own(dve.scalar_tensor_tensor(Mb[:, n, :], TX[n % 2], 1.0, XC[n % 2], ALU.add, ALU.mult))
                    own(dve.tensor_scalar(TX[n % 2], DN[n % 2], 1.0, None, ALU.add))
                    own(dve.reciprocal(TX[n % 2], TX[n % 2]))
                    dve.scalar_tensor_tensor(VB[:, n, :], DN[n % 2], 2.0, TX[n % 2], ALU.mult,
                                             ALU.mult).then_inc(sem("rg_v"), 1)

                for n in range(KT):
                    if n >= 2:
                        scale(n - 2)
                    conv(n)
                scale(6)
                scale(7)
                for n in range(KT):
                    dve.wait_ge(sem("rg_sqrt"), n + 1)
                    u = Mb[:, n, :]
                    own(dve.scalar_tensor_tensor(u, VB[:, n, :], 0.5, u, ALU.mult, ALU.mult))
                    own.tick(dve.tensor_tensor(XC[0][:, T:TA], AC[:, n, T:TA], h0T[:, n, 24:32], ALU.mult))
                    own(dve.tensor_tensor_scan(XC[1][:, 0:T], AC[:, n, 0:T], u[:, 0:T], 0.0, ALU.mult, ALU.add))
                    own(dve.tensor_tensor(XC[1][:, T:TA], XC[0][:, T:TA], u[:, T:TA], ALU.add))
                    own.tick(dve.tensor_copy(states[:, n, 0:9], XC[1][:, T - 1:TA]))
                    dve.tensor_tensor(oaT[:, n, :], oaT[:, n, :], XC[1], ALU.mult).then_inc(sem("rg_states"), 1)
                    dve.wait_ge(sem("rg_states"), n + 1)


        sp1 = Space(arena[:, :])
        GQ, GK = sp1.take(GH, TA), sp1.take(GH, TA)
        EG = sp1.take(GH, NB)
        GVS = sp1.take(GH * DV)
        keep1 = sp1.at
        GB = sp1.take(GH, TA)
        GV = sp1.take(NT, GH * DV)
        ST = sp1.take(NT, DV)
        W = [sp1.take(T) for _ in range(2)]
        QP = [sp1.take(T) for _ in range(2)]
        KP = [sp1.take(T)]
        EB = sp1.take(GH, NT)
        oc1 = Space(OCF)
        NZ = oc1.take(GH * TA)
        oc1.at = 0
        AA, QE, KK, KKT, MS1 = (oc1.take(T) for _ in range(5))
        OSQ = [oc1.take(T) for _ in range(2)]
        KP.append(oc1.take(T))
        gwa, GA = OBF[:, 0:GH * DK], OBF[:, GH * DK:GH * DK + TA]
        chunks = lambda ap: ap.rearrange("p (c t) -> p c t", c=NT)
        NLV = len(LEVELS)

        def halves(ap, half):
            return ap.rearrange("p (n a t) -> p n a t", a=2, t=half)

        with nc.Block() as block:
            @block.sync
            def _(sp):
                sp.dma_start(gwa[0:RANK, :], A["gla_w_a"][l]).then_inc(sem("kc_in"), 16)
                loads_of_phase(sp, 1, l)
                for h in range(GH):
                    sp.wait_ge(sem("gl_s"), h + 1)
                    sp.dma_start(O["p_gla"][l][0, h], ST[:, NT - 1, :]).then_inc(sem("pgla_out"), 16)
                sp.wait_ge(sem("pgla_out"), 16 * GH)

            @block.tensor
            def _(pe):
                w = open_slab(pe, "ga")
                proj_T(pe, ("ga", 0), lambda k: w[:, k, :], hT, m=RANK)
                w = open_slab(pe, "gk")
                for m in range(4):
                    proj_T(pe, ("gk", m), lambda k: w[:, k, m * P:(m + 1) * P], hT)
                pe.wait_ge(sem("proj_read_act"), 2 * KT + 1)
                pe.wait_ge(sem("kc_in"), 16)
                for h in range(GH):
                    if h >= 2:
                        pe.wait_ge(sem("gl_z"), h - 1)
                    for half in range(2):
                        last = pe.matmul(pair[2 + h % 2][:, half, 0:HA], gwa[0:RANK, h * DK:(h + 1) * DK],
                                         GA[0:RANK, half * HA:(half + 1) * HA], start=True, stop=True)
                    last.then_inc(sem("gl_zp"), 1)
                w = open_slab(pe, "gq")
                for m in range(4):
                    proj_T(pe, ("gq", m), lambda k: w[:, k, m * P:(m + 1) * P], hT)
                for i in range(2):
                    w = open_slab(pe, f"gv{i}")
                    for tt in range(NT + 1):
                        proj_rows(pe, ("gv", i, tt), tt, w, 512)
                for i in range(2):
                    w = open_slab(pe, f"gr{i}")
                    for m in range(4):
                        proj_T(pe, ("gr", 4 * i + m), lambda k: w[:, k, m * P:(m + 1) * P], hT)
                pe.wait_ge(sem("proj_read_act"), sum(1 for k, e in TILES[:TI[("gate", 0)]] if e == "act"))
                for h in range(GH):
                    for i in range(NLV + 1):
                        v = h * (NLV + 1) + i
                        if v >= 2:
                            pe.wait_ge(sem("gl_cp"), v - 1)
                        if i < NLV:
                            pe.wait_ge(sem("gl_qk"), h * NLV + i + 1)
                            kk, qq = KP[(h * NLV + i) % 2], QP[(h * NLV + i) % 2]
                        else:
                            kk, qq = GK[:, h, 0:T], GQ[:, h, 0:T]
                        for c_ in range(NT):
                            cs = slice(c_ * P, (c_ + 1) * P)
                            last = pe.matmul(bank[4 + v % 2][:, cs], kk[:, cs], qq[:, cs], start=True, stop=True)
                        last.then_inc(sem("gl_a"), 1)
                    pe.wait_ge(sem("gl_kk"), h + 1)
                    for c_ in range(NT):
                        cs = slice(c_ * P, (c_ + 1) * P)
                        last = pe.transpose(bank[6][:, cs], KK[:, cs], ident)
                    last.then_inc(sem("gl_kt"), 1)
                    pe.wait_ge(sem("gl_kts"), h + 1)
                    for c_ in range(NT):
                        last = pe.matmul(bank[c_ // 2][:, (c_ % 2) * DV:(c_ % 2 + 1) * DV], KKT[:, c_ * P:(c_ + 1) * P],
                                         GV[:, c_, h * DV:(h + 1) * DV], start=True, stop=True)
                    last.then_inc(sem("gl_u"), 1)
                    pe.wait_ge(sem("gl_s"), h + 1)
                    for vh in range(2):
                        for c_ in range(NT):
                            cs = slice(c_ * P, (c_ + 1) * P)
                            last = pe.matmul(bank[2 + vh][:, cs], GV[:, c_, h * DV + vh * P:h * DV + (vh + 1) * P],
                                             AA[:, cs], start=True, stop=(c_ == 0))
                            if c_:
                                last = pe.matmul(bank[2 + vh][:, cs], ST[:, c_ - 1, vh * P:(vh + 1) * P],
                                                 QE[:, cs], start=False, stop=True)
                    last.then_inc(sem("gl_o"), 1)
                    pe.wait_ge(sem("gl_osq"), h + 1)
                    for vh in range(2):
                        last = pe.matmul(bank[7], ones, OSQ[vh], start=(vh == 0), stop=(vh == 1))
                    last.then_inc(sem("gl_osum"), 1)

            @block.scalar
            def _(act):
                own = Own(act, sem("act_own"), own_counts["act"])

                def evac(key, dst, fn=ACT.Copy, scale=1.0):
                    wait_proj(act, key)
                    act.activation(two(dst), both(proj_pair(key)), fn, scale=scale).then_inc(sem("proj_read_act"), 1)

                wait_proj(act, ("ga", 0))
                act.activation(two(GA[0:RANK, :]), both(proj_pair(("ga", 0)))[0:RANK], ACT.Copy
                               ).then_inc(sem("proj_read_act"), 1)
                for m in range(4):
                    evac(("gk", m), GK[:, m, :])
                for m in range(4):
                    evac(("gq", m), GQ[:, m, :], scale=DK ** -0.5)
                act.wait_ge(sem("gl_z"), GH)
                nz = NZ.rearrange("p (h t) -> p h t", h=GH)
                own(act.activation(nz, GB, ACT.Abs))
                own(act.activation(NZ, NZ, ACT.Exp, scale=-1.0))
                act.activation(NZ, NZ, ACT.Ln, bias=1.0).then_inc(sem("gl_ln"), 1)
                for i in range(2):
                    for tt in range(NT + 1):
                        key = ("gv", i, tt)
                        wait_proj(act, key)
                        rows = P if tt < NT else NB
                        dst = GV[:, tt, i * 512:(i + 1) * 512] if tt < NT else GVS[0:NB, i * 512:(i + 1) * 512]
                        act.activation(dst, pair[proj_pair(key)][0:rows, 0, :], ACT.Copy
                                       ).then_inc(sem("proj_read_act"), 1)
                for m in range(KT):
                    evac(("gr", m), obT[:, m, :], ACT.Silu)
                act.wait_ge(sem("gl_scan"), 1)
                own.tick(act.activation(EG, GB[:, :, T:TA], ACT.Exp))
                act.activation(EB, GB[:, :, P - 1:T:P], ACT.Exp).then_inc(sem("gl_eb"), 1)
                for h in range(GH):
                    for i in range(NLV):
                        u = h * NLV + i
                        act.wait_ge(sem("gl_d"), u + 1)
                        act.activation(W[u % 2], W[u % 2], ACT.Exp).then_inc(sem("gl_w"), 1)
                    act.wait_ge(sem("gl_ek"), h + 1)
                    own.tick(act.activation(W[0], W[0], ACT.Exp))
                    act.activation(W[1], GB[:, h, 0:T], ACT.Exp).then_inc(sem("gl_ew"), 1)
                    act.wait_ge(sem("gl_kt"), h + 1)
                    act.activation(KKT, bank[6], ACT.Copy).then_inc(sem("gl_kts"), 1)
                    act.wait_ge(sem("gl_o"), h + 1)
                    for vh in range(2):
                        last = act.activation(OSQ[vh], bank[2 + vh], ACT.Square)
                        if vh == 0:
                            own.tick(last)
                    last.then_inc(sem("gl_osq"), 1)
                    act.wait_ge(sem("gl_oms"), h + 1)
                    act.activation(MS1, MS1, ACT.Sqrt).then_inc(sem("gl_ort"), 1)

            @block.vector
            def _(dve):
                own = Own(dve, sem("dve_own"), own_counts["dve"])
                for h in range(GH):
                    dve.wait_ge(sem("gl_zp"), h + 1)
                    dve.tensor_scalar(two(GB[:, h, :]), both(2 + h % 2), par[:, PR["gba"] + h:PR["gba"] + h + 1],
                                      None, ALU.add).then_inc(sem("gl_z"), 1)
                dve.wait_ge(sem("gl_z"), GH)
                dve.wait_ge(sem("gl_ln"), 1)
                nz = NZ.rearrange("p (h t) -> p h t", h=GH)
                own(dve.scalar_tensor_tensor(GB, GB, 0.0, nz, ALU.min, ALU.subtract))
                own(dve.tensor_scalar(GB, GB, 1.0 / 16, None, ALU.mult))
                onesw = con[:, CC["ones"][0]:CC["ones"][0] + P]
                for h in range(GH):
                    for c_ in range(NT):
                        g = GB[:, h, c_ * P:(c_ + 1) * P]
                        last = own.tick(dve.tensor_tensor_scan(g, onesw, g, 0.0, ALU.mult, ALU.add))
                own.wait()
                dve.nop().then_inc(sem("gl_scan"), 1)
                for i in range(2):
                    own(dve.memset(QP[i], 0.0))
                    own(dve.memset(KP[i], 0.0))
                dve.wait_ge(sem("gl_eb"), 1)

                def diff(h, i):
                    u, half = h * NLV + i, LEVELS[i]
                    b, d = halves(GB[:, h, 0:T], half), halves(W[u % 2], half)
                    mid = b[:, :, 0, half - 1:half].to_broadcast([P, T // (2 * half), half])
                    own.tick(dve.tensor_tensor(d[:, :, 1, :], b[:, :, 1, :], mid, ALU.subtract))
                    dve.tensor_tensor(d[:, :, 0, :], mid, b[:, :, 0, :], ALU.subtract).then_inc(sem("gl_d"), 1)

                def qk(h, i):
                    u, half = h * NLV + i, LEVELS[i]
                    dve.wait_ge(sem("gl_w"), u + 1)
                    v = h * (NLV + 1) + i
                    if v >= 2:
                        dve.wait_ge(sem("gl_a"), v - 1)
                    w_ = halves(W[u % 2], half)
                    own.tick(dve.tensor_tensor(halves(QP[u % 2], half)[:, :, 1, :], halves(GQ[:, h, 0:T], half)[:, :, 1, :],
                                               w_[:, :, 1, :], ALU.mult))
                    dve.tensor_tensor(halves(KP[u % 2], half)[:, :, 0, :], halves(GK[:, h, 0:T], half)[:, :, 0, :],
                                      w_[:, :, 0, :], ALU.mult).then_inc(sem("gl_qk"), 1)
                    dve.wait_ge(sem("gl_qk"), u + 1)

                def merge(h, i):
                    v = h * (NLV + 1) + i
                    dve.wait_ge(sem("gl_a"), v + 1)
                    if i:
                        dve.wait_ge(sem("gl_cp"), v)
                    dve.copy_predicated(chunks(AA), rep(lmask[:, i * P:(i + 1) * P], NT),
                                        chunks(bank[4 + v % 2])).then_inc(sem("gl_cp"), 1)

                for h in range(GH):
                    own(dve.memset(AA, 0.0))
                    diff(h, 0)
                    for i in range(NLV):
                        if i + 1 < NLV:
                            diff(h, i + 1)
                        qk(h, i)
                        if i:
                            merge(h, i - 1)
                    merge(h, NLV - 1)
                    merge(h, NLV)
                    b = chunks(GB[:, h, 0:T])
                    dve.tensor_tensor(chunks(W[0]), b[:, :, P - 1:P].to_broadcast([P, NT, P]), b,
                                      ALU.subtract).then_inc(sem("gl_ek"), 1)
                    dve.wait_ge(sem("gl_ew"), h + 1)
                    own.tick(dve.tensor_tensor(QE, GQ[:, h, 0:T], W[1], ALU.mult))
                    dve.tensor_tensor(KK, GK[:, h, 0:T], W[0], ALU.mult).then_inc(sem("gl_kk"), 1)
                    dve.wait_ge(sem("gl_kk"), h + 1)
                    dve.wait_ge(sem("gl_u"), h + 1)
                    if h:
                        dve.wait_ge(sem("pgla_out"), 16 * h)
                    own(dve.tensor_copy(ST[:, 0, :], bank[0][:, 0:DV]))
                    for c_ in range(1, NT):
                        last = dve.scalar_tensor_tensor(ST[:, c_, :], ST[:, c_ - 1, :], EB[:, h, c_:c_ + 1],
                                                        bank[c_ // 2][:, (c_ % 2) * DV:(c_ % 2 + 1) * DV],
                                                        ALU.mult, ALU.add)
                        if c_ < NT - 1:
                            own(last)
                    last.then_inc(sem("gl_s"), 1)
                    dve.wait_ge(sem("gl_osum"), h + 1)
                    dve.tensor_scalar(MS1, bank[7], 1.0 / DV, EPS, ALU.mult, ALU.add).then_inc(sem("gl_oms"), 1)
                    dve.wait_ge(sem("gl_ort"), h + 1)
                    own(dve.reciprocal(MS1, MS1))
                    for vh in range(2):
                        own(dve.scalar_tensor_tensor(OSQ[vh], bank[2 + vh], par[:, PR["gno"] + vh:PR["gno"] + vh + 1],
                                                     MS1, ALU.mult, ALU.mult))
                        o = obT[:, 2 * h + vh, 0:T]
                        own(dve.tensor_tensor(o, o, OSQ[vh], ALU.mult))

        sp2 = Space(arena[:, :])
        sp2.at = keep1
        S0 = [sp2.take(GH, DV) for _ in range(3)]
        SN = [sp2.take(GH, DV) for _ in range(3)]
        KS = sp2.take(GH * DK)
        KD = [sp2.take(GH * DK) for _ in range(2)]
        OS = sp2.take(KT * NB)
        OS2 = sp2.take(KT * NB)
        MS2 = sp2.take(GH * NB)
        KSF = sp2.take(NB * NPG)
        NPOOL = A["cache_cmp_kv"].shape[1]
        with nc.Block() as block:
            @block.sync
            def _(sp):
                def load(b):
                    if b >= 3:
                        sp.wait_ge(sem("gs_s"), b - 2)
                    sp.dma_start(S0[b % 3], A["state_gla"][l][b].rearrange("h d v -> d h v")
                                 ).then_inc(sem(f"s0_in{b % 3}"), 16)
                for b in range(3):
                    load(b)
                for b in range(NB):
                    sp.wait_ge(sem("gs_s"), b + 1)
                    sp.dma_start(O["s_gla"][l][b].rearrange("h d v -> d h v"), SN[b % 3]
                                 ).then_inc(sem(f"sgla_out{b % 3}"), 16)
                    if b + 3 < NB:
                        load(b + 3)
                for i in range(3):
                    sp.wait_ge(sem(f"sgla_out{i}"), 16 * len(range(i, NB, 3)))

            @block.tensor
            def _(pe):
                for h in range(GH):
                    last = pe.transpose(bank[7][0:NB, h * DK:(h + 1) * DK], GK[:, h, T:TA], ident)
                last.then_inc(sem("gs_kt"), 1)

                def outer(b):
                    pe.wait_ge(sem("gs_kd"), b + 1)
                    if b >= 2:
                        pe.wait_ge(sem("gs_s"), b - 1)
                    for h in range(GH):
                        last = pe.matmul(pair[b % 2][:, h // 2, (h % 2) * DV:(h % 2 + 1) * DV],
                                         KD[b % 2][0:NB, h * DK:(h + 1) * DK], GVS[0:NB, h * DV:(h + 1) * DV],
                                         start=True, stop=True)
                    last.then_inc(sem("gs_u"), 1)

                outer(0)
                for b in range(NB):
                    if b + 1 < NB:
                        outer(b + 1)
                    pe.wait_ge(sem("gs_s"), b + 1)
                    for h in range(GH):
                        for vh in range(2):
                            j = (h * 2 + vh) * NB + b
                            last = pe.matmul(bank[4][:, j:j + 1], SN[b % 3][:, h, vh * P:(vh + 1) * P],
                                             GQ[:, h, T + b:T + b + 1], start=True, stop=True)
                    last.then_inc(sem("gs_o"), 1)
                pe.wait_ge(sem("gs_osq"), 1)
                sq = OS.rearrange("p (h v b) -> p h v b", h=GH, v=2)
                for vh in range(2):
                    last = pe.matmul(bank[5][:, 0:GH * NB], ones, sq[:, :, vh, :], start=(vh == 0), stop=(vh == 1))
                last.then_inc(sem("gs_osum"), 1)

            @block.scalar
            def _(act):
                act.wait_ge(sem("gs_o"), NB)
                act.activation(OS, bank[4][:, 0:KT * NB], ACT.Square).then_inc(sem("gs_osq"), 1)
                act.wait_ge(sem("gs_oms"), 1)
                act.activation(MS2, MS2, ACT.Sqrt).then_inc(sem("gs_ort"), 1)

            @block.vector
            def _(dve):
                own = Own(dve, sem("dve_own"), own_counts["dve"])
                for ct in range(NB // 2):
                    own(dve.scalar_tensor_tensor(gather[:, 4 * ct:4 * ct + 4], pg_rows[:, ct:ct + 1].to_broadcast([P, 4]),
                                                 32.0, c("crow"), ALU.mult, ALU.add))
                for kv in range(2):
                    own(dve.tensor_scalar(gather[:, 16 + kv * 64:80 + kv * 64], pg_rows[:, NB // 2:], 256.0, c("srow"),
                                          ALU.mult, ALU.add))
                own(dve.tensor_scalar(pg_rows[:, :], pg_rows[:, :], float(NPOOL), None, ALU.add))
                own(dve.tensor_copy(KSF, gather[:, 80:144]))
                own(dve.tensor_scalar(gather[:, 80:144], KSF, 1.0, None, ALU.add))
                dve.wait_ge(sem("gs_kt"), 1)
                own(dve.tensor_copy(KS[0:NB, :], bank[7][0:NB, :]))

                def one_token(b):
                    if b >= 2:
                        dve.wait_ge(sem("gs_u"), b - 1)
                    dve.tensor_scalar(KD[b % 2][0:NB, :], KS[0:NB, :], ident[0:NB, b:b + 1], None,
                                      ALU.mult).then_inc(sem("gs_kd"), 1)

                one_token(0)
                one_token(1)
                for b in range(NB):
                    dve.wait_ge(sem("gs_u"), b + 1)
                    dve.wait_ge(sem(f"s0_in{b % 3}"), 16 * (b // 3 + 1))
                    if b >= 3:
                        dve.wait_ge(sem("gs_o"), b - 2)
                        dve.wait_ge(sem(f"sgla_out{b % 3}"), 16 * (b // 3))
                    for h in range(GH):
                        last = dve.scalar_tensor_tensor(SN[b % 3][:, h, :], S0[b % 3][:, h, :], EG[:, h, b:b + 1],
                                                        pair[b % 2][:, h // 2, (h % 2) * DV:(h % 2 + 1) * DV],
                                                        ALU.mult, ALU.add)
                    last.then_inc(sem("gs_s"), 1)
                    if b + 2 < NB:
                        one_token(b + 2)
                dve.wait_ge(sem("gs_osum"), 1)
                dve.tensor_scalar(MS2, bank[5][:, 0:GH * NB], 1.0 / DV, EPS, ALU.mult, ALU.add).then_inc(sem("gs_oms"), 1)
                dve.wait_ge(sem("gs_ort"), 1)
                own(dve.reciprocal(MS2, MS2))
                m = MS2.rearrange("p (h b) -> p h b", h=GH)
                o = bank[4][:, 0:KT * NB].rearrange("p (h v b) -> p h v b", h=GH, v=2)
                t = OS2.rearrange("p (h v b) -> p h v b", h=GH, v=2)
                for vh in range(2):
                    own(dve.scalar_tensor_tensor(t[:, :, vh, :], o[:, :, vh, :], par[:, PR["gno"] + vh:PR["gno"] + vh + 1],
                                                 m, ALU.mult, ALU.mult))
                own(dve.tensor_tensor(obT[:, :, T:TA], obT[:, :, T:TA], OS2.rearrange("p (k b) -> p k b", k=KT), ALU.mult))


        sp3 = Space(arena[:, :])
        GATE = sp3.take(NT, 3 * NH)
        KCP = sp3.take(G, NCP)
        VCP = sp3.take(2 * P)
        keep3 = sp3.at
        gs_row = sp3.take(3 * NH)
        CR = [sp3.take(512) for _ in range(NT + 1)]
        R = [sp3.take(4, 512) for _ in range(2)]
        R2 = [sp3.take(8, 2 * DH) for _ in range(3)]
        CT = [sp3.take(512) for _ in range(3)]
        PH = sp3.take(2, 8, P)
        P1 = [sp3.take(512) for _ in range(2)]
        NKC = 2 * NB * NCS
        oc3 = Space(OCF)
        KC = oc3.take(NKC + 2 * NCP)
        VC = oc3.take(NKC + 2 * NCP)
        SQ3, MS3 = oc3.take(544), oc3.take(544)
        PER = oc3.take(P)
        PEV = oc3.take(32)
        BIA = oc3.take(2)
        CTN = NB // 2 + 1

        def comp_cols(base, ct, gp):
            if ct < CTN - 1:
                v = base[:, 0:NKC].rearrange("p (a b n) -> p a b n", a=2, b=NB)
                return v[:, gp, 2 * ct:2 * ct + 2, :]
            return base[:, NKC + gp * NCP:NKC + (gp + 1) * NCP].unsqueeze(1)

        def page_reg(eng, b, t):
            return eng.value_load(pages[0:1, b * NPG + t:b * NPG + t + 1], min_val=0,
                                  max_val=A["cache_cmp_kv"].shape[1] - 1)

        with nc.Block() as block:
            @block.sync
            def _(sp):
                for kv, t in enumerate(("nsa_phi_k", "nsa_phi_v")):
                    v = A[t][l].rearrange("(r s a) d e -> r a d s e", r=2, a=2)
                    for hf in range(2):
                        for a in range(2):
                            sp.dma_start(PH[a * DH:(a + 1) * DH, kv, :, hf * DH:(hf + 1) * DH], v[hf, a]
                                         ).then_inc(sem("par_in"), 16)
                sp.dma_start(PER[0:32, :], A["nsa_cmp_pe"][l].rearrange("k (r s a) d -> (k r s) (a d)", r=2, a=2)
                             ).then_inc(sem("par_in"), 16)
                loads_of_phase(sp, 2, l)
                for j in range(4 * CTN):
                    ct, qt = j // 4, j % 4
                    if ct == CTN - 1:
                        sp.wait_ge(sem("cr_paired"), 2 * (j - 1))
                        got = sem(f"pr_in{j % 2}")
                        if qt == 0:
                            for tt in range(NT):
                                sp.wait_ge(sem("proj_read_act"), sum(
                                    1 for k, e in TILES[:TI[("cmp", tt)] + 1] if e == "act"))
                                sp.dma_start(O["p_cmp_kv"][l][0, tt * P:(tt + 1) * P].rearrange(
                                    "t k g d -> t (k g d)"), CR[tt]).then_inc(sem("cmp_out"), 16)
                            sp.wait_ge(sem("proj_read_act"), sum(
                                1 for k, e in TILES[:TI[("cmp", NT)] + 1] if e == "act"))
                            sp.dma_start(O["s_cmp_kv"][l][:, 0].rearrange("t k g d -> t (k g d)"), CR[NT][0:NB, :]
                                         ).then_inc(sem("cmp_out"), 16)
                            sp.dma_start(gate_rows, gs_row[0:NB, :]).then_inc(sem("cmp_out"), 16)
                            sp.wait_ge(sem("cmp_out"), 16 * (NT + 2))
                            sp.dma_start(gate_s[:, :], gate_rows.rearrange("b (h r) -> (b h) r", r=3)
                                         ).then_inc(sem("gates_in"), 16)
                        src = O["p_cmp_kv"][l][0].rearrange("(n s) k g d -> n s (k g d)", s=STR)
                        sp.dma_start(R[j % 2][0:NCP], src[:, 4 * qt:4 * qt + 4, :]).then_inc(got, 16)
                sp.wait_ge(sem("gates_in"), 16)
                sp.wait_ge(sem("kc_done"), 1)
                sp.dma_start(cmp_rows[0], KC[:, 0:NKC]).then_inc(sem("kc_out"), 16)
                sp.dma_start(cmp_rows[1], VC[:, 0:NKC]).then_inc(sem("kc_out"), 16)
                sp.wait_ge(sem("kc_out"), 32)

            @block.gpsimd
            def _(pool):
                rows = A["cache_cmp_kv"].rearrange("l p (c q s) k g d -> (l p c q) (s k g d)", c=8, q=4)

                def fetch(j):
                    if j < 4 * (CTN - 1):
                        pool.indirect_dma_start(R[j % 2].rearrange("p s n -> p (s n)"), None, rows,
                                                bass.IndirectOffsetOnAxis(gather[:, j:j + 1], 0)
                                                ).then_inc(sem(f"cr_in{j % 2}"), 16)

                fetch(0)
                fetch(1)
                pool.memset(KC, 0.0)
                pool.memset(VC, 0.0).then_inc(sem("kc_zero"), 1)
                for w_ in range(8 * CTN):
                    j = w_ // 2
                    if w_ % 2 == 0:
                        if j // 4 < CTN - 1:
                            pool.wait_ge(sem(f"cr_in{j % 2}"), 16 * (j // 2 + 1))
                        else:
                            pool.wait_ge(sem(f"pr_in{j % 2}"), 16 * (j // 2 + 1 - 2 * (CTN - 1)))
                    if w_ >= 3:
                        pool.wait_ge(sem("cr_used"), 2 * w_ - 4)
                    n = P if j // 4 < CTN - 1 else NCP
                    src = R[j % 2][0:n, 2 * (w_ % 2):2 * (w_ % 2) + 2, :].rearrange("p s (k d) -> p k s d", d=DH)
                    pool.tensor_copy(R2[w_ % 3][0:n].rearrange("p k (s d) -> p k s d", s=2), src
                                     ).then_inc(sem("cr_paired"), 1)
                    if w_ % 2:
                        pool.wait_ge(sem("cr_paired"), w_ + 1)
                        fetch(j + 2)

            @block.tensor
            def _(pe):
                w = open_slab(pe, "gate")
                for tt in range(NT + 1):
                    proj_rows(pe, ("gate", tt), tt, w, 3 * NH)
                w = open_slab(pe, "cmp")
                for tt in range(NT + 1):
                    proj_rows(pe, ("cmp", tt), tt, w, 512)
                pe.wait_ge(sem("par_in"), PAR_IN + 16 * 9)
                pe.transpose(bank[4][:, 0:32], PER[0:32, :], ident[0:32, 0:32]).then_inc(sem("pe_turned"), 1)
                pe.wait_ge(sem("pe_set"), 1)
                for kv in range(2):
                    for hf in range(2):
                        for s_ in range(8):
                            last = pe.matmul(bank[5][0:DH, kv:kv + 1], PH[:, kv, s_, hf * DH:(hf + 1) * DH],
                                             PEV[:, kv * 16 + hf * 8 + s_:kv * 16 + hf * 8 + s_ + 1],
                                             start=(hf == 0 and s_ == 0), stop=(hf == 1 and s_ == 7))
                last.then_inc(sem("bias_done"), 1)
                pe.wait_ge(sem("bias_set"), 1)

                def turn(z):
                    j, sp2_, kv = z // 4, (z // 2) % 2, z % 2
                    if kv == 0:
                        pe.wait_ge(sem("cr_paired"), z // 2 + 1)
                    if z >= 2:
                        pe.wait_ge(sem("ct_act" if kv == 0 else "ct_dve"), (z - 2) // 2 + 1)
                    n = P if j // 4 < CTN - 1 else NCP
                    for g in range(G):
                        last = pe.transpose(bank[4 + kv][:, g * P:g * P + n],
                                            R2[z // 2 % 3][0:n, kv * G + g, :],
                                            ident[0:n, 0:n])
                    last.then_inc(sem("cr_used"), 1)

                def accumulate(z):
                    j, sp2_, kv = z // 4, (z // 2) % 2, z % 2
                    ct, qt = j // 4, j % 4
                    pe.wait_ge(sem("ct_act" if kv == 0 else "ct_dve"), z // 2 + 1)
                    if qt == 0 and sp2_ == 0 and ct >= 2:
                        pe.wait_ge(sem("ct_sum"), 2 * (ct - 1))
                    acc = bank[6 + kv] if ct % 2 == 0 else bank[2 + kv]
                    n = P if ct < CTN - 1 else NCP
                    src = CT[z % 3].rearrange("p (g n) -> p g n", g=G)[:, :, 0:n]
                    dst = acc.rearrange("p (g n) -> p g n", g=G)[:, :, 0:n]
                    pe.matmul(dst, PH[:, kv, 2 * qt + sp2_, :], src, start=(qt == 0 and sp2_ == 0),
                              stop=(qt == 3 and sp2_ == 1)).then_inc(sem("ct_mm"), 1)

                pe.wait_ge(sem("proj_read_act"), sum(1 for k, e in TILES[:TI[("cmp", NT)] + 1] if e == "act"))
                turn(0)
                for z in range(16 * CTN):
                    if z + 1 < 16 * CTN:
                        turn(z + 1)
                    accumulate(z)
                for i in range(2):
                    pe.wait_ge(sem("kc_sq"), i + 1)
                    for half in range(2):
                        last = pe.matmul(pair[2][:, half, 0:272], blk, SQ3[:, half * 272:(half + 1) * 272],
                                         start=True, stop=True)
                    last.then_inc(sem("kc_ssum"), 1)
                for gp in range(2):
                    last = pe.transpose(bank[6][0:NCP, gp * P:(gp + 1) * P], VC[:, NKC + gp * NCP:NKC + (gp + 1) * NCP],
                                        ident)
                last.then_inc(sem("vc_turned"), 1)

            @block.scalar
            def _(act):
                own = Own(act, sem("act_own"), own_counts["act"])

                def part1(act, ct):
                    act.wait_ge(sem("ct_mm"), 16 * (ct + 1))
                    if ct:
                        act.wait_ge(sem("ct_sum"), 2 * ct)
                    for kv in range(2):
                        acc = bank[6 + kv] if ct % 2 == 0 else bank[2 + kv]
                        n = P if ct < CTN - 1 else NCP
                        act.activation(P1[kv].rearrange("p (g n) -> p g n", g=G)[0:DH, :, 0:n],
                                       acc.rearrange("p (g n) -> p g n", g=G)[DH:P, :, 0:n], ACT.Copy
                                       ).then_inc(sem("ct_p1"), 1)

                for tt in range(NT + 1):
                    wait_proj(act, ("gate", tt))
                    rows = P if tt < NT else NB
                    dst = GATE[:, tt, :] if tt < NT else gs_row[0:NB, :]
                    act.activation(dst, pair[proj_pair(("gate", tt))][0:rows, 0, 0:3 * NH], ACT.Sigmoid
                                   ).then_inc(sem("proj_read_act"), 1)
                for tt in range(NT + 1):
                    wait_proj(act, ("cmp", tt))
                    rows = P if tt < NT else NB
                    act.activation(CR[tt][0:rows, :], pair[proj_pair(("cmp", tt))][0:rows, 0, :], ACT.Copy
                                   ).then_inc(sem("proj_read_act"), 1)
                act.wait_ge(sem("pe_turned"), 1)
                act.activation(PEV, bank[4][:, 0:32], ACT.Copy).then_inc(sem("pe_set"), 1)
                for z in range(0, 16 * CTN, 2):
                    act.wait_ge(sem("cr_used"), z + 1)
                    if z >= 3:
                        act.wait_ge(sem("ct_mm"), z - 2)
                    n = P if z // 16 < CTN - 1 else NCP
                    act.activation(CT[z % 3].rearrange("p (g n) -> p g n", g=G)[:, :, 0:n],
                                   bank[4].rearrange("p (g n) -> p g n", g=G)[:, :, 0:n], ACT.Copy
                                   ).then_inc(sem("ct_act"), 1)
                    ct = z // 16
                    if z % 16 == 2 and ct >= 1:
                        part1(act, ct - 1)
                part1(act, CTN - 1)
                act.wait_ge(sem("ct_sum"), 2 * CTN)
                for i in range(2):
                    if i:
                        act.wait_ge(sem("kc_ssum"), i)
                    act.activation(SQ3, KC[:, i * 544:(i + 1) * 544], ACT.Square).then_inc(sem("kc_sq"), 1)
                    act.wait_ge(sem("kc_ms"), i + 1)
                    act.activation(MS3, MS3, ACT.Sqrt).then_inc(sem("kc_rt"), 1)
                act.wait_ge(sem("vc_turned"), 1)
                own(act.activation(VCP[0:NCP, :], bank[6][0:NCP, 0:2 * P], ACT.Copy))

            @block.vector
            def _(dve):
                own = Own(dve, sem("dve_own"), own_counts["dve"])

                def add_parts(ct):
                    dve.wait_ge(sem("ct_p1"), 2 * ct + 2)
                    nb, n = (2, NCS) if ct < CTN - 1 else (1, NCP)
                    for kv, base in enumerate((KC, VC)):
                        acc = bank[6 + kv] if ct % 2 == 0 else bank[2 + kv]
                        for g in range(G):
                            a = (g % 2) * DH
                            first = acc[0:DH, g * P:g * P + nb * n].rearrange("p (b n) -> p b n", b=nb)[:, :, 0:n - 1]
                            second = P1[kv][0:DH, g * P:g * P + nb * n].rearrange("p (b n) -> p b n", b=nb)[:, :, 1:n]
                            dst = comp_cols(base, ct, g // 2)[a:a + DH, :, 0:n - 1]
                            last = dve.scalar_tensor_tensor(dst, second, BIA[0:DH, kv:kv + 1], first, ALU.add, ALU.add)
                        last.then_inc(sem("ct_sum"), 1)

                dve.wait_ge(sem("kc_zero"), 1)
                dve.wait_ge(sem("bias_done"), 1)
                dve.tensor_copy(BIA[0:DH, :], bank[5][0:DH, 0:2]).then_inc(sem("bias_set"), 1)
                dve.wait_ge(sem("bias_set"), 1)
                for z in range(1, 16 * CTN, 2):
                    dve.wait_ge(sem("cr_used"), z + 1)
                    if z >= 3:
                        dve.wait_ge(sem("ct_mm"), z - 2)
                    n = P if z // 16 < CTN - 1 else NCP
                    dve.tensor_copy(CT[z % 3].rearrange("p (g n) -> p g n", g=G)[:, :, 0:n],
                                    bank[5].rearrange("p (g n) -> p g n", g=G)[:, :, 0:n]).then_inc(sem("ct_dve"), 1)
                    ct = z // 16
                    if z % 16 == 5 and ct >= 1:
                        add_parts(ct - 1)
                add_parts(CTN - 1)
                dve.wait_ge(sem("ct_sum"), 2 * CTN)
                for i in range(2):
                    dve.wait_ge(sem("kc_ssum"), i + 1)
                    dve.tensor_scalar(MS3.rearrange("p (a b) -> p a b", a=2), pair[2][:, :, 0:272], 1.0 / DH, EPS,
                                      ALU.mult, ALU.add).then_inc(sem("kc_ms"), 1)
                    dve.wait_ge(sem("kc_rt"), i + 1)
                    own(dve.reciprocal(MS3, MS3))
                    k = KC[:, i * 544:(i + 1) * 544]
                    own(dve.scalar_tensor_tensor(k, k, par[:, PR["kn"]:PR["kn"] + 1], MS3, ALU.mult, ALU.mult))
                own(dve.memset(KCP, 0.0))
                for a in range(2):
                    own(dve.tensor_copy(KCP[a * DH:(a + 1) * DH, a::2, :], KC[a * DH:(a + 1) * DH, NKC:].rearrange(
                        "p (g n) -> p g n", g=2)))
                dve.nop().then_inc(sem("kc_done"), 1)

        sp4 = Space(arena[:, :])
        sp4.at = keep3
        NQ = sp4.take(KT, TA)
        KTR = [sp4.take(G, T) for _ in range(2)]
        VR = [sp4.take(NT, 256) for _ in range(2)]
        keep4 = sp4.at
        SQ4 = [sp4.take(TA) for _ in range(3)]
        oc4 = Space(OCF)
        ROW = [oc4.take(512) for _ in range(5)]
        MS4 = [oc4.take(TA) for _ in range(3)]
        qg = oc4.take(1)
        chain = [(n, tt) for n in ("slc", "win") for tt in range(NT + 1)] + [("nq", i) for i in range(KT)]
        NKV = 2 * (NT + 1)

        def rows_of(q):
            return P if chain[q][1] < NT else NB

        with nc.Block() as block:
            @block.sync
            def _(sp):
                loads_of_phase(sp, 3, l)

            @block.gpsimd
            def _(pool):
                for br in range(2):
                    for a in range(2):
                        pool.memset(KTR[br][(1 - a) * DH:(2 - a) * DH, a::2, :], 0.0)

            @block.tensor
            def _(pe):
                slabs = {}

                def proj(q):
                    n, i = chain[q]
                    name = n if n != "nq" else f"nq{i // 4}"
                    if name not in slabs:
                        slabs[name] = open_slab(pe, name)
                    w = slabs[name]
                    if n != "nq":
                        proj_rows(pe, (n, i), i, w, 512)
                    else:
                        proj_T(pe, (n, i), lambda k: w[:, k, (i % 4) * P:(i % 4 + 1) * P], hT)

                def sums(q):
                    if q < NKV:
                        return
                    pe.wait_ge(sem("kq_sq"), q + 1)
                    if q > NKV:
                        pe.wait_ge(sem("kq_ms"), q)
                    for half in range(2):
                        last = pe.matmul(pair[3][:, half, 0:HA], blk, SQ4[q % 3][:, half * HA:(half + 1) * HA],
                                         start=True, stop=True)
                    last.then_inc(sem("kq_sum"), 1)

                def turn(q):
                    if q >= NKV or q < 0:
                        return
                    r_ = rows_of(q)
                    pe.wait_ge(sem("kq_norm"), q + 1)
                    if q >= 2:
                        pe.wait_ge(sem("kq_kt"), q - 1)
                    for gp in range(2):
                        last = pe.transpose(bank[4 + q % 2][:, gp * r_:(gp + 1) * r_], ROW[q % 5][0:r_, gp * P:(gp + 1) * P],
                                            ident[0:r_, 0:r_])
                    last.then_inc(sem("kq_turn"), 1)

                for q in range(len(chain) + 4):
                    if q < len(chain):
                        proj(q)
                    if 1 <= q < len(chain) + 1:
                        sums(q - 1)
                    turn(q - 4)

            @block.scalar
            def _(act):
                own = Own(act, sem("act_own"), own_counts["act"])

                def square(q):
                    act.wait_ge(sem("proj_read_dve"), sum(1 for k, e in TILES[:TI[chain[q]] + 1] if e == "dve"))
                    if q >= 3:
                        act.wait_ge(sem("kq_ms"), q - 2)
                    if q < NKV:
                        r_ = rows_of(q)
                        act.activation(SQ4[q % 3][0:r_, 0:256], ROW[q % 5][0:r_, 0:256], ACT.Square
                                       ).then_inc(sem("kq_sq"), 1)
                    else:
                        act.activation(SQ4[q % 3], NQ[:, chain[q][1], :], ACT.Square).then_inc(sem("kq_sq"), 1)

                def root(q):
                    act.wait_ge(sem("kq_ms"), q + 1)
                    r_, w = (rows_of(q), G) if q < NKV else (P, TA)
                    act.activation(MS4[q % 3][0:r_, 0:w], MS4[q % 3][0:r_, 0:w], ACT.Sqrt).then_inc(sem("kq_rt"), 1)

                def keys(q):
                    act.wait_ge(sem("kq_turn"), q + 1)
                    br, tt, r_ = q // (NT + 1), chain[q][1], rows_of(q)
                    src = bank[4 + q % 2][:, 0:2 * r_].rearrange("p (a t) -> p a t", a=2)
                    if tt < NT:
                        for a in range(2):
                            own.tick(act.activation(KTR[br][a * DH:(a + 1) * DH, a::2, tt * P:(tt + 1) * P],
                                                    src[a * DH:(a + 1) * DH], ACT.Copy))
                    else:
                        own.tick(act.activation(knewT[:, br, :, :], src, ACT.Copy))
                    v = ROW[q % 5][0:r_, 256:512]
                    act.activation(VR[br][:, tt, :] if tt < NT else vnew[:, br, :], v, ACT.Copy
                                   ).then_inc(sem("kq_kt"), 1)
                    out = {("slc", 0): "p_slc_kv", ("win", 0): "p_win_kv", ("slc", 1): "s_slc_kv",
                           ("win", 1): "s_win_kv"}[chain[q][0], int(tt == NT)]
                    if tt < NT:
                        dst = O[out][l][0, tt * P:(tt + 1) * P]
                    else:
                        dst = O[out][l][:, 0 if out == "s_slc_kv" else WIN - 1]
                    act.wait_ge(sem("kq_norm"), q + 1)
                    act.dma_start(dst.rearrange("t k g d -> t (k g d)"), ROW[q % 5][0:r_, :]
                                  ).then_inc(sem(f"kv_out{q % 5}"), 16)

                for q in range(len(chain) + 4):
                    if q < len(chain):
                        square(q)
                    if 2 <= q < len(chain) + 2:
                        root(q - 2)
                    if 4 <= q < NKV + 4:
                        keys(q - 4)
                for i in range(5):
                    act.wait_ge(sem(f"kv_out{i}"), 16 * len(range(i, NKV, 5)))

            @block.vector
            def _(dve):
                own = Own(dve, sem("dve_own"), own_counts["dve"])
                own(dve.tensor_scalar(qg, par[:, PR["qn"]:PR["qn"] + 1], DH ** -0.5, None, ALU.mult))

                def evac(q):
                    wait_proj(dve, chain[q])
                    src = pair[proj_pair(chain[q])]
                    if q < NKV:
                        r_ = rows_of(q)
                        if q >= 5:
                            dve.wait_ge(sem("kq_kt"), q - 4)
                            dve.wait_ge(sem(f"kv_out{q % 5}"), 16 * (q // 5))
                        dve.tensor_copy(ROW[q % 5][0:r_, :], src[0:r_, 0, :]).then_inc(sem("proj_read_dve"), 1)
                    else:
                        dve.tensor_copy(two(NQ[:, chain[q][1], :]), src[:, :, 0:HA]).then_inc(sem("proj_read_dve"), 1)

                def mean(q):
                    dve.wait_ge(sem("kq_sq"), q + 1)
                    m = MS4[q % 3]
                    if q < NKV:
                        r_ = rows_of(q)
                        own(dve.reduce_sum(m[0:r_, 0:G], SQ4[q % 3][0:r_, 0:256].rearrange("p (g d) -> p g d", g=G), AX.X))
                        dve.tensor_scalar(m[0:r_, 0:G], m[0:r_, 0:G], 1.0 / DH, EPS, ALU.mult, ALU.add
                                          ).then_inc(sem("kq_ms"), 1)
                    else:
                        dve.wait_ge(sem("kq_sum"), q - NKV + 1)
                        dve.tensor_scalar(two(m), pair[3][:, :, 0:HA], 1.0 / DH, EPS, ALU.mult, ALU.add
                                          ).then_inc(sem("kq_ms"), 1)

                def scale(q):
                    dve.wait_ge(sem("kq_rt"), q + 1)
                    m = MS4[q % 3]
                    if q < NKV:
                        r_, br = rows_of(q), q // (NT + 1)
                        own(dve.reciprocal(m[0:r_, 0:G], m[0:r_, 0:G]))
                        k = ROW[q % 5][0:r_, 0:256].rearrange("p (g d) -> p g d", g=G)
                        own(dve.tensor_tensor(k, k, bc(m[0:r_, 0:G], DH), ALU.mult))
                        dve.tensor_tensor(k, k, rep(kgain[0:r_, br, :], G), ALU.mult).then_inc(sem("kq_norm"), 1)
                        dve.wait_ge(sem("kq_norm"), q + 1)
                    else:
                        own(dve.reciprocal(m, m))
                        x = NQ[:, chain[q][1], :]
                        own(dve.scalar_tensor_tensor(x, x, qg, m, ALU.mult, ALU.mult))

                for q in range(len(chain) + 3):
                    if q < len(chain):
                        evac(q)
                    if 2 <= q < len(chain) + 2:
                        mean(q - 2)
                    if q >= 3:
                        scale(q - 3)
                own(dve.tensor_copy(nqs[:, :, :], NQ[:, :, T:TA]))

        sp5 = Space(arena[:, :])
        sp5.at = keep4
        SC = [sp5.take(T) for _ in range(4)]
        free_slot = ring[:, (MARKS[3] + NSLOT - 1) % NSLOT, :]
        PTS = [free_slot[:, i * NT * T:(i + 1) * NT * T].rearrange("p (k n) -> p k n", k=NT) for i in range(2)]
        stat = sp5.take(4, 3, 4)
        S_BANK, T_BANK = (0, 1, 6), (2, 3, 7)
        units = []
        for i in range(NT):
            for g in range(G):
                units.append((i, g, 0, None))
                units += [(i, g, br, p_) for br in (1, 2) for p_ in range(HPG)]
        NU = len(units)
        last_unit = [9 * (v // 3) + (0, 4, 8)[v % 3] for v in range(3 * NT * G)]
        branch_of = {u: v for v, u in enumerate(last_unit)}
        U2V = [3 * (u // 9) + (0 if u % 9 == 0 else 1 + (u % 9 - 1) // 4) for u in range(NU)]

        with nc.Block() as block:
            @block.tensor
            def _(pe):
                def scores(u):
                    i, g, br, p_ = units[u]
                    a, gp = (g % 2) * DH, g // 2
                    if u >= 3:
                        pe.wait_ge(sem("sa_read"), u - 2)
                    out = bank[S_BANK[u % 3]]
                    if br == 0:
                        for h in range(HPG):
                            last = pe.matmul(out[:, h * NCP:(h + 1) * NCP], NQ[:, gp * 4 + h, i * P:(i + 1) * P],
                                             KCP[:, g, :], start=True, stop=True)
                    else:
                        n = (i + 1) * P
                        last = pe.matmul(out[:, 0:n], NQ[:, gp * 4 + p_, i * P:(i + 1) * P],
                                         KTR[br - 1][:, g, 0:n], start=True, stop=True)
                    last.then_inc(sem("sa_s"), 1)

                def turn(u):
                    i, g, br, p_ = units[u]
                    pe.wait_ge(sem("sa_p"), u + 1)
                    if u >= 3:
                        pe.wait_ge(sem("sa_pt"), u - 2)
                    out = bank[T_BANK[u % 3]]
                    if br == 0:
                        for h in range(HPG):
                            last = pe.transpose(out[0:NCP, h * P:(h + 1) * P], SC[u % 4][:, h * NCP:(h + 1) * NCP], ident)
                    else:
                        for kt in range(i + 1):
                            last = pe.transpose(out[:, kt * P:(kt + 1) * P], SC[u % 4][:, kt * P:(kt + 1) * P], ident)
                    last.then_inc(sem("sa_t"), 1)

                def values(v):
                    i, g, br, _ = units[last_unit[v]]
                    a = (g % 2) * DH
                    pe.wait_ge(sem("sa_pt"), last_unit[v] + 1)
                    q = v // 3
                    if br == 0 and q >= 2:
                        pe.wait_ge(sem("sa_o"), q - 1)
                    out = bank[4 + q % 2][a:a + DH, :]
                    if br == 0:
                        last = pe.matmul(out, VCP[0:NCP, g * DH:(g + 1) * DH], PTS[v % 2][0:NCP, 0, :],
                                         start=True, stop=False)
                    else:
                        for kt in range(i + 1):
                            last = pe.matmul(out, VR[br - 1][:, kt, g * DH:(g + 1) * DH], PTS[v % 2][:, kt, :],
                                             start=False, stop=(br == 2 and kt == i))
                    last.then_inc(sem("sa_pv"), 1)

                scores(0)
                scores(1)
                for u in range(NU + 2):
                    if u + 2 < NU:
                        scores(u + 2)
                    if u < NU:
                        turn(u)
                    if u - 2 in branch_of:
                        values(branch_of[u - 2])

            @block.scalar
            def _(act):
                def exps(u):
                    i, g, br, p_ = units[u]
                    act.wait_ge(sem("sa_m"), u + 1)
                    s = SC[u % 4]
                    if br == 0:
                        act.activation(s[:, 0:P], s[:, 0:P], ACT.Exp).then_inc(sem("sa_e"), 1)
                    else:
                        n = (i + 1) * P
                        act.activation(s[:, 0:n], s[:, 0:n], ACT.Exp, bias=stat[:, u % 4, 0, 0:1],
                                       accum_out=stat[:, u % 4, 1, 0:1]).then_inc(sem("sa_e"), 1)

                def copy(u):
                    i, g, br, p_ = units[u]
                    v = U2V[u]
                    act.wait_ge(sem("sa_t"), u + 1)
                    if v >= 2:
                        act.wait_ge(sem("sa_pv"), v - 1)
                    src = bank[T_BANK[u % 3]]
                    if br == 0:
                        act.activation(PTS[v % 2][0:NCP, 0, :], src[0:NCP, :], ACT.Copy).then_inc(sem("sa_pt"), 1)
                    else:
                        act.activation(PTS[v % 2][:, 0:i + 1, p_ * P:(p_ + 1) * P],
                                       src[:, 0:(i + 1) * P].rearrange("p (k t) -> p k t", t=P), ACT.Copy
                                       ).then_inc(sem("sa_pt"), 1)

                def out(q):
                    i, g = q // G, q % G
                    a, gp = (g % 2) * DH, g // 2
                    act.wait_ge(sem("sa_pv"), 3 * q + 3)
                    act.activation(ocT[a:a + DH, gp * 4:gp * 4 + 4, i * P:(i + 1) * P],
                                   bank[4 + q % 2][a:a + DH, :].rearrange("p (h t) -> p h t", h=HPG), ACT.Copy
                                   ).then_inc(sem("sa_o"), 1)

                for u in range(NU + 5):
                    if u < NU:
                        exps(u)
                    if 1 <= u < NU + 1:
                        copy(u - 1)
                    if u >= 5 and (u - 5) % 9 == 8:
                        out((u - 5) // 9)

            @block.vector
            def _(dve):
                own = Own(dve, sem("dve_own"), own_counts["dve"])
                nsl, dist, dcmp, mcmp = c("nsl"), c("dist"), c("dcmp"), c("mcmp")

                def biased(u):
                    i, g, br, p_ = units[u]
                    s, st = SC[u % 4], stat[:, u % 4]
                    if u >= 4:
                        dve.wait_ge(sem("sa_t"), u - 3)
                    dve.wait_ge(sem("sa_s"), u + 1)
                    src = bank[S_BANK[u % 3]]
                    if br == 0:
                        s3 = s[:, 0:P].rearrange("p (h n) -> p h n", h=HPG)
                        own(dve.tensor_tensor(s3, bc(nsl[:, 4 * g:4 * g + 4], NCP),
                                              rep(dcmp[:, i * NCP:(i + 1) * NCP], HPG), ALU.mult))
                        dve.tensor_tensor(s[:, 0:P], s[:, 0:P], src[:, 0:P], ALU.add).then_inc(sem("sa_read"), 1)
                        dve.wait_ge(sem("sa_read"), u + 1)
                        own(dve.reduce_max(st[:, 0, :], s3, AX.X))
                        dve.tensor_tensor(s3, s3, bc(st[:, 0, :], NCP), ALU.subtract).then_inc(sem("sa_m"), 1)
                    else:
                        n = (i + 1) * P
                        dve.scalar_tensor_tensor(s[:, 0:n], dist[:, 384 - i * P:384 - i * P + n], -SLOPE[4 * g + p_],
                                                 src[:, 0:n], ALU.mult, ALU.add).then_inc(sem("sa_read"), 1)
                        dve.wait_ge(sem("sa_read"), u + 1)
                        dve.tensor_reduce(st[:, 0, 0:1], s[:, 0:n], AX.X, ALU.max, negate=True).then_inc(sem("sa_m"), 1)

                def weighted(u):
                    i, g, br, p_ = units[u]
                    s, st = SC[u % 4], stat[:, u % 4]
                    dve.wait_ge(sem("sa_e"), u + 1)
                    if br == 0:
                        s3 = s[:, 0:P].rearrange("p (h n) -> p h n", h=HPG)
                        own(dve.tensor_tensor(s3, s3, rep(mcmp[:, i * NCP:(i + 1) * NCP], HPG), ALU.mult))
                        own(dve.reduce_sum(st[:, 1, :], s3, AX.X))
                        own(dve.tensor_scalar(st[:, 1, :], st[:, 1, :], TINY, None, ALU.max))
                        own(dve.reciprocal(st[:, 1, :], st[:, 1, :]))
                        gt = GATE[:, i, 12 * g:12 * g + 12].rearrange("p (h r) -> p h r", r=3)[:, :, 0]
                        own(dve.tensor_tensor(st[:, 1, :], st[:, 1, :], gt, ALU.mult))
                        dve.tensor_tensor(s3, s3, bc(st[:, 1, :], NCP), ALU.mult).then_inc(sem("sa_p"), 1)
                    else:
                        n = (i + 1) * P
                        own(dve.reciprocal(st[:, 1, 0:1], st[:, 1, 0:1]))
                        k = (4 * g + p_) * 3 + br
                        dve.tensor_scalar(s[:, 0:n], s[:, 0:n], st[:, 1, 0:1], GATE[:, i, k:k + 1], ALU.mult,
                                          ALU.mult).then_inc(sem("sa_p"), 1)

                biased(0)
                for u in range(NU):
                    if u + 1 < NU:
                        biased(u + 1)
                    weighted(u)


        sp6 = Space(arena[:, :])
        KC6, VC6 = sp6.take(2, NB, NCS), sp6.take(2, NB, NCS)
        VCR = sp6.take(NB, 2 * P)
        QBD = sp6.take(NB, 2, P)
        UR = [sp6.take(4, 256) for _ in range(4)]
        KTS = [sp6.take(512) for _ in range(2)]
        SS = sp6.take(PAST + 1)
        SW = sp6.take(WIN + 1)
        SCC = sp6.take(NCS)
        SCG = sp6.take(NCS)
        IM = sp6.take(14)
        DR = sp6.take(14)
        st6 = sp6.take(16)
        PNR = sp6.take(2, NB)
        PTA = sp6.take(13, P)
        oc6 = None
        PN = sp6.take(2, P)
        kunits = [(0, t, bh) for t in range(NPG) for bh in range(2)] + [(1, t, bh) for t in range(4) for bh in range(2)]
        vunits = [(b, part) for b in range(NB) for part in range(3)]
        NKU, NVU = len(kunits), len(vunits)
        paged = [br == 0 for br, _, _ in kunits] + [part < 2 for _, part in vunits]
        usp = [16 * sum(2 if x else 1 for x in paged[n % 4:n + 1:4]) for n in range(NKU + NVU)]
        upool = [16 * sum(2 for x in paged[n % 4:n + 1:4] if x) for n in range(NKU + NVU)]

        def wait_slot(eng, n):
            if 4 <= n < NKU + 4:
                eng.wait_ge(sem("ku_turned"), 2 * (n - 4) + 2)
            elif n >= NKU + 4:
                eng.wait_ge(sem("vu_used"), n - 4 - NKU + 1)

        def wait_unit(eng, n):
            eng.wait_ge(sem(f"unit_sp{n % 4}"), usp[n])
            if upool[n]:
                eng.wait_ge(sem(f"unit_pool{n % 4}"), upool[n])

        with nc.Block() as block:
            @block.sync
            def _(sp):
                sp.dma_start(KC6.rearrange("p a b n -> p (a b n)"), cmp_rows[0]).then_inc(sem("kc_in"), 16)
                sp.dma_start(VC6.rearrange("p a b n -> p (a b n)"), cmp_rows[1]).then_inc(sem("kc_in"), 16)
                for n in range(NKU + NVU):
                    wait_slot(sp, n)
                    got, u = sem(f"unit_sp{n % 4}"), UR[n % 4]
                    if n < NKU:
                        br, t, bh = kunits[n]
                        if br == 0:
                            for b in range(2):
                                pg = page_reg(sp, 4 * bh + b, t)
                                sp.dma_start(u[:, b, :], A["cache_slc_kv"][l][bass.ds(pg, 1)].rearrange(
                                    "o s k g d -> (o s) k (g d)")[:, 0, :]).then_inc(got, 16)
                        else:
                            sp.dma_start(u, A["cache_win_kv"][l][4 * bh:4 * bh + 4, t * P:(t + 1) * P].rearrange(
                                "b s k g d -> s b k (g d)")[:, :, 0, :]).then_inc(got, 16)
                    else:
                        b, part = vunits[n - NKU]
                        if part < 2:
                            for t in range(2):
                                pg = page_reg(sp, b, 4 * part + t)
                                sp.dma_start(u[:, t, :], A["cache_slc_kv"][l][bass.ds(pg, 1)].rearrange(
                                    "o s k g d -> (o s) k (g d)")[:, 1, :]).then_inc(got, 16)
                        else:
                            sp.dma_start(u, A["cache_win_kv"][l][b].rearrange(
                                "(t s) k g d -> s t k (g d)", s=P)[:, :, 1, :]).then_inc(got, 16)

            @block.gpsimd
            def _(pool):
                pool.memset(QBD, 0.0).then_inc(sem("qbd_zero"), 1)
                rows = A["cache_slc_kv"].rearrange("l p s k g d -> (l p s k) (g d)")
                for n in range(NKU + NVU):
                    if not paged[n]:
                        continue
                    wait_slot(pool, n)
                    for i in range(2, 4):
                        if n < NKU:
                            _, t, bh = kunits[n]
                            col = 16 + (4 * bh + i) * NPG + t
                        else:
                            b, part = vunits[n - NKU]
                            col = 80 + b * NPG + 4 * part + i
                        pool.indirect_dma_start(UR[n % 4][:, i, :], None, rows,
                                                bass.IndirectOffsetOnAxis(gather[:, col:col + 1], 0)
                                                ).then_inc(sem(f"unit_pool{n % 4}"), 16)
                for i in range(4):
                    pool.wait_ge(sem(f"unit_pool{i}"), max(upool[i::4]))

            @block.tensor
            def _(pe):
                pe.wait_ge(sem("qbd"), 1)
                pe.wait_ge(sem("kc_in"), 48)
                for b in range(NB):
                    for gp in range(2):
                        last = pe.matmul(bank[3][:, 64:64 + NCS], QBD[:, b, gp, :], KC6[:, gp, b, :],
                                         start=(b == 0 and gp == 0), stop=(b == NB - 1 and gp == 1))
                for br in range(2):
                    for b in range(NB):
                        for gp in range(2):
                            last = pe.matmul(bank[3][:, br:br + 1], QBD[:, b, gp, :], knewT[:, br, gp, b:b + 1],
                                             start=(b == 0 and gp == 0), stop=(b == NB - 1 and gp == 1))
                last.then_inc(sem("s6_small"), 1)
                for b in range(NB):
                    if b and b % 2 == 0:
                        pe.wait_ge(sem("vcr"), b // 2)
                    for gp in range(2):
                        last = pe.transpose(bank[6][0:NCS, (b % 2) * 256 + gp * P:(b % 2) * 256 + (gp + 1) * P],
                                            VC6[:, gp, b, :], ident)
                    if b % 2:
                        last.then_inc(sem("vc6_turned"), 1)

                def turn(hu):
                    n, h2 = hu // 2, hu % 2
                    if h2 == 0:
                        wait_unit(pe, n)
                    if hu >= 2:
                        pe.wait_ge(sem("kt_act" if h2 == 0 else "kt_dve"), hu // 2)
                    for j in range(4):
                        last = pe.transpose(bank[4 + h2][:, j * P:(j + 1) * P],
                                            UR[n % 4][:, 2 * h2 + j // 2, (j % 2) * P:(j % 2 + 1) * P], ident)
                    last.then_inc(sem("ku_turned"), 1)

                def score(hu):
                    n, h2 = hu // 2, hu % 2
                    br, t, bh = kunits[n]
                    pe.wait_ge(sem("kt_act" if h2 == 0 else "kt_dve"), hu // 2 + 1)
                    out = bank[2 if br else t // 4][:, (t % 4) * P:(t % 4 + 1) * P]
                    for j in range(4):
                        b = 4 * bh + 2 * h2 + j // 2
                        last = pe.matmul(out, QBD[:, b, j % 2, :], KTS[h2][:, j * P:(j + 1) * P],
                                         start=(b == 0 and j == 0), stop=(b == NB - 1 and j == 3))
                    last.then_inc(sem("ku_scored"), 1)

                turn(0)
                for hu in range(2 * NKU):
                    if hu + 1 < 2 * NKU:
                        turn(hu + 1)
                    score(hu)
                pe.wait_ge(sem("pc"), 1)
                pe.transpose(bank[6][0:NCS, 0:P], SCC, ident).then_inc(sem("pc_turned"), 1)
                pe.wait_ge(sem("pct"), 1)
                pe.matmul(bank[7][:, 0:14], PTA[0:NCS, 12, :], c("c2s", NCS), start=True, stop=True
                          ).then_inc(sem("imp_head"), 1)
                pe.wait_ge(sem("imp_copied"), 1)
                pe.matmul(bank[7][:, 16:30], c("grp"), IM, start=True, stop=True).then_inc(sem("imp_group"), 1)
                pe.wait_ge(sem("p6"), 1)
                for t in range(12):
                    src = SS[:, t * P:(t + 1) * P] if t < NPG else SW[:, (t - NPG) * P:(t - NPG + 1) * P]
                    last = pe.transpose(bank[3 + t // 4][:, (t % 4) * P:(t % 4 + 1) * P], src, ident)
                pe.transpose(bank[6][0:NCS, 0:P], SCG, ident)
                for br in range(2):
                    last = pe.transpose(bank[6][0:NB, P * (1 + br):P * (2 + br)], PNR[:, br, :], ident)
                last.then_inc(sem("p6_turned"), 1)
                pe.wait_ge(sem("pta"), 1)
                for b in range(NB):
                    for part in range(3):
                        n = NKU + 3 * b + part
                        wait_unit(pe, n)
                        for gp in range(2):
                            out = bank[gp][:, b * 8:b * 8 + 8]
                            cols = slice(b * NH + gp * 8, b * NH + gp * 8 + 8)
                            gs = slice(gp * P, (gp + 1) * P)
                            if part == 0:
                                pe.matmul(out, VCR[0:NCS, b, gs], PTA[0:NCS, 12, cols], start=True, stop=False)
                                for br in range(2):
                                    pe.matmul(out, vnew[:, br, gs], PN[0:NB, br, cols], start=False, stop=False)
                            for t in range(4):
                                last = pe.matmul(out, UR[n % 4][:, t, gs], PTA[:, part * 4 + t, cols], start=False,
                                                 stop=(part == 2 and t == 3))
                        last.then_inc(sem("vu_used"), 1)

            @block.scalar
            def _(act):
                own = Own(act, sem("act_own"), own_counts["act"])
                for i in range(4):
                    act.wait_ge(sem("vc6_turned"), i + 1)
                    act.activation(VCR[0:NCS, 2 * i:2 * i + 2, :],
                                   bank[6][0:NCS, :].rearrange("p (b n) -> p b n", b=2), ACT.Copy
                                   ).then_inc(sem("vcr"), 1)
                for hu in range(0, 2 * NKU, 2):
                    act.wait_ge(sem("ku_turned"), hu + 1)
                    if hu >= 2:
                        act.wait_ge(sem("ku_scored"), hu - 1)
                    act.activation(KTS[0], bank[4], ACT.Copy).then_inc(sem("kt_act"), 1)
                for i, (s_, k) in enumerate(((SCC, 0), (SS, 2), (SW, 4))):
                    act.wait_ge(sem("s6_max"), i + 1)
                    act.activation(s_, s_, ACT.Exp, bias=st6[:, k:k + 1], accum_out=st6[:, k + 1:k + 2]
                                   ).then_inc(sem("s6_exp"), 1)

            @block.vector
            def _(dve):
                own = Own(dve, sem("dve_own"), own_counts["dve"])
                dve.wait_ge(sem("qbd_zero"), 1)
                for b in range(NB):
                    for gp in range(2):
                        for a in range(2):
                            c0 = b * NH + gp * 8 + a * 4
                            last = own.tick(dve.tensor_copy(QBD[a * DH:(a + 1) * DH, b, gp, c0:c0 + 4],
                                                            nqs[a * DH:(a + 1) * DH, gp * 4:gp * 4 + 4, b]))
                own.wait()
                dve.nop().then_inc(sem("qbd"), 1)
                nslr, drow = c("nslr"), c("drow")
                for hu in range(1, 2 * NKU, 2):
                    dve.wait_ge(sem("ku_turned"), hu + 1)
                    if hu >= 2:
                        dve.wait_ge(sem("ku_scored"), hu - 1)
                    dve.tensor_copy(KTS[1], bank[5]).then_inc(sem("kt_dve"), 1)
                dve.wait_ge(sem("s6_small"), 1)
                own(dve.scalar_tensor_tensor(SCC, c("dcs"), nslr, bank[3][:, 64:64 + NCS], ALU.mult, ALU.add))
                own(dve.tensor_copy(SS[:, PAST:PAST + 1], bank[3][:, 0:1]))
                own(dve.tensor_copy(SW[:, WIN:WIN + 1], bank[3][:, 1:2]))
                dve.tensor_reduce(st6[:, 0:1], SCC, AX.X, ALU.max, negate=True).then_inc(sem("s6_max"), 1)
                dve.wait_ge(sem("s6_exp"), 1)
                own(dve.reciprocal(st6[:, 1:2], st6[:, 1:2]))
                dve.tensor_scalar(SCC, SCC, st6[:, 1:2], None, ALU.mult).then_inc(sem("pc"), 1)
                dve.wait_ge(sem("pc"), 1)
                own(dve.tensor_scalar(SCG, SCC, gate_s[:, 0:1], None, ALU.mult))
                dve.wait_ge(sem("pc_turned"), 1)
                dve.tensor_copy(PTA[0:NCS, 12, :], bank[6][0:NCS, 0:P]).then_inc(sem("pct"), 1)
                dve.wait_ge(sem("imp_head"), 1)
                dve.tensor_copy(IM, bank[7][:, 0:14]).then_inc(sem("imp_copied"), 1)
                dve.wait_ge(sem("imp_group"), 1)
                own(dve.tensor_copy(IM, bank[7][:, 16:30]))
                own(dve.tensor_reduce(st6[:, 6:7], IM, AX.X, ALU.min))
                own(dve.tensor_scalar(DR, IM, st6[:, 6:7], None, ALU.is_equal))
                own(dve.tensor_tensor(DR, DR, c("jj"), ALU.mult))
                own(dve.tensor_reduce(st6[:, 7:8], DR, AX.X, ALU.max))
                own(dve.tensor_scalar(DR, c("jj"), st6[:, 7:8], -1e30, ALU.is_equal, ALU.mult))
                dve.wait_ge(sem("ku_scored"), 2 * NKU)
                for i in range(2):
                    own(dve.scalar_tensor_tensor(SS[:, 512 * i:512 * i + 512], drow[:, 512 * i:512 * i + 512], nslr,
                                                 bank[i], ALU.mult, ALU.add))
                own(dve.scalar_tensor_tensor(SW[:, 0:WIN], drow[:, PAST - WIN:PAST], nslr, bank[2], ALU.mult, ALU.add))
                mid = SS[:, SEL:15 * SEL].rearrange("p (j s) -> p j s", s=SEL)
                own(dve.tensor_tensor(mid, mid, bc(DR, SEL), ALU.add))
                dve.tensor_reduce(st6[:, 2:3], SS, AX.X, ALU.max, negate=True).then_inc(sem("s6_max"), 1)
                dve.tensor_reduce(st6[:, 4:5], SW, AX.X, ALU.max, negate=True).then_inc(sem("s6_max"), 1)
                for i, (s_, k) in enumerate(((SS, 2), (SW, 4))):
                    dve.wait_ge(sem("s6_exp"), i + 2)
                    own(dve.reciprocal(st6[:, k + 1:k + 2], st6[:, k + 1:k + 2]))
                    own(dve.tensor_scalar(s_, s_, st6[:, k + 1:k + 2], gate_s[:, i + 1:i + 2], ALU.mult, ALU.mult))
                own(dve.tensor_scalar(PNR[:, 0, :], c("bsel"), SS[:, PAST:PAST + 1], None, ALU.mult))
                dve.tensor_scalar(PNR[:, 1, :], c("bsel"), SW[:, WIN:WIN + 1], None, ALU.mult).then_inc(sem("p6"), 1)
                dve.wait_ge(sem("p6_turned"), 1)
                for i in range(3):
                    own(dve.tensor_copy(PTA[:, 4 * i:4 * i + 4, :], bank[3 + i].rearrange("p (t n) -> p t n", t=4)))
                own(dve.tensor_copy(PTA[0:NCS, 12, :], bank[6][0:NCS, 0:P]))
                dve.tensor_copy(PN[0:NB, :, :], bank[6][0:NB, P:3 * P].rearrange("p (r n) -> p r n", r=2)
                                ).then_inc(sem("pta"), 1)
                dve.wait_ge(sem("vu_used"), NVU)
                for gp in range(2):
                    for a in range(2):
                        o = bank[gp][a * DH:(a + 1) * DH, 0:NB * 8].rearrange("p (b h) -> p h b", h=8)
                        own(dve.tensor_copy(ocT[a * DH:(a + 1) * DH, gp * 4:gp * 4 + 4, T:TA], o[:, a * 4:a * 4 + 4, :]))

        sp7 = Space(arena[:, :])
        MG = sp7.take(KT, TA)
        SG = [sp7.take(TA) for _ in range(3)]
        TMP = sp7.take(TA)
        mkeys = [(hf, br, m) for hf in range(2) for br in range(3) for m in range(4)]

        def dve_reads(key):
            return sum(1 for _, e in TILES[:TI[key] + 1] if e == "dve")

        def act_reads(key):
            return sum(1 for _, e in TILES[:TI[key] + 1] if e == "act")

        with nc.Block() as block:
            @block.sync
            def _(sp):
                loads_of_phase(sp, 4, l)

            @block.tensor
            def _(pe):
                acts = (oaT, obT, ocT)
                for hf in range(2):
                    for br in range(3):
                        wg, wo = open_slab(pe, f"mg{hf}{br}"), open_slab(pe, f"mo{hf}{br}")
                        for m in range(4):
                            proj_T(pe, ("mg", hf, br, m), lambda k: wg[:, k, m * P:(m + 1) * P], hT)
                            proj_T(pe, ("mo", hf, br, m), lambda k: wo[:, k, m * P:(m + 1) * P], acts[br])
                pe.wait_ge(sem("merged"), 16)
                for hf in range(2):
                    w = open_slab(pe, f"wo{hf}")
                    for m in range(4):
                        proj_T(pe, ("wo", 4 * hf + m), lambda k: w[:, k, m * P:(m + 1) * P], MG)

            @block.scalar
            def _(act):
                for i, (hf, br, m) in enumerate(mkeys):
                    wait_proj(act, ("mg", hf, br, m))
                    if i >= 3:
                        act.wait_ge(sem("proj_read_dve"), dve_reads(("mo",) + mkeys[i - 3]))
                    act.activation(two(SG[i % 3]), both(proj_pair(("mg", hf, br, m))), ACT.Sigmoid
                                   ).then_inc(sem("proj_read_act"), 1)

            @block.vector
            def _(dve):
                for i, (hf, br, m) in enumerate(mkeys):
                    key, j = ("mo", hf, br, m), 4 * hf + m
                    wait_proj(dve, key)
                    dve.wait_ge(sem("proj_read_act"), act_reads(("mg", hf, br, m)))
                    dst = MG[:, j, :] if br == 0 else TMP
                    if i >= 5 and br:
                        dve.wait_ge(sem("merged"), 8 * hf + 4 * (br - 1) + m)
                    dve.tensor_tensor(two(dst), both(proj_pair(key)), two(SG[i % 3]), ALU.mult
                                      ).then_inc(sem("proj_read_dve"), 1)
                    if br:
                        dve.wait_ge(sem("proj_read_dve"), dve_reads(key))
                        dve.tensor_tensor(MG[:, j, :], MG[:, j, :], TMP, ALU.add).then_inc(sem("merged"), 1)
                for j in range(KT):
                    wait_proj(dve, ("wo", j))
                    dve.tensor_tensor(two(xT[:, j, :]), both(proj_pair(("wo", j))), two(xT[:, j, :]), ALU.add
                                      ).then_inc(sem("proj_read_dve"), 1)

        sp8 = Space(arena[:, :])
        FA = sp8.take(FT, TA)
        SGF = [sp8.take(TA) for _ in range(2)]
        tag_sq["ffn"] = [sp8.take(TA) for _ in range(2)]
        ms8 = sp8.take(TA)
        with nc.Block() as block:
            @block.sync
            def _(sp):
                loads_of_phase(sp, 5, l)

            @block.tensor
            def _(pe):
                norm_pe(pe, "ffn")
                pe.wait_ge(sem("ffn_h"), KT)
                for i in range(FT):
                    if i % 4 == 0:
                        wg, wu = open_slab(pe, f"fg{i // 4}"), open_slab(pe, f"fu{i // 4}")
                    cs = slice((i % 4) * P, (i % 4 + 1) * P)
                    proj_T(pe, ("fg", i), lambda k: wg[:, k, cs], hT)
                    proj_T(pe, ("fu", i), lambda k: wu[:, k, cs], hT)
                pe.wait_ge(sem("proj_read_dve"), dve_reads(("fu", FT - 1)))
                for hf in range(2):
                    for r in range(0, FT, 8):
                        w = open_slab(pe, f"fd{hf}{r}")
                        rt = min(8, FT - r)
                        for m in range(4):
                            j = 4 * hf + m
                            if r == 0:
                                wait_proj_bank(pe, ("fd", j))
                            for half in range(2):
                                for k in range(rt):
                                    last = pe.matmul(pair[m][:, half, 0:HA], w[:, k, m * P:(m + 1) * P],
                                                     FA[:, r + k, half * HA:(half + 1) * HA],
                                                     start=(r + k == 0), stop=(r + k == FT - 1))
                            if r == 16:
                                last.then_inc(sem("proj_done"), 1)
                        if r < 16:
                            last.then_inc(sem("ffn_down_slab"), 1)

            @block.scalar
            def _(act):
                norm_act(act, "ffn", ms8)
                for i in range(FT):
                    wait_proj(act, ("fg", i))
                    if i >= 2:
                        act.wait_ge(sem("proj_read_dve"), dve_reads(("fu", i - 2)))
                    act.activation(two(SGF[i % 2]), both(proj_pair(("fg", i))), ACT.Silu
                                   ).then_inc(sem("proj_read_act"), 1)

            @block.vector
            def _(dve):
                own = Own(dve, sem("dve_own"), own_counts["dve"])
                norm_dve(dve, own, "ffn", ms8, "ffn")
                for i in range(FT):
                    wait_proj(dve, ("fu", i))
                    dve.wait_ge(sem("proj_read_act"), act_reads(("fg", i)))
                    dve.tensor_tensor(two(FA[:, i, :]), both(proj_pair(("fu", i))), two(SGF[i % 2]), ALU.mult
                                      ).then_inc(sem("proj_read_dve"), 1)
                for j in range(KT):
                    wait_proj(dve, ("fd", j))
                    dve.tensor_tensor(two(xT[:, j, :]), both(proj_pair(("fd", j))), two(xT[:, j, :]), ALU.add
                                      ).then_inc(sem("proj_read_dve"), 1)

        with nc.Block() as block:
            @block.sync
            def _(sp):
                sp.wait_ge(sem("win_moved"), 16)
        nums = sorted(s.num for s in sems.values())
        assert nums == list(range(nums[0], nums[-1] + 1)), nums
        nc.gpsimd.dma_reset()
        nc.gpsimd.sem_clear(range(nums[0], nums[-1] + 1))
        nc.all_engine_barrier()

    yr = arena[:, 0:5 * DM].rearrange("p (t n) -> p t n", t=5)
    y_turned, y_copied, y_out = sem("io_turned"), sem("io_copied"), sem("io_moved")
    with nc.Block() as block:
        @block.tensor
        def _(pe):
            for tt in range(NT + 1):
                if tt >= 4:
                    pe.wait_ge(y_copied, tt - 3)
                n = P if tt < NT else NB
                for k in range(KT):
                    last = pe.transpose(bank[2 * (tt % 4) + k // 4][0:n, (k % 4) * P:(k % 4 + 1) * P],
                                        xT[:, k, tt * P:tt * P + n], ident)
                last.then_inc(y_turned, 1)

        @block.vector
        def _(dve):
            for tt in range(NT + 1):
                n = P if tt < NT else NB
                dve.wait_ge(y_turned, tt + 1)
                dve.tensor_copy(yr[0:n, tt, :].rearrange("p (a b) -> p a b", a=2), pair[tt % 4][0:n, :, :]
                                ).then_inc(y_copied, 1)

        @block.sync
        def _(sp):
            for tt in range(NT + 1):
                sp.wait_ge(y_copied, tt + 1)
                dst = O["y_prompt"][0, tt * P:(tt + 1) * P, :] if tt < NT else O["y_sample"][:, 0, :]
                sp.dma_start(dst, yr[0:(P if tt < NT else NB), tt, :]).then_inc(y_out, 16)
            sp.wait_ge(y_out, 16 * (NT + 1))


_INS = ['x_prompt', 'x_sample', 'cache_cmp_kv', 'cache_slc_kv', 'cache_win_kv', 'state_gla', 'state_rglru',
        'state_conv', 'page_table', 'norm_mix_g', 'w_in', 'rg_conv_w', 'rg_conv_b', 'rg_w_a', 'rg_b_a', 'rg_w_x',
        'rg_b_x', 'rg_lambda', 'gla_w_a', 'gla_b_a', 'gla_norm_g', 'nsa_q_norm_g', 'nsa_k_norm_g', 'nsa_phi_k',
        'nsa_phi_v', 'nsa_cmp_pe', 'w_rg_out', 'w_gla_out', 'w_nsa_out', 'w_out', 'norm_ffn_g', 'w_ffn_gate',
        'w_ffn_up', 'w_ffn_down']
_OUTS = [('y_prompt', (1, T, DM)), ('y_sample', (NB, 1, DM)),
         ('p_cmp_kv', (L, 1, T, 2, G, DH)), ('p_slc_kv', (L, 1, T, 2, G, DH)), ('p_win_kv', (L, 1, WIN, 2, G, DH)),
         ('p_gla', (L, 1, GH, DK, DV)), ('p_rglru', (L, 1, DM)), ('p_conv', (L, 1, 3, DM)),
         ('s_cmp_kv', (L, NB, 1, 2, G, DH)), ('s_slc_kv', (L, NB, 1, 2, G, DH)), ('s_win_kv', (L, NB, WIN, 2, G, DH)),
         ('s_gla', (L, NB, GH, DK, DV)), ('s_rglru', (L, NB, DM)), ('s_conv', (L, NB, 3, DM))]


def kernel(**inputs):
    import numpy as _np
    import concourse.bacc as _bacc
    from concourse import mybir as _mybir
    from concourse.bass_utils import run_bass_kernel_spmd as _run

    nc = _bacc.Bacc("TRN2", target_bir_lowering=False, num_devices=1)
    con, lmask = constants()
    arrays, args, consts, outs = {}, {}, {}, {}
    for name, a in [(n, inputs[n]) for n in _INS] + [("con", con), ("lmask", lmask)]:
        a = _np.ascontiguousarray(a)
        arrays[f"in_{name}_dram"] = a
        where = consts if name in ("con", "lmask") else args
        where[name] = nc.dram_tensor(f"in_{name}_dram", a.shape, _mybir.dt.from_np(a.dtype), kind="ExternalInput").ap()
    for name, shape in _OUTS:
        outs[name] = nc.dram_tensor(f"out_{name}_dram", shape, _mybir.dt.from_np(_np.dtype("float32")),
                                    kind="ExternalOutput").ap()
    build(nc, args, outs, consts)
    r = _run(nc, [arrays], core_ids=[0])
    return tuple(r.results[0][f"out_{name}_dram"] for name, _ in _OUTS)
```

```python
import numpy as np

import concourse.bass as bass
from concourse import mybir

F32 = mybir.dt.float32
U8 = mybir.dt.uint8
I32 = mybir.dt.int32
U32 = mybir.dt.uint32
ALU = mybir.AluOpType
ACT = mybir.ActivationFunctionType
AX = mybir.AxisListType

P = 128
DM, T, NB, L = 1024, 512, 8, 2
TA = T + NB
KT = DM // P
NT = T // P
GH, DK, DV, RANK = 4, 128, 256, 16
NH, G, HPG, DH = 16, 4, 4, 64
KVW = 2 * G * DH
PAST, PAGE, WIN = 1024, 128, 512
NPG = PAST // PAGE
STR, SEL = 16, 64
NCP, NCS = T // STR, PAST // STR
NSEL = PAST // SEL + 1
FF = 2816
FT = FF // P
EPS, TINY = 1e-6, 1e-30
BIG = 2.56e32
SLOPE = [2.0 ** (-8.0 * h / NH) for h in range(1, NH + 1)]

IN = {}
_at = 0
for _n, _w in (("rgy", DM), ("rgx", DM), ("gq", 512), ("gk", 512), ("gv", 1024), ("gr", 1024), ("ga", RANK),
               ("nq", DM), ("cmp", KVW), ("slc", KVW), ("win", KVW), ("gate", 3 * NH), ("merge", 3 * DM)):
    IN[_n] = _at
    _at += _w

PR = {"mix": 0, "ffn": 8, "cw": 16, "cb": 48, "ba": 56, "bx": 64, "lam": 72, "gba": 80, "gno": 84, "qn": 86, "kn": 87}
NPR = 88

CC, _at = {}, 0
for _n, _w in (("ident", 128), ("ones", 128), ("blk", 128), ("grp", 128), ("bsel", 8), ("nsl", 16), ("nslr", 1),
               ("dist", 896), ("drow", PAST), ("dcmp", NT * NCP), ("mcmp", NT * NCP), ("dcs", NCS), ("c2s", 14),
               ("jj", 14), ("crow", 4), ("srow", 1)):
    CC[_n] = (_at, _w)
    _at += _w
NCC = _at
LEVELS = (64, 32, 16, 8, 4, 2, 1)


def constants():
    c = np.zeros((P, NCC), np.float32)
    p = np.arange(P)

    def put(name, a):
        c[:, CC[name][0]:CC[name][0] + CC[name][1]] = a

    put("ident", np.eye(P))
    put("ones", np.ones((P, P)))
    put("blk", (p[:, None] // DH) == (p[None, :] // DH))
    put("grp", (p[:, None] // HPG) == (p[None, :] // HPG))
    put("bsel", (p[:, None] // NH) == np.arange(NB)[None, :])
    put("nsl", -np.array(SLOPE)[None, :])
    put("nslr", -np.array(SLOPE)[p % NH][:, None])
    d = p[:, None] + 384 - np.arange(896)[None, :]
    put("dist", np.where(d >= 0, d, BIG))
    put("drow", PAST - np.arange(PAST)[None, :])
    q = (np.arange(NT)[None, :, None] * P + p[:, None, None])
    n = np.arange(NCP)[None, None, :]
    ok = (n * STR + 31 <= q) & (n < NCP - 1)
    put("dcmp", np.where(ok, q - (n * STR + 31), BIG).reshape(P, -1))
    put("mcmp", ok.reshape(P, -1))
    m = np.arange(NCS)
    put("dcs", np.where(m < NCS - 1, PAST - (m * STR + 31), BIG)[None, :])
    st = p[:, None] * STR
    sel = np.arange(1, 15)[None, :] * SEL
    put("c2s", (st < sel + SEL) & (st + 32 > sel) & (p[:, None] < NCS - 1))
    put("jj", np.arange(1, 15)[None, :])
    put("crow", (p % 8)[:, None] * 4 + np.arange(4)[None, :])
    put("srow", 2 * p[:, None])
    s, t = p[:, None], p[None, :]
    mask = np.zeros((P, len(LEVELS) + 1, P), np.int32)
    for i, h in enumerate(LEVELS):
        mask[:, i] = (s // (2 * h) == t // (2 * h)) & (s % (2 * h) < h) & (t % (2 * h) >= h)
    mask[:, len(LEVELS)] = s == t
    return c, mask.reshape(P, -1)


class Own:

    def __init__(self, eng, sem, count):
        self.eng, self.sem, self.count = eng, sem, count

    def tick(self, ins):
        ins.then_inc(self.sem, 1)
        self.count[0] += 1
        return self.count[0]

    def wait(self, n=None):
        self.eng.wait_ge(self.sem, self.count[0] if n is None else n)

    def __call__(self, ins):
        self.tick(ins)
        self.wait()


def slabs_of_layer():
    s = {}

    def add(name, tensor, r0, rt, c0, w):
        s[name] = (tensor, r0, rt, c0, w)

    for n in ("rgx", "rgy"):
        for i in range(2):
            add(f"{n}{i}", "w_in", 0, KT, IN[n] + 512 * i, 512)
    marks = [len(s)]
    add("ga", "w_in", 0, KT, IN["ga"], RANK)
    add("gk", "w_in", 0, KT, IN["gk"], 512)
    add("gq", "w_in", 0, KT, IN["gq"], 512)
    for n in ("gv", "gr"):
        for i in range(2):
            add(f"{n}{i}", "w_in", 0, KT, IN[n] + 512 * i, 512)
    marks.append(len(s))
    add("gate", "w_in", 0, KT, IN["gate"], 3 * NH)
    add("cmp", "w_in", 0, KT, IN["cmp"], 512)
    marks.append(len(s))
    for n in ("slc", "win"):
        add(n, "w_in", 0, KT, IN[n], 512)
    for i in range(2):
        add(f"nq{i}", "w_in", 0, KT, IN["nq"] + 512 * i, 512)
    marks.append(len(s))
    for hf in range(2):
        for br, t in enumerate(("w_rg_out", "w_gla_out", "w_nsa_out")):
            add(f"mg{hf}{br}", "w_in", 0, KT, IN["merge"] + br * DM + 512 * hf, 512)
            add(f"mo{hf}{br}", t, 0, KT, 512 * hf, 512)
    for hf in range(2):
        add(f"wo{hf}", "w_out", 0, KT, 512 * hf, 512)
    marks.append(len(s))
    for c in range((FT + 3) // 4):
        w = min(512, FF - 512 * c)
        add(f"fg{c}", "w_ffn_gate", 0, KT, 512 * c, w)
        add(f"fu{c}", "w_ffn_up", 0, KT, 512 * c, w)
    for hf in range(2):
        for r in range(0, FT, 8):
            add(f"fd{hf}{r}", "w_ffn_down", r, min(8, FT - r), 512 * hf, 512)
    marks.append(len(s))
    return s, marks


def tiles_of_layer():
    t = []
    t += [(("rgx", i), "act") for i in range(KT)] + [(("rgy", i), "act") for i in range(KT)]
    t += [(("ga", 0), "act")] + [(("gk", i), "act") for i in range(4)] + [(("gq", i), "act") for i in range(4)]
    t += [(("gv", i, tt), "act") for i in range(2) for tt in range(NT + 1)]
    t += [(("gr", i), "act") for i in range(KT)]
    t += [(("gate", tt), "act") for tt in range(NT + 1)]
    t += [(("cmp", tt), "act") for tt in range(NT + 1)]
    t += [((n, tt), "dve") for n in ("slc", "win") for tt in range(NT + 1)]
    t += [(("nq", i), "dve") for i in range(KT)]
    for hf in range(2):
        for br in range(3):
            for m in range(4):
                t += [(("mg", hf, br, m), "act"), (("mo", hf, br, m), "dve")]
    t += [(("wo", i), "dve") for i in range(KT)]
    for i in range(FT):
        t += [(("fg", i), "act"), (("fu", i), "dve")]
    t += [(("fd", i), "dve") for i in range(KT)]
    return t


NSLOT = 3


def build(nc, A, O, C):
    sems = {}

    def sem(name):
        if name not in sems:
            sems[name] = nc.alloc_semaphore(name)
        return sems[name]

    def sb(name, shape, dt=F32):
        return nc.alloc_sbuf_tensor(name, shape, dt)

    con = sb("con", [P, NCC])
    lmask = sb("lmask", [P, 8 * P], U8)
    xT, hT, oaT, obT, ocT = (sb(n, [P, KT, TA]) for n in ("xT", "hT", "oaT", "obT", "ocT"))
    ring = sb("ring", [P, NSLOT, KT * 512])
    par = sb("par", [P, P])
    kgain = sb("kgain", [P, 2, DH])
    gate_s = sb("gate_s", [P, 3])
    nqs = sb("nqs", [P, KT, NB])
    knewT = sb("knewT", [P, 2, 2, NB])
    vnew = sb("vnew", [NB, 2, 256])
    pages = sb("pages", [1, NB * NPG], I32)
    pg_rows = sb("pg_rows", [P, NB // 2 + NB * NPG])
    gather = sb("gather", [P, 16 + 2 * NB * NPG], U32)
    ARENA = 15744
    arena = sb("arena", [P, ARENA])
    pair = [nc.alloc_psum_tensor(f"pair{i}", [P, 2, 512], F32) for i in range(4)]
    bank = [pair[i // 2][:, i % 2, :] for i in range(8)]
    gate_rows = nc.dram_tensor("gate_rows", [NB, 3 * NH], F32, kind="Internal").ap()
    cmp_rows = nc.dram_tensor("cmp_rows", [2, P, 2 * NB * NCS], F32, kind="Internal").ap()
    HA = TA // 2

    def both(i):
        return pair[i][:, :, 0:HA]

    def two(ap):
        return ap.rearrange("p (a b) -> p a b", a=2)

    def c(name, rows=P):
        a, w = CC[name]
        return con[0:rows, a:a + w]

    ident, ones, blk = c("ident"), c("ones"), c("blk")

    class Space:

        def __init__(self, flat):
            self.flat, self.at, self.end = flat, 0, flat.shape[1]

        def take(self, *dims):
            n = int(np.prod(dims))
            assert self.at + n <= self.end, (self.at, n, self.end)
            v = self.flat[:, self.at:self.at + n]
            self.at += n
            if len(dims) == 2:
                v = v.rearrange("p (a b) -> p a b", a=dims[0])
            if len(dims) == 3:
                v = v.rearrange("p (a b c) -> p a b c", a=dims[0], b=dims[1])
            if len(dims) == 4:
                v = v.rearrange("p (a b c d) -> p a b c d", a=dims[0], b=dims[1], c=dims[2])
            return v

    def flat(t):
        return t[:, :, :].rearrange("p a b -> p (a b)")

    SLABS, MARKS = slabs_of_layer()
    names = list(SLABS)
    TILES = tiles_of_layer()
    TI = {k: i for i, (k, _) in enumerate(TILES)}
    own_counts = {"act": [0], "dve": [0], "pool": [0]}

    def pieces(name):
        return 4 if name.startswith("mo") and name.endswith("2") else 2 * KT if name.startswith("nq") else 1

    def slab_view(name):
        _, _, rt, _, w = SLABS[name]
        i = names.index(name)
        return ring[:, i % NSLOT, 0:rt * w].rearrange("p (k n) -> p k n", k=rt)

    def slab_ready(name):
        i = names.index(name)
        return sem(f"slab_in{i % NSLOT}"), 16 * sum(pieces(n) for n in names[i % NSLOT:i + 1:NSLOT])

    def slab_used(name):
        n, d = name.rstrip("0123456789"), name[len(name.rstrip("0123456789")):]
        if n == "fd" and int(d[1:]) != 16:
            return sem("ffn_down_slab"), int(d[0]) * 2 + int(d[1:]) // 8 + 1
        if n in ("mg", "mo"):
            key = (n, int(d[0]), int(d[1]), 3)
        elif n == "gv":
            key = (n, int(d), NT)
        elif n in ("gate", "slc", "win", "cmp"):
            key = (n, NT)
        elif n == "ga":
            key = (n, 0)
        elif n == "fd":
            key = (n, 4 * int(d[0]) + 3)
        else:
            key = (n, min(4 * int(d or 0) + 3, FT - 1))
        return sem("proj_done"), TI[key] + 1

    def load_slab(eng, name, l):
        t, r0, rt, c0, w = SLABS[name]
        i = names.index(name)
        if i >= NSLOT:
            eng.wait_ge(*slab_used(names[i - NSLOT]))
        got = sem(f"slab_in{i % NSLOT}")
        src = A[t][l][r0 * P:(r0 + rt) * P, c0:c0 + w]
        if pieces(name) == 1:
            eng.dma_start(slab_view(name), src.rearrange("(k p) n -> p k n", p=P)).then_inc(got, 16)
            return
        if name.startswith("nq"):
            for k in range(KT):
                v = src[k * P:(k + 1) * P].rearrange("p (a h c) -> p a h c", a=2, h=HPG)
                d = slab_view(name)[:, k, :].rearrange("p (h a c) -> p a h c", a=2, h=HPG)
                for a in range(2):
                    eng.dma_start(d[:, a], v[:, a]).then_inc(got, 16)
            return
        v = src.rearrange("(gp a h d) n -> gp a d h n", gp=2, a=2, h=HPG)
        for gp in range(2):
            for a in range(2):
                eng.dma_start(slab_view(name)[a * DH:(a + 1) * DH, gp * 4:gp * 4 + 4, :],
                              v[gp, a]).then_inc(got, 16)

    def loads_of_phase(eng, ph, l):
        ahead = [0] + [min(m + NSLOT - (j == 3), len(names)) for j, m in enumerate(MARKS)]
        for n in names[ahead[ph]:ahead[ph + 1]]:
            load_slab(eng, n, l)

    def proj_pair(key):
        return key[1] % 4 if key[0] == "fd" else TI[key] % 2

    def wait_proj_bank(pe, key):
        i = TI[key] - 2
        if key[0] == "fd":
            i = TI[("fd", 0)] - 1 if key[1] < 4 else TI[key] - 4
        if i < 0:
            return
        for e in ("act", "dve"):
            if key[0] == "fd" or TILES[i][1] == e:
                pe.wait_ge(sem(f"proj_read_{e}"), sum(1 for _, x in TILES[:i + 1] if x == e))

    def wait_proj(eng, key):
        eng.wait_ge(sem("proj_done"), TI[key] + 1)

    def proj_T(pe, key, lhs, rhs, nk=KT, m=P, made=None):
        wait_proj_bank(pe, key)
        o = proj_pair(key)
        for half in range(2):
            for k in range(nk):
                if made and half == 0:
                    pe.wait_ge(sem(made), k + 1)
                last = pe.matmul(pair[o][0:m, half, 0:HA], lhs(k), rhs[:, k, half * HA:(half + 1) * HA],
                                 start=(k == 0), stop=(k == nk - 1))
        last.then_inc(sem("proj_done"), 1)

    def proj_rows(pe, key, tt, slab, w):
        wait_proj_bank(pe, key)
        big = pair[proj_pair(key)][:, 0, :]
        rows = P if tt < NT else NB
        for k in range(KT):
            last = pe.matmul(big[0:rows, 0:w], hT[:, k, tt * P:tt * P + rows], slab[:, k, 0:w],
                             start=(k == 0), stop=(k == KT - 1))
        last.then_inc(sem("proj_done"), 1)

    def open_slab(pe, name):
        s, v = slab_ready(name)
        pe.wait_ge(s, v)
        return slab_view(name)

    def bc(ap, n):
        return ap.unsqueeze(len(ap.shape)).to_broadcast(list(ap.shape) + [n])

    def rep(ap, n):
        return ap.unsqueeze(1).to_broadcast([ap.shape[0], n, ap.shape[1]])

    xr = arena[:, 0:5 * DM].rearrange("p (t n) -> p t n", t=5)
    lmask_in = arena[:, 5 * DM:6 * DM].bitcast(I32)
    pg_in = arena[:, 6 * DM:6 * DM + NB // 2 + NB * NPG].bitcast(I32)
    page_rows = NB // 2
    with nc.Block() as block:
        @block.sync
        def _(sp):
            sp.dma_start(con[:, :], C["con"]).then_inc(sem("io_moved"), 16)
            sp.dma_start(lmask_in, C["lmask"]).then_inc(sem("io_moved"), 16)
            sp.dma_start(pages[:, :], A["page_table"].rearrange("(a b) t -> a (b t)", a=1)).then_inc(sem("io_moved"), 16)
            for ct in range(NB // 2):
                for b2 in range(2):
                    src = A["page_table"][2 * ct + b2].unsqueeze(1).to_broadcast([NPG, 8]).unsqueeze(2)
                    sp.dma_start(pg_in[b2 * 64:b2 * 64 + 64, ct:ct + 1], src,
                                 allow_slow_non_contiguous=True).then_inc(sem("pages_in"), 16)
            sp.dma_start(pg_in[:, NB // 2:], A["page_table"].rearrange("(a b) t -> a (b t)", a=1)
                         .to_broadcast([P, NB * NPG])).then_inc(sem("pages_in"), 16)
            sp.dma_start(xr[:, 0:NT, :], A["x_prompt"][0].rearrange("(t p) n -> p t n", p=P)).then_inc(sem("io_moved"), 16)
            sp.dma_start(xr[0:NB, NT, :], A["x_sample"][:, 0, :]).then_inc(sem("io_moved"), 16)

        @block.tensor
        def _(pe):
            pe.wait_ge(sem("io_moved"), 80)
            for k in range(KT):
                if k >= 4:
                    pe.wait_ge(sem("io_copied"), k - 3)
                for tt in range(NT):
                    pe.transpose(bank[k % 4][:, tt * P:(tt + 1) * P], xr[:, tt, k * P:(k + 1) * P], ident)
                pe.transpose(bank[4 + k % 4][:, 0:NB], xr[0:NB, NT, k * P:(k + 1) * P],
                             ident[0:NB, 0:NB]).then_inc(sem("io_turned"), 1)

        @block.vector
        def _(dve):
            for k in range(KT):
                dve.wait_ge(sem("io_turned"), k + 1)
                dve.tensor_copy(xT[:, k, 0:T], bank[k % 4][:, :])
                dve.tensor_copy(xT[:, k, T:TA], bank[4 + k % 4][:, 0:NB]).then_inc(sem("io_copied"), 1)
            dve.tensor_copy(lmask[:, :], lmask_in)
            dve.wait_ge(sem("pages_in"), 16 * (NB + 1))
            dve.tensor_copy(pg_rows[:, :], pg_in)

    def norm_pe(pe, tag, n=KT):
        for k in range(n):
            sum_tile(pe, tag, k, n)

    def sum_tile(pe, tag, k, n=KT):
        pe.wait_ge(sem(f"{tag}_sq"), k + 1)
        for half in range(2):
            last = pe.matmul(pair[2][:, half, 0:HA], ones, tag_sq[tag][k % 2][:, half * HA:(half + 1) * HA],
                             start=(k == 0), stop=(k == n - 1))
        last.then_inc(sem(f"{tag}_sum"), 1)

    def square_tile(act, tag, k):
        if k >= 2:
            act.wait_ge(sem(f"{tag}_sum"), k - 1)
        act.activation(tag_sq[tag][k % 2], xT[:, k, :], ACT.Square).then_inc(sem(f"{tag}_sq"), 1)

    def norm_root(act, tag, ms):
        act.wait_ge(sem(f"{tag}_ms"), 1)
        act.activation(ms, ms, ACT.Sqrt).then_inc(sem(f"{tag}_rt"), 1)

    def norm_mean(dve, tag, ms):
        dve.wait_ge(sem(f"{tag}_sum"), KT)
        dve.tensor_scalar(two(ms), both(2), 1.0 / DM, EPS, ALU.mult, ALU.add).then_inc(sem(f"{tag}_ms"), 1)

    def norm_dve(dve, own, tag, ms, gain):
        dve.wait_ge(sem(f"{tag}_rt"), 1)
        own(dve.reciprocal(ms, ms))
        for k in range(KT):
            dve.scalar_tensor_tensor(hT[:, k, :], xT[:, k, :], par[:, PR[gain] + k:PR[gain] + k + 1], ms,
                                     ALU.mult, ALU.mult).then_inc(sem(f"{tag}_h"), 1)

    tag_sq = {}
    OCF, OBF = flat(ocT), flat(obT)

    with nc.Fori(0, L) as l:
        for cnt in own_counts.values():
            cnt[0] = 0

        sp0 = Space(arena[:, :])
        prow = sp0.take(P)
        strow = sp0.take(DM)
        Mb = sp0.take(KT, TA)
        XP = [sp0.take(3 + TA) for _ in range(2)]
        XS = [sp0.take(NB, 4) for _ in range(2)]
        XC = [sp0.take(TA) for _ in range(2)]
        TR = [sp0.take(TA) for _ in range(2)]
        TX = [sp0.take(TA) for _ in range(2)]
        DN = [sp0.take(TA) for _ in range(2)]
        h0T = sp0.take(KT, 32)
        tag_sq["mix"] = [sp0.take(TA) for _ in range(2)]
        ms0 = sp0.take(TA)
        pk = sp0.take(8, KT)
        gw = sp0.take(2, 8, P)
        AC, VB = ocT, obT
        states = sp0.take(KT, 36)

        def conv_w(j, n):
            k = PR["cw"] + 8 * j + n
            return par[:, k:k + 1]

        def pcol(name, n):
            return par[:, PR[name] + n:PR[name] + n + 1]

        PAR_IN = 16 * 17

        with nc.Block() as block:
            @block.sync
            def _(sp):
                def rows(r, src):
                    sp.dma_start(prow[r:r + src.shape[0], 0:src.shape[1]], src).then_inc(sem("par_in"), 16)

                def as_rows(v):
                    return v.rearrange("(a n) -> a n", n=P)

                rows(PR["mix"], as_rows(A["norm_mix_g"][l]))
                rows(PR["ffn"], as_rows(A["norm_ffn_g"][l]))
                rows(PR["cw"], A["rg_conv_w"][l].rearrange("j (a n) -> (j a) n", n=P))
                rows(PR["cb"], as_rows(A["rg_conv_b"][l]))
                rows(PR["ba"], as_rows(A["rg_b_a"][l]))
                rows(PR["bx"], as_rows(A["rg_b_x"][l]))
                rows(PR["lam"], as_rows(A["rg_lambda"][l]))
                rows(PR["gba"], as_rows(A["gla_b_a"][l]))
                rows(PR["gno"], as_rows(A["gla_norm_g"][l]))
                for a in range(2):
                    sp.dma_start(prow[PR["qn"]:PR["qn"] + 1, a * DH:(a + 1) * DH],
                                 A["nsa_q_norm_g"][l].unsqueeze(0)).then_inc(sem("par_in"), 16)
                    sp.dma_start(prow[PR["kn"]:PR["kn"] + 1, a * DH:(a + 1) * DH],
                                 A["nsa_k_norm_g"][l][0:1, :]).then_inc(sem("par_in"), 16)
                sp.dma_start(strow[0:24, :], A["state_conv"][l].rearrange("b j n -> (b j) n")).then_inc(sem("par_in"), 16)
                sp.dma_start(strow[24:32, :], A["state_rglru"][l]).then_inc(sem("par_in"), 16)
                for r in range(2):
                    sp.dma_start(kgain[:, r, :], A["nsa_k_norm_g"][l][r + 1].unsqueeze(0).to_broadcast([P, DH])
                                 ).then_inc(sem("par_in"), 16)
                loads_of_phase(sp, 0, l)
                sp.wait_ge(sem("rg_out"), 1)
                sp.dma_start(O["p_rglru"][l], strow[0:1, :]).then_inc(sem("rg_st"), 16)
                sp.dma_start(O["s_rglru"][l], strow[1:9, :]).then_inc(sem("rg_st"), 16)
                sp.dma_start(O["p_conv"][l][0], strow[9:12, :]).then_inc(sem("rg_st"), 16)
                sp.dma_start(O["s_conv"][l].rearrange("b j n -> (b j) n"), strow[12:36, :]).then_inc(sem("rg_st"), 16)
                sp.wait_ge(sem("rg_st"), 64)


            @block.tensor
            def _(pe):
                norm_pe(pe, "mix")
                pe.wait_ge(sem("par_in"), PAR_IN)
                pe.transpose(bank[7][:, 0:NPR], prow[0:NPR, :], ident[0:NPR, 0:NPR])
                for k in range(KT):
                    last = pe.transpose(bank[7][:, 128 + 32 * k:160 + 32 * k], strow[0:32, k * P:(k + 1) * P],
                                        ident[0:32, 0:32])
                last.then_inc(sem("par_turned"), 1)

                def gates(n):
                    pe.wait_ge(sem("gw_in"), 32)
                    pe.wait_ge(sem("conv"), n + 1)
                    if n >= 1:
                        pe.wait_ge(sem("rg_tanh"), 2 * n)
                    else:
                        pe.wait_ge(sem("mix_h"), 1)
                    for j in range(2):
                        for half in range(2):
                            last = pe.matmul(pair[2 + j][:, half, 0:HA], gw[:, j, n, :],
                                             XC[n % 2][:, half * HA:(half + 1) * HA], start=True, stop=True)
                    last.then_inc(sem("rg_gate"), 1)

                for nm in ("rgx", "rgy"):
                    for i in range(2):
                        w = open_slab(pe, f"{nm}{i}")
                        for m in range(4):
                            n = 4 * i + m
                            proj_T(pe, (nm, n), lambda k: w[:, k, m * P:(m + 1) * P], hT,
                                   made="mix_h" if nm == "rgx" and n == 0 else None)
                            if nm == "rgx" and n >= 2:
                                gates(n - 2)
                            if nm == "rgy" and n < 2:
                                gates(6 + n)
                pe.wait_ge(sem("rg_states"), KT)
                for k in range(KT):
                    last = pe.transpose(bank[6 + k // 4][0:36, (k % 4) * P:(k % 4 + 1) * P], states[:, k, :], ident)
                last.then_inc(sem("rg_rows"), 1)

            @block.scalar
            def _(act):
                own = Own(act, sem("act_own"), own_counts["act"])
                act.dma_start(gw[:, 0, :, :], A["rg_w_a"][l].rearrange("n c d -> c n d")).then_inc(sem("gw_in"), 16)
                act.dma_start(gw[:, 1, :, :], A["rg_w_x"][l].rearrange("n c d -> c n d")).then_inc(sem("gw_in"), 16)
                for k in range(KT):
                    square_tile(act, "mix", k)
                norm_root(act, "mix", ms0)
                act.wait_ge(sem("par_set"), 1)
                own(act.activation(pk[:, 0, :], par[:, PR["lam"]:PR["lam"] + 8], ACT.Abs))
                own(act.activation(pk[:, 1, :], pk[:, 0, :], ACT.Exp, scale=-1.0))
                act.activation(pk[:, 2, :], pk[:, 1, :], ACT.Ln, bias=1.0).then_inc(sem("sp_ln"), 1)

                def evac_x(n):
                    wait_proj(act, ("rgx", n))
                    if n >= 2:
                        act.wait_ge(sem("conv"), n - 1)
                    act.activation(two(XP[n % 2][:, 3:3 + TA]), both(proj_pair(("rgx", n))),
                                   ACT.Copy).then_inc(sem("proj_read_act"), 1)

                def gate_tanh(n):
                    act.wait_ge(sem("rg_gate"), n + 1)
                    act.wait_ge(sem("sp_done"), 1)
                    if n >= 2:
                        act.wait_ge(sem("rg_v"), n - 1)
                    for j, (dst, b) in enumerate(((TR, 4), (TX, 5))):
                        act.activation(two(dst[n % 2]), both(2 + j), ACT.Tanh, scale=0.5,
                                       bias=pk[:, b, n:n + 1]).then_inc(sem("rg_tanh"), 1)
                    act.wait_ge(sem("rg_tanh"), 2 * n + 2)
                    own.tick(act.activation(DN[n % 2], TR[n % 2], ACT.Tanh, scale=pk[:, 3, n:n + 1],
                                            bias=pk[:, 3, n:n + 1]))
                    act.activation(AC[:, n, :], TR[n % 2], ACT.Exp, scale=pk[:, 6, n:n + 1],
                                   bias=pk[:, 6, n:n + 1]).then_inc(sem("rg_a"), 1)

                for n in range(KT):
                    evac_x(n)
                    if n >= 2:
                        gate_tanh(n - 2)
                gate_tanh(6)
                def gelu(n):
                    wait_proj(act, ("rgy", n))
                    act.activation(two(oaT[:, n, :]), both(proj_pair(("rgy", n))),
                                   ACT.Gelu_apprx_tanh).then_inc(sem("proj_read_act"), 1)
                gelu(0)
                gate_tanh(7)
                for n in range(1, 5):
                    gelu(n)
                for n in range(KT):
                    act.wait_ge(sem("rg_v"), n + 1)
                    act.activation(VB[:, n, :], VB[:, n, :], ACT.Sqrt).then_inc(sem("rg_sqrt"), 1)
                for n in range(5, KT):
                    gelu(n)
                act.wait_ge(sem("rg_rows"), 1)
                own.tick(act.activation(strow[0:36, 0:512], bank[6][0:36, :], ACT.Copy))
                act.activation(strow[0:36, 512:1024], bank[7][0:36, :], ACT.Copy).then_inc(sem("rg_out"), 1)

            @block.vector
            def _(dve):
                own = Own(dve, sem("dve_own"), own_counts["dve"])
                norm_mean(dve, "mix", ms0)
                dve.wait_ge(sem("par_turned"), 1)
                dve.tensor_copy(par[:, 0:NPR], bank[7][:, 0:NPR]).then_inc(sem("par_set"), 1)
                dve.wait_ge(sem("par_set"), 1)
                own(dve.tensor_copy(h0T, bank[7][:, 128:384].rearrange("p (k r) -> p k r", k=KT)))
                lam = par[:, PR["lam"]:PR["lam"] + 8]
                norm_dve(dve, own, "mix", ms0, "mix")
                dve.wait_ge(sem("sp_ln"), 1)
                own(dve.tensor_scalar(pk[:, 3, :], pk[:, 1, :], 1.0, 1.0, ALU.add, ALU.subtract))
                own(dve.tensor_scalar(pk[:, 4, :], pk[:, 3, :], 0.0, None, ALU.is_equal))
                own(dve.tensor_scalar(pk[:, 3, :], pk[:, 3, :], TINY, None, ALU.max))
                own(dve.reciprocal(pk[:, 3, :], pk[:, 3, :]))
                own(dve.tensor_tensor(pk[:, 2, :], pk[:, 2, :], pk[:, 3, :], ALU.mult))
                own(dve.tensor_tensor(pk[:, 2, :], pk[:, 2, :], pk[:, 4, :], ALU.add))
                own(dve.tensor_tensor(pk[:, 2, :], pk[:, 2, :], pk[:, 1, :], ALU.mult))
                own(dve.tensor_scalar(pk[:, 5, :], lam, -1.0, 0.0, ALU.mult, ALU.max))
                own(dve.tensor_tensor(pk[:, 2, :], pk[:, 2, :], pk[:, 5, :], ALU.add))
                own(dve.tensor_scalar(pk[:, 3, :], pk[:, 2, :], 4.0, None, ALU.mult))
                own(dve.tensor_scalar(pk[:, 6, :], pk[:, 2, :], -4.0, None, ALU.mult))
                own(dve.tensor_scalar(pk[:, 4, :], par[:, PR["ba"]:PR["ba"] + 8], 0.5, None, ALU.mult))
                dve.tensor_scalar(pk[:, 5, :], par[:, PR["bx"]:PR["bx"] + 8], 0.5, None,
                                  ALU.mult).then_inc(sem("sp_done"), 1)
                for i in range(2):
                    own(dve.memset(XP[i][:, 0:3], 0.0))

                def conv(n):
                    xp, xs, xc = XP[n % 2], XS[n % 2], XC[n % 2]
                    own.tick(dve.tensor_copy(xs[:, :, 0:3], h0T[:, n, 0:24].rearrange("p (b j) -> p b j", b=NB)))
                    dve.wait_ge(sem("proj_read_act"), n + 1)
                    if n >= 2:
                        dve.wait_ge(sem("rg_gate"), n - 1)
                    own.tick(dve.tensor_copy(xs[:, :, 3], xp[:, 3 + T:3 + TA]))
                    own(dve.tensor_scalar(xc[:, 0:T], xp[:, 0:T], conv_w(0, n), pcol("cb", n), ALU.mult, ALU.add))
                    own(dve.tensor_scalar(xc[:, T:TA], xs[:, :, 0], conv_w(0, n), pcol("cb", n), ALU.mult, ALU.add))
                    for j in range(1, 4):
                        own.tick(dve.scalar_tensor_tensor(xc[:, 0:T], xp[:, j:j + T], conv_w(j, n), xc[:, 0:T],
                                                          ALU.mult, ALU.add))
                        own(dve.scalar_tensor_tensor(xc[:, T:TA], xs[:, :, j], conv_w(j, n), xc[:, T:TA],
                                                     ALU.mult, ALU.add))
                    own.tick(dve.tensor_copy(states[:, n, 9:12], xp[:, T:T + 3]))
                    dve.tensor_copy(states[:, n, 12:36].rearrange("p (b j) -> p b j", b=NB),
                                    xs[:, :, 1:4]).then_inc(sem("conv"), 1)

                def scale(n):
                    dve.wait_ge(sem("rg_a"), n + 1)
                    own(dve.scalar_tensor_tensor(Mb[:, n, :], TX[n % 2], 1.0, XC[n % 2], ALU.add, ALU.mult))
                    own(dve.tensor_scalar(TX[n % 2], DN[n % 2], 1.0, None, ALU.add))
                    own(dve.reciprocal(TX[n % 2], TX[n % 2]))
                    dve.scalar_tensor_tensor(VB[:, n, :], DN[n % 2], 2.0, TX[n % 2], ALU.mult,
                                             ALU.mult).then_inc(sem("rg_v"), 1)

                for n in range(KT):
                    if n >= 2:
                        scale(n - 2)
                    conv(n)
                scale(6)
                scale(7)
                for n in range(KT):
                    dve.wait_ge(sem("rg_sqrt"), n + 1)
                    u = Mb[:, n, :]
                    own(dve.scalar_tensor_tensor(u, VB[:, n, :], 0.5, u, ALU.mult, ALU.mult))
                    own.tick(dve.tensor_tensor(XC[0][:, T:TA], AC[:, n, T:TA], h0T[:, n, 24:32], ALU.mult))
                    own(dve.tensor_tensor_scan(XC[1][:, 0:T], AC[:, n, 0:T], u[:, 0:T], 0.0, ALU.mult, ALU.add))
                    own(dve.tensor_tensor(XC[1][:, T:TA], XC[0][:, T:TA], u[:, T:TA], ALU.add))
                    own.tick(dve.tensor_copy(states[:, n, 0:9], XC[1][:, T - 1:TA]))
                    dve.wait_ge(sem("proj_read_act"), KT + n + 1)
                    dve.tensor_tensor(oaT[:, n, :], oaT[:, n, :], XC[1], ALU.mult).then_inc(sem("rg_states"), 1)
                    dve.wait_ge(sem("rg_states"), n + 1)


        sp1 = Space(arena[:, :])
        GQ, GK = sp1.take(GH, TA), sp1.take(GH, TA)
        EG = sp1.take(GH, NB)
        GVS = sp1.take(GH * DV)
        keep1 = sp1.at
        GB = sp1.take(GH, TA)
        GV = sp1.take(NT, GH * DV)
        ST = sp1.take(NT, DV)
        W = [sp1.take(T) for _ in range(2)]
        QP = [sp1.take(T) for _ in range(2)]
        KP = [sp1.take(T)]
        AA = [sp1.take(T)]
        EB = sp1.take(GH, NT)
        oc1 = Space(OCF)
        NZ = oc1.take(GH * TA)
        oc1.at = 0
        QE, KK, KKT, MS1 = (oc1.take(T) for _ in range(4))
        AA.append(oc1.take(T))
        OSQ = [oc1.take(T) for _ in range(2)]
        KP.append(oc1.take(T))
        gwa, GA = OBF[:, 0:GH * DK], OBF[:, GH * DK:GH * DK + TA]
        chunks = lambda ap: ap.rearrange("p (c t) -> p c t", c=NT)
        NLV = len(LEVELS)
        NPOOL = A["cache_cmp_kv"].shape[1]

        def act_before(key):
            return sum(1 for _, e in TILES[:TI[key]] if e == "act")

        def halves(ap, half):
            return ap.rearrange("p (n a t) -> p n a t", a=2, t=half)

        with nc.Block() as block:
            @block.sync
            def _(sp):
                sp.dma_start(gwa[0:RANK, :], A["gla_w_a"][l]).then_inc(sem("kc_in"), 16)
                loads_of_phase(sp, 1, l)

            @block.gpsimd
            def _(pool):
                for h in range(GH):
                    pool.wait_ge(sem("gl_s"), h + 1)
                    pool.dma_start(O["p_gla"][l][0, h], ST[:, NT - 1, :]).then_inc(sem("pgla_out"), 16)
                pool.wait_ge(sem("pgla_out"), 16 * GH)

            @block.tensor
            def _(pe):
                w = open_slab(pe, "ga")
                proj_T(pe, ("ga", 0), lambda k: w[:, k, :], hT, m=RANK)
                w = open_slab(pe, "gk")
                for m in range(4):
                    proj_T(pe, ("gk", m), lambda k: w[:, k, m * P:(m + 1) * P], hT)
                pe.wait_ge(sem("proj_read_act"), 2 * KT + 1)
                pe.wait_ge(sem("kc_in"), 16)
                for h in range(GH):
                    if h >= 2:
                        pe.wait_ge(sem("gl_z"), h - 1)
                    for half in range(2):
                        last = pe.matmul(pair[2 + h % 2][:, half, 0:HA], gwa[0:RANK, h * DK:(h + 1) * DK],
                                         GA[0:RANK, half * HA:(half + 1) * HA], start=True, stop=True)
                    last.then_inc(sem("gl_zp"), 1)
                w = open_slab(pe, "gq")
                for m in range(4):
                    proj_T(pe, ("gq", m), lambda k: w[:, k, m * P:(m + 1) * P], hT)
                for i in range(2):
                    w = open_slab(pe, f"gv{i}")
                    for tt in range(NT + 1):
                        proj_rows(pe, ("gv", i, tt), tt, w, 512)
                pe.wait_ge(sem("proj_read_act"), act_before(("gr", 0)))

                gr = {}

                def gate_steps(m):
                    key = ("gr", m)
                    if m % 4 == 0:
                        gr[0] = open_slab(pe, f"gr{m // 4}")
                    wait_proj_bank(pe, key)
                    if m >= 2:
                        pe.wait_ge(sem("gl_out" if m % 2 else "gl_s"), m // 2)
                    for half in range(2):
                        for k in range(KT):
                            last = pe.matmul(pair[proj_pair(key)][:, half, 0:HA], gr[0][:, k, m % 4 * P:(m % 4 + 1) * P],
                                             hT[:, k, half * HA:(half + 1) * HA], start=(k == 0), stop=(k == KT - 1))
                            if half and k == KT - 1:
                                last.then_inc(sem("proj_done"), 1)
                            yield

                def scores(h, i):
                    v = h * (NLV + 1) + i
                    if v >= 2:
                        pe.wait_ge(sem("gl_cp"), v - 1)
                    if i < NLV:
                        pe.wait_ge(sem("gl_qk"), h * NLV + i + 1)
                        kk, qq = KP[(h * NLV + i) % 2], QP[(h * NLV + i) % 2]
                    else:
                        kk, qq = GK[:, h, 0:T], GQ[:, h, 0:T]
                    for c_ in range(NT):
                        cs = slice(c_ * P, (c_ + 1) * P)
                        last = pe.matmul(bank[4 + v % 2][:, cs], kk[:, cs], qq[:, cs], start=True, stop=True)
                    last.then_inc(sem("gl_a"), 1)

                def turn_keys(h):
                    pe.wait_ge(sem("gl_kk"), h + 1)
                    for c_ in range(NT):
                        cs = slice(c_ * P, (c_ + 1) * P)
                        last = pe.transpose(bank[6][:, cs], KK[:, cs], ident)
                    last.then_inc(sem("gl_kt"), 1)

                def chunk_updates(h):
                    pe.wait_ge(sem("gl_kts"), h + 1)
                    pe.wait_ge(sem("proj_read_act"), act_before(("gr", 2 * h)) + 1)
                    for c_ in range(NT):
                        last = pe.matmul(bank[2 + c_ // 2][:, (c_ % 2) * DV:(c_ % 2 + 1) * DV],
                                         KKT[:, c_ * P:(c_ + 1) * P], GV[:, c_, h * DV:(h + 1) * DV],
                                         start=True, stop=True)
                    last.then_inc(sem("gl_u"), 1)

                def outputs(h):
                    pe.wait_ge(sem("gl_s"), h + 1)
                    pe.wait_ge(sem("gl_cp"), (h + 1) * (NLV + 1))
                    pe.wait_ge(sem("proj_read_act"), act_before(("gr", 2 * h + 1)) + 1)
                    for vh in range(2):
                        for c_ in range(NT):
                            cs = slice(c_ * P, (c_ + 1) * P)
                            last = pe.matmul(bank[vh][:, cs], GV[:, c_, h * DV + vh * P:h * DV + (vh + 1) * P],
                                             AA[h % 2][:, cs], start=True, stop=(c_ == 0))
                            if c_:
                                last = pe.matmul(bank[vh][:, cs], ST[:, c_ - 1, vh * P:(vh + 1) * P],
                                                 QE[:, cs], start=False, stop=True)
                    last.then_inc(sem("gl_o"), 1)

                def square_sums(h):
                    pe.wait_ge(sem("gl_osq"), h + 1)
                    for vh in range(2):
                        last = pe.matmul(bank[7], ones, OSQ[vh], start=(vh == 0), stop=(vh == 1))
                    last.then_inc(sem("gl_osum"), 1)

                for h in range(GH):
                    for i in range(NLV + 1):
                        scores(h, i)
                        if i == 0 and h:
                            outputs(h - 1)
                        if i == 2 and h:
                            square_sums(h - 1)
                        if i == 3:
                            turn_keys(h)
                        if i % 4 == 0:
                            steps = gate_steps(2 * h + i // 4)
                        for _ in range(4):
                            next(steps)
                        if i % 4 == 3:
                            next(steps, None)
                        if i == 5:
                            chunk_updates(h)
                outputs(GH - 1)
                square_sums(GH - 1)

            @block.scalar
            def _(act):
                own = Own(act, sem("act_own"), own_counts["act"])

                def evac(key, dst, fn=ACT.Copy, scale=1.0):
                    wait_proj(act, key)
                    act.activation(two(dst), both(proj_pair(key)), fn, scale=scale).then_inc(sem("proj_read_act"), 1)

                wait_proj(act, ("ga", 0))
                act.activation(two(GA[0:RANK, :]), both(proj_pair(("ga", 0)))[0:RANK], ACT.Copy
                               ).then_inc(sem("proj_read_act"), 1)
                for m in range(4):
                    evac(("gk", m), GK[:, m, :])
                for m in range(4):
                    evac(("gq", m), GQ[:, m, :], scale=DK ** -0.5)
                act.wait_ge(sem("gl_z"), GH)
                nz = NZ.rearrange("p (h t) -> p h t", h=GH)
                own(act.activation(nz, GB, ACT.Abs))
                own(act.activation(NZ, NZ, ACT.Exp, scale=-1.0))
                act.activation(NZ, NZ, ACT.Ln, bias=1.0).then_inc(sem("gl_ln"), 1)
                for i in range(2):
                    for tt in range(NT + 1):
                        key = ("gv", i, tt)
                        wait_proj(act, key)
                        rows = P if tt < NT else NB
                        dst = GV[:, tt, i * 512:(i + 1) * 512] if tt < NT else GVS[0:NB, i * 512:(i + 1) * 512]
                        act.activation(dst, pair[proj_pair(key)][0:rows, 0, :], ACT.Copy
                                       ).then_inc(sem("proj_read_act"), 1)
                act.wait_ge(sem("gl_scan"), 1)
                own.tick(act.activation(EG, GB[:, :, T:TA], ACT.Exp))
                act.activation(EB, GB[:, :, P - 1:T:P], ACT.Exp).then_inc(sem("gl_eb"), 1)

                def output_gate(m):
                    evac(("gr", m), obT[:, m, :])

                def squares(h):
                    act.wait_ge(sem("gl_o"), h + 1)
                    for vh in range(2):
                        last = act.activation(OSQ[vh], bank[vh], ACT.Square)
                        if vh == 0:
                            own.tick(last)
                    last.then_inc(sem("gl_osq"), 1)

                def decays(h):
                    act.wait_ge(sem("gl_ek"), h + 1)
                    own.tick(act.activation(KK, KK, ACT.Exp))
                    act.activation(QE, GB[:, h, 0:T], ACT.Exp).then_inc(sem("gl_ew"), 1)

                def root_and_gate(h):
                    act.wait_ge(sem("gl_oms"), h + 1)
                    act.activation(MS1, MS1, ACT.Sqrt).then_inc(sem("gl_ort"), 1)
                    act.wait_ge(sem("proj_read_act"), act_before(("gr", 2 * h + 1)) + 1)
                    o = obT[:, 2 * h:2 * h + 2, :]
                    act.activation(o, o, ACT.Silu).then_inc(sem("gl_silu"), 1)

                for h in range(GH):
                    for i in range(NLV):
                        u = h * NLV + i
                        act.wait_ge(sem("gl_d"), u + 1)
                        act.activation(W[u % 2], W[u % 2], ACT.Exp).then_inc(sem("gl_w"), 1)
                        if i == 0 and h:
                            output_gate(2 * h - 1)
                        if i == 1 and h:
                            squares(h - 1)
                        if i == 2:
                            decays(h)
                        if i == 3 and h:
                            root_and_gate(h - 1)
                        if i == 4:
                            output_gate(2 * h)
                            act.wait_ge(sem("gl_kt"), h + 1)
                            act.activation(KKT, bank[6], ACT.Copy).then_inc(sem("gl_kts"), 1)
                output_gate(2 * GH - 1)
                squares(GH - 1)
                root_and_gate(GH - 1)

            @block.vector
            def _(dve):
                own = Own(dve, sem("dve_own"), own_counts["dve"])
                own(dve.memset(GVS, 0.0))
                ksf = W[0][:, 0:NB * NPG]
                for ct in range(NB // 2):
                    own(dve.scalar_tensor_tensor(gather[:, 4 * ct:4 * ct + 4], pg_rows[:, ct:ct + 1].to_broadcast([P, 4]),
                                                 32.0, c("crow"), ALU.mult, ALU.add))
                for kv in range(2):
                    own(dve.tensor_scalar(gather[:, 16 + kv * 64:80 + kv * 64], pg_rows[:, NB // 2:], 256.0, c("srow"),
                                          ALU.mult, ALU.add))
                own(dve.tensor_scalar(pg_rows[:, :], pg_rows[:, :], float(NPOOL), None, ALU.add))
                own(dve.tensor_copy(ksf, gather[:, 80:144]))
                own(dve.tensor_scalar(gather[:, 80:144], ksf, 1.0, None, ALU.add))
                for h in range(GH):
                    dve.wait_ge(sem("gl_zp"), h + 1)
                    dve.tensor_scalar(two(GB[:, h, :]), both(2 + h % 2), par[:, PR["gba"] + h:PR["gba"] + h + 1],
                                      None, ALU.add).then_inc(sem("gl_z"), 1)
                dve.wait_ge(sem("gl_z"), GH)
                dve.wait_ge(sem("gl_ln"), 1)
                nz = NZ.rearrange("p (h t) -> p h t", h=GH)
                own(dve.scalar_tensor_tensor(GB, GB, 0.0, nz, ALU.min, ALU.subtract))
                own(dve.tensor_scalar(GB, GB, 1.0 / 16, None, ALU.mult))
                onesw = con[:, CC["ones"][0]:CC["ones"][0] + P]
                for h in range(GH):
                    for c_ in range(NT):
                        g = GB[:, h, c_ * P:(c_ + 1) * P]
                        last = own.tick(dve.tensor_tensor_scan(g, onesw, g, 0.0, ALU.mult, ALU.add))
                own.wait()
                dve.nop().then_inc(sem("gl_scan"), 1)
                for i in range(2):
                    own(dve.memset(QP[i], 0.0))
                    own(dve.memset(KP[i], 0.0))
                dve.wait_ge(sem("gl_eb"), 1)

                def diff(h, i):
                    u, half = h * NLV + i, LEVELS[i]
                    b, d = halves(GB[:, h, 0:T], half), halves(W[u % 2], half)
                    mid = b[:, :, 0, half - 1:half].to_broadcast([P, T // (2 * half), half])
                    own.tick(dve.tensor_tensor(d[:, :, 1, :], b[:, :, 1, :], mid, ALU.subtract))
                    dve.tensor_tensor(d[:, :, 0, :], mid, b[:, :, 0, :], ALU.subtract).then_inc(sem("gl_d"), 1)

                def qk(h, i):
                    u, half = h * NLV + i, LEVELS[i]
                    dve.wait_ge(sem("gl_w"), u + 1)
                    v = h * (NLV + 1) + i
                    if v >= 2:
                        dve.wait_ge(sem("gl_a"), v - 1)
                    w_ = halves(W[u % 2], half)
                    own.tick(dve.tensor_tensor(halves(QP[u % 2], half)[:, :, 1, :], halves(GQ[:, h, 0:T], half)[:, :, 1, :],
                                               w_[:, :, 1, :], ALU.mult))
                    dve.tensor_tensor(halves(KP[u % 2], half)[:, :, 0, :], halves(GK[:, h, 0:T], half)[:, :, 0, :],
                                      w_[:, :, 0, :], ALU.mult).then_inc(sem("gl_qk"), 1)
                    dve.wait_ge(sem("gl_qk"), u + 1)

                def merge(h, i):
                    v = h * (NLV + 1) + i
                    dve.wait_ge(sem("gl_a"), v + 1)
                    if i:
                        dve.wait_ge(sem("gl_cp"), v)
                    dve.copy_predicated(chunks(AA[h % 2]), rep(lmask[:, i * P:(i + 1) * P], NT),
                                        chunks(bank[4 + v % 2])).then_inc(sem("gl_cp"), 1)

                def decay_logs(h):
                    b = chunks(GB[:, h, 0:T])
                    dve.tensor_tensor(chunks(KK), b[:, :, P - 1:P].to_broadcast([P, NT, P]), b,
                                      ALU.subtract).then_inc(sem("gl_ek"), 1)

                def decayed(h):
                    dve.wait_ge(sem("gl_ew"), h + 1)
                    own.tick(dve.tensor_tensor(QE, GQ[:, h, 0:T], QE, ALU.mult))
                    dve.tensor_tensor(KK, GK[:, h, 0:T], KK, ALU.mult).then_inc(sem("gl_kk"), 1)

                def states(h):
                    dve.wait_ge(sem("gl_u"), h + 1)
                    if h:
                        dve.wait_ge(sem("gl_o"), h)
                        dve.wait_ge(sem("pgla_out"), 16 * h)
                    own(dve.tensor_copy(ST[:, 0, :], bank[2][:, 0:DV]))
                    for c_ in range(1, NT):
                        last = dve.scalar_tensor_tensor(ST[:, c_, :], ST[:, c_ - 1, :], EB[:, h, c_:c_ + 1],
                                                        bank[2 + c_ // 2][:, (c_ % 2) * DV:(c_ % 2 + 1) * DV],
                                                        ALU.mult, ALU.add)
                        if c_ < NT - 1:
                            own(last)
                    last.then_inc(sem("gl_s"), 1)

                def mean_squares(h):
                    dve.wait_ge(sem("gl_osum"), h + 1)
                    dve.tensor_scalar(MS1, bank[7], 1.0 / DV, EPS, ALU.mult, ALU.add).then_inc(sem("gl_oms"), 1)

                def gated_output(h):
                    dve.wait_ge(sem("gl_ort"), h + 1)
                    own(dve.reciprocal(MS1, MS1))
                    for vh in range(2):
                        last = dve.scalar_tensor_tensor(OSQ[vh], bank[vh], par[:, PR["gno"] + vh:PR["gno"] + vh + 1],
                                                        MS1, ALU.mult, ALU.mult)
                        if vh == 0:
                            own.tick(last)
                    last.then_inc(sem("gl_out"), 1)
                    dve.wait_ge(sem("gl_silu"), h + 1)
                    own.wait()
                    o = obT[:, 2 * h, 0:T]
                    own(dve.tensor_tensor(o, o, OSQ[0], ALU.mult))
                    dve.wait_ge(sem("gl_out"), h + 1)
                    o = obT[:, 2 * h + 1, 0:T]
                    own(dve.tensor_tensor(o, o, OSQ[1], ALU.mult))

                diff(0, 0)
                for h in range(GH):
                    if h >= 2:
                        dve.wait_ge(sem("gl_o"), h - 1)
                    own(dve.memset(AA[h % 2], 0.0))
                    for i in range(NLV):
                        if i + 1 < NLV:
                            diff(h, i + 1)
                        elif h + 1 < GH:
                            diff(h + 1, 0)
                        qk(h, i)
                        if i:
                            merge(h, i - 1)
                        elif h:
                            merge(h - 1, NLV - 1)
                            merge(h - 1, NLV)
                        if i == 1:
                            decay_logs(h)
                        if i == 2:
                            decayed(h)
                            if h:
                                mean_squares(h - 1)
                        if i == 4 and h:
                            gated_output(h - 1)
                        if i == 6:
                            states(h)
                merge(GH - 1, NLV - 1)
                merge(GH - 1, NLV)
                mean_squares(GH - 1)
                gated_output(GH - 1)

        sp2 = Space(arena[:, :])
        sp2.at = keep1
        S0 = [sp2.take(GH, DV) for _ in range(3)]
        SN = [sp2.take(GH, DV) for _ in range(3)]
        KS = sp2.take(GH * DK)
        KD = [sp2.take(GH * DK) for _ in range(2)]
        OS = sp2.take(KT * NB)
        OS2 = sp2.take(KT * NB)
        MS2 = sp2.take(GH * NB)
        with nc.Block() as block:
            @block.sync
            def _(sp):
                def load(b):
                    if b >= 3:
                        sp.wait_ge(sem("gs_s"), b - 2)
                    sp.dma_start(S0[b % 3], A["state_gla"][l][b].rearrange("h d v -> d h v")
                                 ).then_inc(sem(f"s0_in{b % 3}"), 16)
                for b in range(3):
                    load(b)
                for b in range(NB):
                    sp.wait_ge(sem("gs_s"), b + 1)
                    sp.dma_start(O["s_gla"][l][b].rearrange("h d v -> d h v"), SN[b % 3]
                                 ).then_inc(sem(f"sgla_out{b % 3}"), 16)
                    if b + 3 < NB:
                        load(b + 3)
                for i in range(3):
                    sp.wait_ge(sem(f"sgla_out{i}"), 16 * len(range(i, NB, 3)))

            @block.tensor
            def _(pe):
                for h in range(GH):
                    last = pe.transpose(bank[7][0:NB, h * DK:(h + 1) * DK], GK[:, h, T:TA], ident)
                last.then_inc(sem("gs_kt"), 1)

                def outer(b):
                    pe.wait_ge(sem("gs_kd"), b + 1)
                    if b >= 2:
                        pe.wait_ge(sem("gs_s"), b - 1)
                    for h in range(GH):
                        last = pe.matmul(pair[b % 2][:, h // 2, (h % 2) * DV:(h % 2 + 1) * DV],
                                         KD[b % 2][:, h * DK:(h + 1) * DK], GVS[:, h * DV:(h + 1) * DV],
                                         start=True, stop=True)
                    last.then_inc(sem("gs_u"), 1)

                outer(0)
                for b in range(NB):
                    if b + 1 < NB:
                        outer(b + 1)
                    pe.wait_ge(sem("gs_s"), b + 1)
                    for h in range(GH):
                        for vh in range(2):
                            j = (h * 2 + vh) * NB + b
                            last = pe.matmul(bank[4][:, j:j + 1], SN[b % 3][:, h, vh * P:(vh + 1) * P],
                                             GQ[:, h, T + b:T + b + 1], start=True, stop=True)
                    last.then_inc(sem("gs_o"), 1)
                pe.wait_ge(sem("gs_osq"), 1)
                sq = OS.rearrange("p (h v b) -> p h v b", h=GH, v=2)
                for vh in range(2):
                    last = pe.matmul(bank[5][:, 0:GH * NB], ones, sq[:, :, vh, :], start=(vh == 0), stop=(vh == 1))
                last.then_inc(sem("gs_osum"), 1)

            @block.scalar
            def _(act):
                act.wait_ge(sem("gs_o"), NB)
                act.activation(OS, bank[4][:, 0:KT * NB], ACT.Square).then_inc(sem("gs_osq"), 1)
                act.wait_ge(sem("gs_oms"), 1)
                act.activation(MS2, MS2, ACT.Sqrt).then_inc(sem("gs_ort"), 1)

            @block.vector
            def _(dve):
                own = Own(dve, sem("dve_own"), own_counts["dve"])
                own(dve.memset(KS, 0.0))
                dve.wait_ge(sem("gs_kt"), 1)
                own(dve.tensor_copy(KS[0:NB, :], bank[7][0:NB, :]))

                def one_token(b):
                    if b >= 2:
                        dve.wait_ge(sem("gs_u"), b - 1)
                    dve.tensor_scalar(KD[b % 2], KS, ident[:, b:b + 1], None,
                                      ALU.mult).then_inc(sem("gs_kd"), 1)

                one_token(0)
                one_token(1)
                for b in range(NB):
                    dve.wait_ge(sem("gs_u"), b + 1)
                    dve.wait_ge(sem(f"s0_in{b % 3}"), 16 * (b // 3 + 1))
                    if b >= 3:
                        dve.wait_ge(sem("gs_o"), b - 2)
                        dve.wait_ge(sem(f"sgla_out{b % 3}"), 16 * (b // 3))
                    for h in range(GH):
                        last = dve.scalar_tensor_tensor(SN[b % 3][:, h, :], S0[b % 3][:, h, :], EG[:, h, b:b + 1],
                                                        pair[b % 2][:, h // 2, (h % 2) * DV:(h % 2 + 1) * DV],
                                                        ALU.mult, ALU.add)
                    last.then_inc(sem("gs_s"), 1)
                    if b + 2 < NB:
                        one_token(b + 2)
                dve.wait_ge(sem("gs_osum"), 1)
                dve.tensor_scalar(MS2, bank[5][:, 0:GH * NB], 1.0 / DV, EPS, ALU.mult, ALU.add).then_inc(sem("gs_oms"), 1)
                dve.wait_ge(sem("gs_ort"), 1)
                own(dve.reciprocal(MS2, MS2))
                m = MS2.rearrange("p (h b) -> p h b", h=GH)
                o = bank[4][:, 0:KT * NB].rearrange("p (h v b) -> p h v b", h=GH, v=2)
                t = OS2.rearrange("p (h v b) -> p h v b", h=GH, v=2)
                for vh in range(2):
                    own(dve.scalar_tensor_tensor(t[:, :, vh, :], o[:, :, vh, :], par[:, PR["gno"] + vh:PR["gno"] + vh + 1],
                                                 m, ALU.mult, ALU.mult))
                own(dve.tensor_tensor(obT[:, :, T:TA], obT[:, :, T:TA], OS2.rearrange("p (k b) -> p k b", k=KT), ALU.mult))


        sp3 = Space(arena[:, :])
        GATE = sp3.take(NT, 3 * NH)
        KCP = sp3.take(G, NCP)
        VCP = sp3.take(2 * P)
        keep3 = sp3.at
        gs_row = sp3.take(3 * NH)
        CR = [sp3.take(512) for _ in range(NT + 1)]
        CTN = NB // 2 + 1
        R = [sp3.take(4, 512) for _ in range(2)]
        R2 = [sp3.take(8, 2 * DH) for _ in range(3)]
        PAIRED = ("cr_by_pool", "cr_by_act", "cr_by_dve")
        NW = 8 * CTN

        def wait_paired(eng, w_):
            for i in range(3):
                if w_ >= i:
                    eng.wait_ge(sem(PAIRED[i]), (w_ - i) // 3 + 1)

        def regroup(eng, w_):
            j = w_ // 2
            if j // 4 < CTN - 1:
                eng.wait_ge(sem(f"cr_in{j % 2}"), 16 * (j // 2 + 1))
            else:
                eng.wait_ge(sem(f"pr_in{j % 2}"), 16 * (j // 2 + 1 - 2 * (CTN - 1)))
            if w_ >= 3:
                eng.wait_ge(sem("cr_used"), 2 * w_ - 4)
            n = P if j // 4 < CTN - 1 else NCP
            src = R[j % 2][0:n, 2 * (w_ % 2):2 * (w_ % 2) + 2, :].rearrange("p s (k d) -> p k s d", d=DH)
            dst = R2[w_ % 3][0:n].rearrange("p k (s d) -> p k s d", s=2)
            return dst, src
        CT = [sp3.take(512) for _ in range(3)]
        PH = sp3.take(2, 8, P)
        P1 = [sp3.take(512) for _ in range(2)]
        NKC = 2 * NB * NCS
        oc3 = Space(OCF)
        KC = oc3.take(NKC + 2 * NCP)
        VC = oc3.take(NKC + 2 * NCP)
        SQ3 = [oc3.take(544) for _ in range(2)]
        PER = oc3.take(P)
        PEV = oc3.take(32)
        BIA = oc3.take(2)

        def comp_cols(base, ct, gp):
            if ct < CTN - 1:
                v = base[:, 0:NKC].rearrange("p (a b n) -> p a b n", a=2, b=NB)
                return v[:, gp, 2 * ct:2 * ct + 2, :]
            return base[:, NKC + gp * NCP:NKC + (gp + 1) * NCP].unsqueeze(1)

        def page_reg(eng, b, t):
            return eng.value_load(pages[0:1, b * NPG + t:b * NPG + t + 1], min_val=0,
                                  max_val=A["cache_cmp_kv"].shape[1] - 1)

        with nc.Block() as block:
            @block.sync
            def _(sp):
                for kv, t in enumerate(("nsa_phi_k", "nsa_phi_v")):
                    v = A[t][l].rearrange("(r s a) d e -> r a d s e", r=2, a=2)
                    for hf in range(2):
                        for a in range(2):
                            sp.dma_start(PH[a * DH:(a + 1) * DH, kv, :, hf * DH:(hf + 1) * DH], v[hf, a]
                                         ).then_inc(sem("par_in"), 16)
                sp.dma_start(PER[0:32, :], A["nsa_cmp_pe"][l].rearrange("k (r s a) d -> (k r s) (a d)", r=2, a=2)
                             ).then_inc(sem("par_in"), 16)
                loads_of_phase(sp, 2, l)
                for j in range(4 * CTN):
                    ct, qt = j // 4, j % 4
                    if ct == CTN - 1:
                        wait_paired(sp, 2 * (j - 1) - 1)
                        got = sem(f"pr_in{j % 2}")
                        if qt == 0:
                            for tt in range(NT):
                                sp.wait_ge(sem("proj_read_act"), sum(
                                    1 for k, e in TILES[:TI[("cmp", tt)] + 1] if e == "act"))
                                sp.dma_start(O["p_cmp_kv"][l][0, tt * P:(tt + 1) * P].rearrange(
                                    "t k g d -> t (k g d)"), CR[tt]).then_inc(sem("cmp_out"), 16)
                            sp.wait_ge(sem("proj_read_act"), sum(
                                1 for k, e in TILES[:TI[("cmp", NT)] + 1] if e == "act"))
                            sp.dma_start(O["s_cmp_kv"][l][:, 0].rearrange("t k g d -> t (k g d)"), CR[NT][0:NB, :]
                                         ).then_inc(sem("cmp_out"), 16)
                            sp.dma_start(gate_rows, gs_row[0:NB, :]).then_inc(sem("cmp_out"), 16)
                            sp.wait_ge(sem("cmp_out"), 16 * (NT + 2))
                            sp.dma_start(gate_s[:, :], gate_rows.rearrange("b (h r) -> (b h) r", r=3)
                                         ).then_inc(sem("gates_in"), 16)
                        src = O["p_cmp_kv"][l][0].rearrange("(n s) k g d -> n s (k g d)", s=STR)
                        sp.dma_start(R[j % 2][0:NCP], src[:, 4 * qt:4 * qt + 4, :]).then_inc(got, 16)
                sp.wait_ge(sem("gates_in"), 16)
                sp.wait_ge(sem("ct_sum"), 2 * CTN)
                sp.dma_start(cmp_rows[1], VC[:, 0:NKC]).then_inc(sem("kc_out"), 16)
                sp.wait_ge(sem("kc_done"), 1)
                sp.dma_start(cmp_rows[0], KC[:, 0:NKC]).then_inc(sem("kc_out"), 16)
                sp.wait_ge(sem("kc_out"), 32)

            @block.gpsimd
            def _(pool):
                rows = A["cache_cmp_kv"].rearrange("l p (c q s) k g d -> (l p c q) (s k g d)", c=8, q=4)

                def fetch(j):
                    if j < 4 * (CTN - 1):
                        pool.indirect_dma_start(R[j % 2].rearrange("p s n -> p (s n)"), None, rows,
                                                bass.IndirectOffsetOnAxis(gather[:, j:j + 1], 0)
                                                ).then_inc(sem(f"cr_in{j % 2}"), 16)

                fetch(0)
                fetch(1)
                pool.memset(KC, 0.0)
                pool.memset(VC, 0.0).then_inc(sem("kc_zero"), 1)
                for w_ in range(NW):
                    if w_ % 3 == 0:
                        dst, src = regroup(pool, w_)
                        pool.tensor_copy(dst, src).then_inc(sem(PAIRED[0]), 1)
                    if w_ % 2 and w_ // 2 + 2 < 4 * (CTN - 1):
                        wait_paired(pool, w_)
                        fetch(w_ // 2 + 2)

            @block.tensor
            def _(pe):
                w = open_slab(pe, "gate")
                for tt in range(NT + 1):
                    proj_rows(pe, ("gate", tt), tt, w, 3 * NH)
                w = open_slab(pe, "cmp")
                for tt in range(NT + 1):
                    proj_rows(pe, ("cmp", tt), tt, w, 512)
                pe.wait_ge(sem("par_in"), PAR_IN + 16 * 9)
                pe.transpose(bank[4][:, 0:32], PER[0:32, :], ident[0:32, 0:32]).then_inc(sem("pe_turned"), 1)
                pe.wait_ge(sem("pe_set"), 1)
                for kv in range(2):
                    for hf in range(2):
                        for s_ in range(8):
                            last = pe.matmul(bank[5][0:DH, kv:kv + 1], PH[:, kv, s_, hf * DH:(hf + 1) * DH],
                                             PEV[:, kv * 16 + hf * 8 + s_:kv * 16 + hf * 8 + s_ + 1],
                                             start=(hf == 0 and s_ == 0), stop=(hf == 1 and s_ == 7))
                last.then_inc(sem("bias_done"), 1)
                pe.wait_ge(sem("bias_set"), 1)

                def turn(z):
                    j, sp2_, kv = z // 4, (z // 2) % 2, z % 2
                    if kv == 0:
                        pe.wait_ge(sem(PAIRED[z // 2 % 3]), z // 6 + 1)
                    if z >= 2:
                        pe.wait_ge(sem("ct_act" if kv == 0 else "ct_dve"), (z - 2) // 2 + 1)
                    n = P if j // 4 < CTN - 1 else NCP
                    for g in range(G):
                        last = pe.transpose(bank[4 + kv][:, g * P:g * P + n],
                                            R2[z // 2 % 3][0:n, kv * G + g, :],
                                            ident[0:n, 0:n])
                    last.then_inc(sem("cr_used"), 1)

                def accumulate(z):
                    j, sp2_, kv = z // 4, (z // 2) % 2, z % 2
                    ct, qt = j // 4, j % 4
                    pe.wait_ge(sem("ct_act" if kv == 0 else "ct_dve"), z // 2 + 1)
                    if qt == 0 and sp2_ == 0 and ct >= 2:
                        pe.wait_ge(sem("ct_sum"), 2 * (ct - 1))
                    acc = bank[6 + kv] if ct % 2 == 0 else bank[2 + kv]
                    n = P if ct < CTN - 1 else NCP
                    src = CT[z % 3].rearrange("p (g n) -> p g n", g=G)[:, :, 0:n]
                    dst = acc.rearrange("p (g n) -> p g n", g=G)[:, :, 0:n]
                    pe.matmul(dst, PH[:, kv, 2 * qt + sp2_, :], src, start=(qt == 0 and sp2_ == 0),
                              stop=(qt == 3 and sp2_ == 1)).then_inc(sem("ct_mm"), 1)

                pe.wait_ge(sem("proj_read_act"), sum(1 for k, e in TILES[:TI[("cmp", NT)] + 1] if e == "act"))
                turn(0)
                for z in range(16 * CTN):
                    if z + 1 < 16 * CTN:
                        turn(z + 1)
                    accumulate(z)
                for i in range(2):
                    pe.wait_ge(sem("kc_sq"), i + 1)
                    for half in range(2):
                        last = pe.matmul(pair[2 - i][:, half, 0:272], blk, SQ3[i][:, half * 272:(half + 1) * 272],
                                         start=True, stop=True)
                    last.then_inc(sem("kc_ssum"), 1)
                for gp in range(2):
                    last = pe.transpose(bank[6][0:NCP, gp * P:(gp + 1) * P], VC[:, NKC + gp * NCP:NKC + (gp + 1) * NCP],
                                        ident)
                last.then_inc(sem("vc_turned"), 1)

            @block.scalar
            def _(act):
                own = Own(act, sem("act_own"), own_counts["act"])

                def part1(act, ct):
                    act.wait_ge(sem("ct_mm"), 16 * (ct + 1))
                    if ct:
                        act.wait_ge(sem("ct_sum"), 2 * ct)
                    for kv in range(2):
                        acc = bank[6 + kv] if ct % 2 == 0 else bank[2 + kv]
                        n = P if ct < CTN - 1 else NCP
                        act.activation(P1[kv].rearrange("p (g n) -> p g n", g=G)[0:DH, :, 0:n],
                                       acc.rearrange("p (g n) -> p g n", g=G)[DH:P, :, 0:n], ACT.Copy
                                       ).then_inc(sem("ct_p1"), 1)

                for tt in range(NT + 1):
                    wait_proj(act, ("gate", tt))
                    rows = P if tt < NT else NB
                    dst = GATE[:, tt, :] if tt < NT else gs_row[0:NB, :]
                    act.activation(dst, pair[proj_pair(("gate", tt))][0:rows, 0, 0:3 * NH], ACT.Sigmoid
                                   ).then_inc(sem("proj_read_act"), 1)
                for tt in range(NT + 1):
                    wait_proj(act, ("cmp", tt))
                    rows = P if tt < NT else NB
                    act.activation(CR[tt][0:rows, :], pair[proj_pair(("cmp", tt))][0:rows, 0, :], ACT.Copy
                                   ).then_inc(sem("proj_read_act"), 1)
                act.wait_ge(sem("pe_turned"), 1)
                act.activation(PEV, bank[4][:, 0:32], ACT.Copy).then_inc(sem("pe_set"), 1)
                def act_regroup(w_):
                    if w_ < NW and w_ % 3 == 1:
                        dst, src = regroup(act, w_)
                        act.activation(dst, src, ACT.Copy).then_inc(sem(PAIRED[1]), 1)

                act_regroup(1)
                for z in range(0, 16 * CTN, 2):
                    act_regroup(z // 2 + 2)
                    act.wait_ge(sem("cr_used"), z + 1)
                    if z >= 3:
                        act.wait_ge(sem("ct_mm"), z - 2)
                    n = P if z // 16 < CTN - 1 else NCP
                    act.activation(CT[z % 3].rearrange("p (g n) -> p g n", g=G)[:, :, 0:n],
                                   bank[4].rearrange("p (g n) -> p g n", g=G)[:, :, 0:n], ACT.Copy
                                   ).then_inc(sem("ct_act"), 1)
                    ct = z // 16
                    if z % 16 == 2 and ct >= 1:
                        part1(act, ct - 1)
                part1(act, CTN - 1)
                act.wait_ge(sem("ct_sum"), 2 * CTN)
                for i in range(2):
                    act.activation(SQ3[i], KC[:, i * 544:(i + 1) * 544], ACT.Square).then_inc(sem("kc_sq"), 1)
                for i in range(2):
                    act.wait_ge(sem("kc_ms"), i + 1)
                    act.activation(SQ3[i], SQ3[i], ACT.Sqrt).then_inc(sem("kc_rt"), 1)
                act.wait_ge(sem("vc_turned"), 1)
                own(act.activation(VCP[0:NCP, :], bank[6][0:NCP, 0:2 * P], ACT.Copy))

            @block.vector
            def _(dve):
                own = Own(dve, sem("dve_own"), own_counts["dve"])

                def add_parts(ct):
                    dve.wait_ge(sem("ct_p1"), 2 * ct + 2)
                    nb, n = (2, NCS) if ct < CTN - 1 else (1, NCP)
                    for kv, base in enumerate((KC, VC)):
                        acc = bank[6 + kv] if ct % 2 == 0 else bank[2 + kv]
                        for g in range(G):
                            a = (g % 2) * DH
                            first = acc[0:DH, g * P:g * P + nb * n].rearrange("p (b n) -> p b n", b=nb)[:, :, 0:n - 1]
                            second = P1[kv][0:DH, g * P:g * P + nb * n].rearrange("p (b n) -> p b n", b=nb)[:, :, 1:n]
                            dst = comp_cols(base, ct, g // 2)[a:a + DH, :, 0:n - 1]
                            last = dve.scalar_tensor_tensor(dst, second, BIA[0:DH, kv:kv + 1], first, ALU.add, ALU.add)
                        last.then_inc(sem("ct_sum"), 1)

                own(dve.memset(KCP, 0.0))
                own(dve.memset(VCP, 0.0))
                dve.wait_ge(sem("kc_zero"), 1)
                dve.wait_ge(sem("bias_done"), 1)
                dve.tensor_copy(BIA[0:DH, :], bank[5][0:DH, 0:2]).then_inc(sem("bias_set"), 1)
                dve.wait_ge(sem("bias_set"), 1)
                def dve_regroup(w_):
                    if w_ < NW and w_ % 3 == 2:
                        dst, src = regroup(dve, w_)
                        dve.tensor_copy(dst, src).then_inc(sem(PAIRED[2]), 1)

                for z in range(1, 16 * CTN, 2):
                    dve_regroup(z // 2 + 2)
                    dve.wait_ge(sem("cr_used"), z + 1)
                    if z >= 3:
                        dve.wait_ge(sem("ct_mm"), z - 2)
                    n = P if z // 16 < CTN - 1 else NCP
                    dve.tensor_copy(CT[z % 3].rearrange("p (g n) -> p g n", g=G)[:, :, 0:n],
                                    bank[5].rearrange("p (g n) -> p g n", g=G)[:, :, 0:n]).then_inc(sem("ct_dve"), 1)
                    ct = z // 16
                    if z % 16 == 5 and ct >= 1:
                        add_parts(ct - 1)
                add_parts(CTN - 1)
                dve.wait_ge(sem("ct_sum"), 2 * CTN)
                for i in range(2):
                    dve.wait_ge(sem("kc_ssum"), i + 1)
                    dve.tensor_scalar(SQ3[i].rearrange("p (a b) -> p a b", a=2), pair[2 - i][:, :, 0:272], 1.0 / DH, EPS,
                                      ALU.mult, ALU.add).then_inc(sem("kc_ms"), 1)
                for i in range(2):
                    dve.wait_ge(sem("kc_rt"), i + 1)
                    own(dve.reciprocal(SQ3[i], SQ3[i]))
                    k = KC[:, i * 544:(i + 1) * 544]
                    own(dve.scalar_tensor_tensor(k, k, par[:, PR["kn"]:PR["kn"] + 1], SQ3[i], ALU.mult, ALU.mult))
                for a in range(2):
                    own(dve.tensor_copy(KCP[a * DH:(a + 1) * DH, a::2, :], KC[a * DH:(a + 1) * DH, NKC:].rearrange(
                        "p (g n) -> p g n", g=2)))
                dve.nop().then_inc(sem("kc_done"), 1)

        sp4 = Space(arena[:, :])
        sp4.at = keep3
        NQ = sp4.take(KT, TA)
        KTR = [sp4.take(G, T) for _ in range(2)]
        VR = [sp4.take(NT, 256) for _ in range(2)]
        keep4 = sp4.at
        SQ4 = [sp4.take(TA) for _ in range(3)]
        oc4 = Space(OCF)
        ROW = [oc4.take(512) for _ in range(5)]
        MS4 = [oc4.take(TA) for _ in range(3)]
        qg = oc4.take(1)
        chain = [(n, tt) for n in ("slc", "win") for tt in range(NT + 1)] + [("nq", i) for i in range(KT)]
        NKV = 2 * (NT + 1)

        def rows_of(q):
            return P if chain[q][1] < NT else NB

        with nc.Block() as block:
            @block.sync
            def _(sp):
                loads_of_phase(sp, 3, l)

            @block.gpsimd
            def _(pool):
                for br in range(2):
                    for a in range(2):
                        pool.memset(KTR[br][(1 - a) * DH:(2 - a) * DH, a::2, :], 0.0)

            @block.tensor
            def _(pe):
                slabs = {}

                def proj(q):
                    n, i = chain[q]
                    name = n if n != "nq" else f"nq{i // 4}"
                    if name not in slabs:
                        slabs[name] = open_slab(pe, name)
                    w = slabs[name]
                    if n != "nq":
                        proj_rows(pe, (n, i), i, w, 512)
                    else:
                        proj_T(pe, (n, i), lambda k: w[:, k, (i % 4) * P:(i % 4 + 1) * P], hT)

                def sums(q):
                    if q < NKV:
                        return
                    pe.wait_ge(sem("kq_sq"), q + 1)
                    if q > NKV:
                        pe.wait_ge(sem("kq_ms"), q)
                    for half in range(2):
                        last = pe.matmul(pair[3][:, half, 0:HA], blk, SQ4[q % 3][:, half * HA:(half + 1) * HA],
                                         start=True, stop=True)
                    last.then_inc(sem("kq_sum"), 1)

                def turn(q):
                    if q >= NKV or q < 0:
                        return
                    r_ = rows_of(q)
                    pe.wait_ge(sem("kq_norm"), q + 1)
                    if q >= 2:
                        pe.wait_ge(sem("kq_kt"), q - 1)
                    for gp in range(2):
                        last = pe.transpose(bank[4 + q % 2][:, gp * r_:(gp + 1) * r_], ROW[q % 5][0:r_, gp * P:(gp + 1) * P],
                                            ident[0:r_, 0:r_])
                    last.then_inc(sem("kq_turn"), 1)

                for q in range(len(chain) + 4):
                    if q < len(chain):
                        proj(q)
                    if 1 <= q < len(chain) + 1:
                        sums(q - 1)
                    turn(q - 4)

            @block.scalar
            def _(act):
                own = Own(act, sem("act_own"), own_counts["act"])

                def square(q):
                    act.wait_ge(sem("proj_read_dve"), sum(1 for k, e in TILES[:TI[chain[q]] + 1] if e == "dve"))
                    if q >= 3:
                        act.wait_ge(sem("kq_ms"), q - 2)
                    if q < NKV:
                        r_ = rows_of(q)
                        act.activation(SQ4[q % 3][0:r_, 0:256], ROW[q % 5][0:r_, 0:256], ACT.Square
                                       ).then_inc(sem("kq_sq"), 1)
                    else:
                        act.activation(SQ4[q % 3], NQ[:, chain[q][1], :], ACT.Square).then_inc(sem("kq_sq"), 1)

                def root(q):
                    act.wait_ge(sem("kq_ms"), q + 1)
                    r_, w = (rows_of(q), G) if q < NKV else (P, TA)
                    act.activation(MS4[q % 3][0:r_, 0:w], MS4[q % 3][0:r_, 0:w], ACT.Sqrt).then_inc(sem("kq_rt"), 1)

                def keys(q):
                    act.wait_ge(sem("kq_turn"), q + 1)
                    br, tt, r_ = q // (NT + 1), chain[q][1], rows_of(q)
                    src = bank[4 + q % 2][:, 0:2 * r_].rearrange("p (a t) -> p a t", a=2)
                    if tt < NT:
                        for a in range(2):
                            own.tick(act.activation(KTR[br][a * DH:(a + 1) * DH, a::2, tt * P:(tt + 1) * P],
                                                    src[a * DH:(a + 1) * DH], ACT.Copy))
                    else:
                        own.tick(act.activation(knewT[:, br, :, :], src, ACT.Copy))
                    v = ROW[q % 5][0:r_, 256:512]
                    act.activation(VR[br][:, tt, :] if tt < NT else vnew[:, br, :], v, ACT.Copy
                                   ).then_inc(sem("kq_kt"), 1)
                    out = {("slc", 0): "p_slc_kv", ("win", 0): "p_win_kv", ("slc", 1): "s_slc_kv",
                           ("win", 1): "s_win_kv"}[chain[q][0], int(tt == NT)]
                    if tt < NT:
                        dst = O[out][l][0, tt * P:(tt + 1) * P]
                    else:
                        dst = O[out][l][:, 0 if out == "s_slc_kv" else WIN - 1]
                    act.wait_ge(sem("kq_norm"), q + 1)
                    act.dma_start(dst.rearrange("t k g d -> t (k g d)"), ROW[q % 5][0:r_, :]
                                  ).then_inc(sem(f"kv_out{q % 5}"), 16)

                for q in range(len(chain) + 4):
                    if q < len(chain):
                        square(q)
                    if 4 <= q < NKV + 4:
                        keys(q - 4)
                    if 1 <= q < len(chain) + 1:
                        root(q - 1)
                for i in range(5):
                    act.wait_ge(sem(f"kv_out{i}"), 16 * len(range(i, NKV, 5)))

            @block.vector
            def _(dve):
                own = Own(dve, sem("dve_own"), own_counts["dve"])
                own(dve.tensor_scalar(qg, par[:, PR["qn"]:PR["qn"] + 1], DH ** -0.5, None, ALU.mult))

                def evac(q):
                    wait_proj(dve, chain[q])
                    src = pair[proj_pair(chain[q])]
                    if q < NKV:
                        r_ = rows_of(q)
                        if q >= 5:
                            dve.wait_ge(sem("kq_kt"), q - 4)
                            dve.wait_ge(sem(f"kv_out{q % 5}"), 16 * (q // 5))
                        dve.tensor_copy(ROW[q % 5][0:r_, :], src[0:r_, 0, :]).then_inc(sem("proj_read_dve"), 1)
                    else:
                        dve.tensor_copy(two(NQ[:, chain[q][1], :]), src[:, :, 0:HA]).then_inc(sem("proj_read_dve"), 1)

                def mean(q):
                    dve.wait_ge(sem("kq_sq"), q + 1)
                    m = MS4[q % 3]
                    if q < NKV:
                        r_ = rows_of(q)
                        own(dve.reduce_sum(m[0:r_, 0:G], SQ4[q % 3][0:r_, 0:256].rearrange("p (g d) -> p g d", g=G), AX.X))
                        dve.tensor_scalar(m[0:r_, 0:G], m[0:r_, 0:G], 1.0 / DH, EPS, ALU.mult, ALU.add
                                          ).then_inc(sem("kq_ms"), 1)
                    else:
                        dve.wait_ge(sem("kq_sum"), q - NKV + 1)
                        dve.tensor_scalar(two(m), pair[3][:, :, 0:HA], 1.0 / DH, EPS, ALU.mult, ALU.add
                                          ).then_inc(sem("kq_ms"), 1)

                def scale(q):
                    dve.wait_ge(sem("kq_rt"), q + 1)
                    m = MS4[q % 3]
                    if q < NKV:
                        r_, br = rows_of(q), q // (NT + 1)
                        own(dve.reciprocal(m[0:r_, 0:G], m[0:r_, 0:G]))
                        k = ROW[q % 5][0:r_, 0:256].rearrange("p (g d) -> p g d", g=G)
                        own(dve.tensor_tensor(k, k, bc(m[0:r_, 0:G], DH), ALU.mult))
                        dve.tensor_tensor(k, k, rep(kgain[0:r_, br, :], G), ALU.mult).then_inc(sem("kq_norm"), 1)
                        dve.wait_ge(sem("kq_norm"), q + 1)
                    else:
                        own(dve.reciprocal(m, m))
                        x = NQ[:, chain[q][1], :]
                        own(dve.scalar_tensor_tensor(x, x, qg, m, ALU.mult, ALU.mult))

                for q in range(len(chain) + 2):
                    if q < len(chain):
                        evac(q)
                    if q >= 2:
                        scale(q - 2)
                    if 1 <= q < len(chain) + 1:
                        mean(q - 1)
                own(dve.tensor_copy(nqs[:, :, :], NQ[:, :, T:TA]))

        sp5 = Space(arena[:, :])
        sp5.at = keep4
        NSC = 7
        SC = [sp5.take(T) for _ in range(NSC)]
        free_slot = ring[:, (MARKS[3] + NSLOT - 1) % NSLOT, :]
        PTS = [free_slot[:, i * NT * T:(i + 1) * NT * T].rearrange("p (k n) -> p k n", k=NT) for i in range(2)]
        PTC = sp5.take(1, T)
        PT = [PTC, PTS[0], PTS[1]]
        stat = sp5.take(NSC, 3, 4)
        DG = [sp5.take(P) for _ in range(4)]
        S_BANK, T_BANK = (0, 1, 6, 7), (2, 3)
        NSB, NTB = len(S_BANK), len(T_BANK)
        AHEAD_S, AHEAD_B, AHEAD_M, LAG_C, LAG_V = 4, 3, 2, 2, 3
        units = []
        for i in range(NT):
            for g in range(G):
                units.append((i, g, 0, None))
                units += [(i, g, br, p_) for br in (1, 2) for p_ in range(HPG)]
        NU = len(units)
        last_unit = [9 * (v // 3) + (0, 4, 8)[v % 3] for v in range(3 * NT * G)]
        branch_of = {u: v for v, u in enumerate(last_unit)}
        U2V = [3 * (u // 9) + (0 if u % 9 == 0 else 1 + (u % 9 - 1) // 4) for u in range(NU)]

        with nc.Block() as block:
            @block.sync
            def _(sp):
                sp.dma_start(O["s_win_kv"][l][:, 0:WIN - 1].rearrange("b w k g d -> b (w k g d)"),
                             A["cache_win_kv"][l][:, 1:WIN].rearrange("b w k g d -> b (w k g d)")
                             ).then_inc(sem("win_moved"), 16)

            @block.tensor
            def _(pe):
                def scores(u):
                    i, g, br, p_ = units[u]
                    a, gp = (g % 2) * DH, g // 2
                    if u >= NSB:
                        pe.wait_ge(sem("sa_read"), u - NSB + 1)
                    out = bank[S_BANK[u % NSB]]
                    if br == 0:
                        for h in range(HPG):
                            last = pe.matmul(out[:, h * NCP:(h + 1) * NCP], NQ[:, gp * 4 + h, i * P:(i + 1) * P],
                                             KCP[:, g, :], start=True, stop=True)
                    else:
                        n = (i + 1) * P
                        last = pe.matmul(out[:, 0:n], NQ[:, gp * 4 + p_, i * P:(i + 1) * P],
                                         KTR[br - 1][:, g, 0:n], start=True, stop=True)
                    last.then_inc(sem("sa_s"), 1)

                def turn(u):
                    i, g, br, p_ = units[u]
                    if br == 0:
                        pe.wait_ge(sem("sa_pc"), u // 9 + 1)
                    else:
                        pe.wait_ge(sem("sa_p"), u - u // 9)
                    if u >= NTB:
                        pe.wait_ge(sem("sa_pt"), u - NTB + 1)
                    out = bank[T_BANK[u % NTB]]
                    if br == 0:
                        for h in range(HPG):
                            last = pe.transpose(out[0:NCP, h * P:(h + 1) * P], SC[u % NSC][:, h * NCP:(h + 1) * NCP], ident)
                    else:
                        for kt in range(i + 1):
                            last = pe.matmul(out[:, kt * P:(kt + 1) * P], SC[u % NSC][:, kt * P:(kt + 1) * P],
                                             DG[u % 4], start=True, stop=True)
                    last.then_inc(sem("sa_t"), 1)

                def values(v):
                    i, g, br, _ = units[last_unit[v]]
                    a = (g % 2) * DH
                    pe.wait_ge(sem("sa_pt"), last_unit[v] + 1)
                    q = v // 3
                    if br == 0 and q >= 2:
                        pe.wait_ge(sem("sa_o"), q - 1)
                    out = bank[4 + q % 2][a:a + DH, :]
                    if br == 0:
                        last = pe.matmul(out, VCP[:, g * DH:(g + 1) * DH], PTC[:, 0, :],
                                         start=True, stop=False)
                    else:
                        for kt in range(i + 1):
                            last = pe.matmul(out, VR[br - 1][:, kt, g * DH:(g + 1) * DH], PT[br][:, kt, :],
                                             start=False, stop=(br == 2 and kt == i))
                    last.then_inc(sem("sa_pv"), 1)

                for u in range(AHEAD_S):
                    scores(u)
                for u in range(NU + LAG_V):
                    if u + AHEAD_S < NU:
                        scores(u + AHEAD_S)
                    if u < NU:
                        turn(u)
                    if u - LAG_V in branch_of:
                        values(branch_of[u - LAG_V])

            @block.scalar
            def _(act):
                def exps(u):
                    i, g, br, p_ = units[u]
                    act.wait_ge(sem("sa_m"), u + 1)
                    s = SC[u % NSC]
                    if br == 0:
                        act.activation(s[:, 0:P], s[:, 0:P], ACT.Exp).then_inc(sem("sa_e"), 1)
                    else:
                        n = (i + 1) * P
                        act.activation(s[:, 0:n], s[:, 0:n], ACT.Exp, bias=stat[:, u % NSC, 0, 0:1],
                                       accum_out=stat[:, u % NSC, 1, 0:1]).then_inc(sem("sa_e"), 1)

                def copy(u):
                    i, g, br, p_ = units[u]
                    v = U2V[u]
                    act.wait_ge(sem("sa_t"), u + 1)
                    if v >= 3:
                        act.wait_ge(sem("sa_pv"), v - 2)
                    src = bank[T_BANK[u % NTB]]
                    if br == 0:
                        act.activation(PTC[0:NCP, 0, :], src[0:NCP, :], ACT.Copy).then_inc(sem("sa_pt"), 1)
                    else:
                        act.activation(PT[br][:, 0:i + 1, p_ * P:(p_ + 1) * P],
                                       src[:, 0:(i + 1) * P].rearrange("p (k t) -> p k t", t=P), ACT.Copy
                                       ).then_inc(sem("sa_pt"), 1)

                def out(q):
                    i, g = q // G, q % G
                    a, gp = (g % 2) * DH, g // 2
                    act.wait_ge(sem("sa_pv"), 3 * q + 3)
                    act.activation(ocT[a:a + DH, gp * 4:gp * 4 + 4, i * P:(i + 1) * P],
                                   bank[4 + q % 2][a:a + DH, :].rearrange("p (h t) -> p h t", h=HPG), ACT.Copy
                                   ).then_inc(sem("sa_o"), 1)

                for u in range(NU + 6):
                    if u < NU:
                        exps(u)
                    if LAG_C <= u < NU + LAG_C:
                        copy(u - LAG_C)
                    if u >= 6 and (u - 6) % 9 == 8:
                        out((u - 6) // 9)

            @block.vector
            def _(dve):
                own = Own(dve, sem("dve_own"), own_counts["dve"])
                nsl, dist, dcmp, mcmp = c("nsl"), c("dist"), c("dcmp"), c("mcmp")

                def biased(u):
                    i, g, br, p_ = units[u]
                    s = SC[u % NSC]
                    if u >= NSC:
                        dve.wait_ge(sem("sa_t"), u - NSC + 1)
                    dve.wait_ge(sem("sa_s"), u + 1)
                    src = bank[S_BANK[u % NSB]]
                    if br == 0:
                        s3 = s[:, 0:P].rearrange("p (h n) -> p h n", h=HPG)
                        own(dve.tensor_tensor(s3, bc(nsl[:, 4 * g:4 * g + 4], NCP),
                                              rep(dcmp[:, i * NCP:(i + 1) * NCP], HPG), ALU.mult))
                        dve.tensor_tensor(s[:, 0:P], s[:, 0:P], src[:, 0:P], ALU.add).then_inc(sem("sa_read"), 1)
                    else:
                        n = (i + 1) * P
                        dve.scalar_tensor_tensor(s[:, 0:n], dist[:, 384 - i * P:384 - i * P + n], -SLOPE[4 * g + p_],
                                                 src[:, 0:n], ALU.mult, ALU.add).then_inc(sem("sa_read"), 1)

                def maximum(u):
                    i, g, br, p_ = units[u]
                    s, st = SC[u % NSC], stat[:, u % NSC]
                    dve.wait_ge(sem("sa_read"), u + 1)
                    if br == 0:
                        s3 = s[:, 0:P].rearrange("p (h n) -> p h n", h=HPG)
                        own(dve.reduce_max(st[:, 0, :], s3, AX.X))
                        dve.tensor_tensor(s3, s3, bc(st[:, 0, :], NCP), ALU.subtract).then_inc(sem("sa_m"), 1)
                    else:
                        dve.tensor_reduce(st[:, 0, 0:1], s[:, 0:(i + 1) * P], AX.X, ALU.max, negate=True
                                          ).then_inc(sem("sa_m"), 1)

                def scale(u):
                    i, g, br, p_ = units[u]
                    s, st = SC[u % NSC], stat[:, u % NSC]
                    dve.wait_ge(sem("sa_e"), u + 1)
                    if br == 0:
                        s3 = s[:, 0:P].rearrange("p (h n) -> p h n", h=HPG)
                        own(dve.tensor_tensor(s3, s3, rep(mcmp[:, i * NCP:(i + 1) * NCP], HPG), ALU.mult))
                        own(dve.reduce_sum(st[:, 1, :], s3, AX.X))
                        own(dve.tensor_scalar(st[:, 1, :], st[:, 1, :], TINY, None, ALU.max))
                        own(dve.reciprocal(st[:, 1, :], st[:, 1, :]))
                        gt = GATE[:, i, 12 * g:12 * g + 12].rearrange("p (h r) -> p h r", r=3)[:, :, 0]
                        own(dve.tensor_tensor(st[:, 1, :], st[:, 1, :], gt, ALU.mult))
                        dve.tensor_tensor(s3, s3, bc(st[:, 1, :], NCP), ALU.mult).then_inc(sem("sa_pc"), 1)
                    else:
                        dve.reciprocal(st[:, 1, 0:1], st[:, 1, 0:1]).then_inc(sem("sa_r"), 1)

                def diagonal(u):
                    i, g, br, p_ = units[u]
                    k = (4 * g + p_) * 3 + br
                    dve.wait_ge(sem("sa_r"), u - u // 9)
                    if u >= 4:
                        dve.wait_ge(sem("sa_t"), u - 3)
                    dve.tensor_scalar(DG[u % 4], ident, stat[:, u % NSC, 1, 0:1], GATE[:, i, k:k + 1], ALU.mult,
                                      ALU.mult).then_inc(sem("sa_p"), 1)

                own(dve.memset(PTC, 0.0))
                for u in range(-AHEAD_B, NU):
                    if u >= 0:
                        scale(u)
                    if u + AHEAD_B < NU:
                        biased(u + AHEAD_B)
                    if 0 <= u + AHEAD_M < NU:
                        maximum(u + AHEAD_M)
                    if u >= 0 and units[u][2] > 0:
                        diagonal(u)

        sp6 = Space(arena[:, :])
        KC6, VC6 = sp6.take(2, NB, NCS), sp6.take(2, NB, NCS)
        VCR = sp6.take(NB, 2 * P)
        qbd_at = sp6.at
        QBD = sp6.take(NB, 2, P)
        UR = [sp6.take(4, 256) for _ in range(4)]
        UR += [free_slot[:, i * 1024:(i + 1) * 1024].rearrange("p (a n) -> p a n", a=4) for i in range(4)]
        NUR = len(UR)
        KTS = [sp6.take(512) for _ in range(2)]
        SS = sp6.take(PAST + 1)
        SW = sp6.take(WIN + 1)
        SCC = sp6.take(NCS)
        SCG = sp6.take(NCS)
        IM = sp6.take(14)
        DR = sp6.take(14)
        st6 = sp6.take(16)
        PNR = sp6.take(2, NB)
        PTA = sp6.take(13, P)
        oc6 = None
        OUT_BANK = (0, 1, 2, 7)
        OALL = SS[:, 0:512]
        OPART = [sp6.take(DH) for _ in range(4)]
        OROW = sp6.take(P)
        kunits = [(0, t, bh) for t in range(NPG) for bh in range(2)] + [(1, t, bh) for t in range(4) for bh in range(2)]
        vunits = [(b, part) for b in range(NB) for part in range(3)]
        NKU, NVU = len(kunits), len(vunits)
        paged = [br == 0 for br, _, _ in kunits] + [part < 2 for _, part in vunits]
        SPQ = [(f"s0_in{i}", 16 * len(range(i, NB, 3))) for i in range(3)]
        SPQ += [(f"sgla_out{i}", 16 * len(range(i, NB, 3))) for i in range(3)] + [("unit_sp6", 0), ("unit_sp7", 0)]
        POOLQ = [(f"cr_in{i}", 16 * 2 * (CTN - 1)) for i in range(2)] + [(f"unit_pool{i}", 0) for i in range(2, NUR)]
        usp = [SPQ[n % NUR][1] + 16 * sum(3 if x else 1 for x in paged[n % NUR:n + 1:NUR]) for n in range(NKU + NVU)]
        upool = [POOLQ[n % NUR][1] + 16 * sum(paged[n % NUR:n + 1:NUR]) for n in range(NKU + NVU)]

        def wait_slot(eng, n):
            if NUR <= n < NKU + NUR:
                eng.wait_ge(sem("ku_turned"), 2 * (n - NUR) + 2)
            elif n >= NKU + NUR:
                eng.wait_ge(sem("vu_used"), n - NUR - NKU + 1)

        def wait_unit(eng, n):
            eng.wait_ge(sem(SPQ[n % NUR][0]), usp[n])
            if paged[n]:
                eng.wait_ge(sem(POOLQ[n % NUR][0]), upool[n])

        def load_page(eng, n, i):
            kv, t, b = (0, kunits[n][1], 4 * kunits[n][2] + i) if n < NKU else (
                1, 4 * vunits[n - NKU][1] + i, vunits[n - NKU][0])
            pg = page_reg(eng, b, t)
            eng.dma_start(UR[n % NUR][:, i, :], A["cache_slc_kv"][l][bass.ds(pg, 1)].rearrange(
                "o s k g d -> (o s) k (g d)")[:, kv, :]).then_inc(sem(SPQ[n % NUR][0]), 16)

        with nc.Block() as block:
            @block.sync
            def _(sp):
                for n in range(NKU + NVU):
                    if n == 2:
                        sp.dma_start(KC6.rearrange("p a b n -> p (a b n)"), cmp_rows[0]).then_inc(sem("kc_in"), 16)
                        sp.dma_start(VC6.rearrange("p a b n -> p (a b n)"), cmp_rows[1]).then_inc(sem("kc_in"), 16)
                    wait_slot(sp, n)
                    got, u = sem(SPQ[n % NUR][0]), UR[n % NUR]
                    if paged[n]:
                        for i in range(3 if n < NKU + NUR else 2):
                            load_page(sp, n, i)
                    elif n < NKU:
                        _, t, bh = kunits[n]
                        sp.dma_start(u, A["cache_win_kv"][l][4 * bh:4 * bh + 4, t * P:(t + 1) * P].rearrange(
                            "b s k g d -> s b k (g d)")[:, :, 0, :]).then_inc(got, 16)
                    else:
                        sp.dma_start(u, A["cache_win_kv"][l][vunits[n - NKU][0]].rearrange(
                            "(t s) k g d -> s t k (g d)", s=P)[:, :, 1, :]).then_inc(got, 16)

            @block.gpsimd
            def _(pool):
                rows = A["cache_slc_kv"].rearrange("l p s k g d -> (l p s k) (g d)")
                for n in range(NKU + NVU):
                    if not paged[n]:
                        continue
                    wait_slot(pool, n)
                    if n < NKU:
                        _, t, bh = kunits[n]
                        col = 16 + (4 * bh + 3) * NPG + t
                    else:
                        b, part = vunits[n - NKU]
                        col = 80 + b * NPG + 4 * part + 3
                    pool.indirect_dma_start(UR[n % NUR][:, 3, :], None, rows,
                                            bass.IndirectOffsetOnAxis(gather[:, col:col + 1], 0)
                                            ).then_inc(sem(POOLQ[n % NUR][0]), 16)
                for i, (got, _) in enumerate(POOLQ):
                    pool.wait_ge(sem(got), max(upool[i::NUR]))

            @block.tensor
            def _(pe):
                def compressed_scores():
                    pe.wait_ge(sem("kc_in"), 48)
                    for b in range(NB):
                        for gp in range(2):
                            last = pe.matmul(bank[3][:, 64:64 + NCS], QBD[:, b, gp, :], KC6[:, gp, b, :],
                                             start=(b == 0 and gp == 0), stop=(b == NB - 1 and gp == 1))
                    for br in range(2):
                        for b in range(NB):
                            for gp in range(2):
                                last = pe.matmul(bank[3][:, br:br + 1], QBD[:, b, gp, :], knewT[:, br, gp, b:b + 1],
                                                 start=(b == 0 and gp == 0), stop=(b == NB - 1 and gp == 1))
                    last.then_inc(sem("s6_small"), 1)

                def turn_vc(i):
                    if i:
                        pe.wait_ge(sem("vcr"), i)
                    for b in range(2 * i, 2 * i + 2):
                        for gp in range(2):
                            last = pe.transpose(bank[6][0:NCS, (b % 2) * 256 + gp * P:(b % 2) * 256 + (gp + 1) * P],
                                                VC6[:, gp, b, :], ident)
                    last.then_inc(sem("vc6_turned"), 1)

                def turn(hu):
                    n, h2 = hu // 2, hu % 2
                    if h2 == 0:
                        wait_unit(pe, n)
                    if hu >= 2:
                        pe.wait_ge(sem("kt_act" if h2 == 0 else "kt_dve"), hu // 2)
                    for j in range(4):
                        last = pe.transpose(bank[4 + h2][:, j * P:(j + 1) * P],
                                            UR[n % NUR][:, 2 * h2 + j // 2, (j % 2) * P:(j % 2 + 1) * P], ident)
                    last.then_inc(sem("ku_turned"), 1)

                def score(hu):
                    n, h2 = hu // 2, hu % 2
                    br, t, bh = kunits[n]
                    pe.wait_ge(sem("kt_act" if h2 == 0 else "kt_dve"), hu // 2 + 1)
                    out = bank[2 if br else t // 4][:, (t % 4) * P:(t % 4 + 1) * P]
                    for j in range(4):
                        b = 4 * bh + 2 * h2 + j // 2
                        last = pe.matmul(out, QBD[:, b, j % 2, :], KTS[h2][:, j * P:(j + 1) * P],
                                         start=(b == 0 and j == 0), stop=(b == NB - 1 and j == 3))
                    last.then_inc(sem("ku_scored"), 1)

                turn(0)
                for hu in range(2 * NKU):
                    if hu + 1 < 2 * NKU:
                        turn(hu + 1)
                    if hu == 0:
                        pe.wait_ge(sem("qbd"), 4)
                    score(hu)
                    if hu == 5:
                        compressed_scores()
                    if hu % 8 == 6 and hu < 32:
                        turn_vc(hu // 8)
                    if hu == 14:
                        pe.wait_ge(sem("pc"), 1)
                        pe.transpose(bank[7][0:NCS, P:2 * P], SCC, ident).then_inc(sem("pc_turned"), 1)
                    if hu == 17:
                        pe.wait_ge(sem("pct"), 1)
                        pe.matmul(bank[7][:, 0:14], PTA[0:NCS, 12, :], c("c2s", NCS), start=True, stop=True
                                  ).then_inc(sem("pc_turned"), 1)
                    if hu == 20:
                        pe.wait_ge(sem("pct"), 2)
                        pe.matmul(bank[7][:, 16:30], c("grp"), IM, start=True, stop=True
                                  ).then_inc(sem("pc_turned"), 1)
                    if hu == 44:
                        pe.wait_ge(sem("p6"), 1)
                        for t in range(NPG):
                            last = pe.transpose(bank[t // 4][:, (t % 4) * P:(t % 4 + 1) * P],
                                                SS[:, t * P:(t + 1) * P], ident)
                        last.then_inc(sem("p6_turned"), 1)
                pe.wait_ge(sem("p6"), 2)
                for t in range(4):
                    pe.transpose(bank[3][:, t * P:(t + 1) * P], SW[:, t * P:(t + 1) * P], ident)
                pe.transpose(bank[6][0:NCS, 0:P], SCG, ident)
                for br in range(2):
                    last = pe.transpose(bank[6][0:NB, P * (1 + br):P * (2 + br)], PNR[:, br, :], ident)
                last.then_inc(sem("p6_turned"), 1)
                pe.wait_ge(sem("pta"), 2)
                for b in range(NB):
                    out = bank[OUT_BANK[b // 2]][:, (b % 2) * 256:(b % 2 + 1) * 256]
                    pe.matmul(out, PTA[:, 12, :], VCR[:, b, :], start=True, stop=False)
                    for part in range(3):
                        n = NKU + 3 * b + part
                        wait_unit(pe, n)
                        for t in range(4):
                            last = pe.matmul(out, PTA[:, part * 4 + t, :],
                                             UR[n % NUR][:, t, :], start=False, stop=(part == 2 and t == 3))
                        last.then_inc(sem("vu_used"), 1)
                pe.wait_ge(sem("pta"), 3)
                pe.transpose(bank[6][:, 0:P], OROW[:, 0:P], ident).then_inc(sem("p6_turned"), 1)

            @block.scalar
            def _(act):
                own = Own(act, sem("act_own"), own_counts["act"])
                def exps(i):
                    s_, k = ((SCC, 0), (SS, 2), (SW, 4))[i]
                    act.wait_ge(sem("s6_max"), i + 1)
                    act.activation(s_, s_, ACT.Exp, bias=st6[:, k:k + 1], accum_out=st6[:, k + 1:k + 2]
                                   ).then_inc(sem("s6_exp"), 1)

                for hu in range(0, 2 * NKU, 2):
                    act.wait_ge(sem("ku_turned"), hu + 1)
                    if hu >= 2:
                        act.wait_ge(sem("ku_scored"), hu - 1)
                    act.activation(KTS[0], bank[4], ACT.Copy).then_inc(sem("kt_act"), 1)
                    if hu in (12, 38):
                        exps(0 if hu == 12 else 1)
                    if hu % 8 == 0 and 8 <= hu < 40:
                        i = hu // 8 - 1
                        act.wait_ge(sem("vc6_turned"), i + 1)
                        act.wait_ge(sem("qbd"), 6)
                        act.activation(VCR[0:NCS, 2 * i:2 * i + 2, :],
                                       bank[6][0:NCS, :].rearrange("p (b n) -> p b n", b=2), ACT.Copy
                                       ).then_inc(sem("vcr"), 1)
                exps(2)
                for n in range(NKU + NUR, NKU + NVU):
                    if paged[n]:
                        wait_slot(act, n)
                        load_page(act, n, 2)

            @block.vector
            def _(dve):
                own = Own(dve, sem("dve_own"), own_counts["dve"])
                own(dve.memset(QBD, 0.0))
                for gp in range(2):
                    for a in range(2):
                        c0 = qbd_at + gp * P + gp * 8 + a * 4
                        dst = arena[a * DH:(a + 1) * DH, c0:c0 + NB * (2 * P + NH)].rearrange(
                            "p (b n) -> p b n", b=NB)[:, :, 0:4]
                        dve.tensor_copy(dst, nqs[a * DH:(a + 1) * DH, gp * 4:gp * 4 + 4, :].rearrange(
                            "p h b -> p b h")).then_inc(sem("qbd"), 1)
                own(dve.memset(PTA[:, 12, :], 0.0))
                own(dve.memset(VCR, 0.0))
                for br in range(2):
                    dve.tensor_copy(VCR[DH + 32 * br:DH + 32 * br + NB, :, :], rep(vnew[:, br, :], NB)
                                    ).then_inc(sem("qbd"), 1)
                nslr, drow = c("nslr"), c("drow")

                def compressed_biased():
                    dve.wait_ge(sem("s6_small"), 1)
                    own(dve.scalar_tensor_tensor(SCC, c("dcs"), nslr, bank[3][:, 64:64 + NCS], ALU.mult, ALU.add))
                    own(dve.tensor_copy(SS[:, PAST:PAST + 1], bank[3][:, 0:1]))
                    own(dve.tensor_copy(SW[:, WIN:WIN + 1], bank[3][:, 1:2]))
                    dve.tensor_reduce(st6[:, 0:1], SCC, AX.X, ALU.max, negate=True).then_inc(sem("s6_max"), 1)

                def compressed_probs():
                    dve.wait_ge(sem("s6_exp"), 1)
                    own(dve.reciprocal(st6[:, 1:2], st6[:, 1:2]))
                    dve.tensor_scalar(SCC, SCC, st6[:, 1:2], None, ALU.mult).then_inc(sem("pc"), 1)
                    dve.wait_ge(sem("pc"), 1)
                    own(dve.tensor_scalar(SCG, SCC, gate_s[:, 0:1], None, ALU.mult))

                def importance_of_heads():
                    dve.wait_ge(sem("pc_turned"), 1)
                    dve.tensor_copy(PTA[0:NCS, 12, :], bank[7][0:NCS, P:2 * P]).then_inc(sem("pct"), 1)

                def importance_copied():
                    dve.wait_ge(sem("pc_turned"), 2)
                    dve.tensor_copy(IM, bank[7][:, 0:14]).then_inc(sem("pct"), 1)

                def dropped():
                    dve.wait_ge(sem("pc_turned"), 3)
                    own(dve.tensor_copy(IM, bank[7][:, 16:30]))
                    own(dve.tensor_reduce(st6[:, 6:7], IM, AX.X, ALU.min))
                    own(dve.tensor_scalar(DR, IM, st6[:, 6:7], None, ALU.is_equal))
                    own(dve.tensor_tensor(DR, DR, c("jj"), ALU.mult))
                    own(dve.tensor_reduce(st6[:, 7:8], DR, AX.X, ALU.max))
                    own(dve.tensor_scalar(DR, c("jj"), st6[:, 7:8], -1e30, ALU.is_equal, ALU.mult))

                def selected_biased(i):
                    dve.wait_ge(sem("ku_scored"), 16 * (i + 1))
                    own(dve.scalar_tensor_tensor(SS[:, 512 * i:512 * i + 512], drow[:, 512 * i:512 * i + 512], nslr,
                                                 bank[i], ALU.mult, ALU.add))

                def selected_max():
                    mid = SS[:, SEL:15 * SEL].rearrange("p (j s) -> p j s", s=SEL)
                    own(dve.tensor_tensor(mid, mid, bc(DR, SEL), ALU.add))
                    dve.tensor_reduce(st6[:, 2:3], SS, AX.X, ALU.max, negate=True).then_inc(sem("s6_max"), 1)

                def window_max():
                    dve.wait_ge(sem("ku_scored"), 2 * NKU)
                    own(dve.scalar_tensor_tensor(SW[:, 0:WIN], drow[:, PAST - WIN:PAST], nslr, bank[2],
                                                 ALU.mult, ALU.add))
                    dve.tensor_reduce(st6[:, 4:5], SW, AX.X, ALU.max, negate=True).then_inc(sem("s6_max"), 1)

                def weighted(i):
                    s_, k, n = ((SS, 2, PAST), (SW, 4, WIN))[i]
                    dve.wait_ge(sem("s6_exp"), i + 2)
                    own(dve.reciprocal(st6[:, k + 1:k + 2], st6[:, k + 1:k + 2]))
                    own(dve.tensor_scalar(s_, s_, st6[:, k + 1:k + 2], gate_s[:, i + 1:i + 2], ALU.mult, ALU.mult))
                    dve.tensor_scalar(PNR[:, i, :], c("bsel"), s_[:, n:n + 1], None, ALU.mult).then_inc(sem("p6"), 1)

                for hu in range(1, 2 * NKU, 2):
                    dve.wait_ge(sem("ku_turned"), hu + 1)
                    if hu >= 2:
                        dve.wait_ge(sem("ku_scored"), hu - 1)
                    dve.tensor_copy(KTS[1], bank[5]).then_inc(sem("kt_dve"), 1)
                    if hu == 11:
                        compressed_biased()
                    if hu == 15:
                        compressed_probs()
                    if hu == 17:
                        importance_of_heads()
                    if hu == 19:
                        importance_copied()
                        selected_biased(0)
                    if hu == 23:
                        dropped()
                    if hu == 35:
                        selected_biased(1)
                    if hu == 37:
                        selected_max()
                    if hu == 41:
                        weighted(0)
                window_max()
                dve.wait_ge(sem("p6_turned"), 1)
                for i in range(2):
                    own.tick(dve.tensor_copy(PTA[:, 4 * i:4 * i + 4, :], bank[i].rearrange("p (t n) -> p t n", t=4)))
                weighted(1)
                dve.wait_ge(sem("p6_turned"), 2)
                own(dve.tensor_copy(PTA[:, 8:12, :], bank[3].rearrange("p (t n) -> p t n", t=4)))
                own(dve.tensor_copy(PTA[0:NCS, 12, :], bank[6][0:NCS, 0:P]))
                for br in range(2):
                    dve.tensor_copy(PTA[DH + 32 * br:DH + 32 * br + NB, 12, :], bank[6][0:NB, P * (1 + br):P * (2 + br)]
                                    ).then_inc(sem("pta"), 1)
                own_part = c("grp")[:, ::HPG]
                for i in range(4):
                    dve.wait_ge(sem("vu_used"), 6 * i + 6)
                    own(dve.tensor_tensor(OALL.rearrange("p (n d) -> p n d", d=DH),
                                          bank[OUT_BANK[i]].rearrange("p (n d) -> p n d", d=DH),
                                          bc(own_part[:, 8 * i:8 * i + 8], DH), ALU.mult))
                    own(dve.tensor_reduce(OPART[i], OALL.rearrange("p (n d) -> p d n", d=DH), AX.X, ALU.add))
                    if i:
                        own(dve.tensor_tensor(OPART[i], OPART[i - 1], OPART[i], ALU.add))
                dve.tensor_copy(OROW.rearrange("p (a d) -> p a d", a=2), rep(OPART[3], 2)).then_inc(sem("pta"), 1)
                dve.wait_ge(sem("p6_turned"), 3)
                for gp in range(2):
                    for a in range(2):
                        o = bank[6][a * DH:(a + 1) * DH, 0:P].rearrange("p (b h) -> p h b", h=NH)
                        own(dve.tensor_copy(ocT[a * DH:(a + 1) * DH, gp * 4:gp * 4 + 4, T:TA],
                                            o[:, gp * 8 + a * 4:gp * 8 + a * 4 + 4, :]))

        sp7 = Space(arena[:, :])
        MG = sp7.take(KT, TA)
        SG = [sp7.take(TA) for _ in range(3)]
        TMP = sp7.take(TA)
        sp8 = Space(arena[:, :])
        FA = sp8.take(FT, TA)
        SGF = [sp8.take(TA) for _ in range(2)]
        assert sp7.at <= sp8.at
        tag_sq["ffn"] = [sp8.take(TA) for _ in range(2)]
        ms8 = sp8.take(TA)
        mkeys = [(hf, br, m) for hf in range(2) for br in range(3) for m in range(4)]

        def dve_reads(key):
            return sum(1 for _, e in TILES[:TI[key] + 1] if e == "dve")

        def act_reads(key):
            return sum(1 for _, e in TILES[:TI[key] + 1] if e == "act")

        with nc.Block() as block:
            @block.sync
            def _(sp):
                loads_of_phase(sp, 4, l)

            @block.tensor
            def _(pe):
                acts = (oaT, obT, ocT)
                for hf in range(2):
                    for br in range(3):
                        wg, wo = open_slab(pe, f"mg{hf}{br}"), open_slab(pe, f"mo{hf}{br}")
                        for m in range(4):
                            proj_T(pe, ("mg", hf, br, m), lambda k: wg[:, k, m * P:(m + 1) * P], hT)
                            proj_T(pe, ("mo", hf, br, m), lambda k: wo[:, k, m * P:(m + 1) * P], acts[br])
                pe.wait_ge(sem("merged"), 16)
                for hf in range(2):
                    w = open_slab(pe, f"wo{hf}")
                    for m in range(4):
                        j = 4 * hf + m
                        proj_T(pe, ("wo", j), lambda k: w[:, k, m * P:(m + 1) * P], MG)
                        if j:
                            sum_tile(pe, "ffn", j - 1)
                sum_tile(pe, "ffn", KT - 1)

            @block.scalar
            def _(act):
                for i, (hf, br, m) in enumerate(mkeys):
                    wait_proj(act, ("mg", hf, br, m))
                    if i >= 3:
                        act.wait_ge(sem("proj_read_dve"), dve_reads(("mo",) + mkeys[i - 3]))
                    act.activation(two(SG[i % 3]), both(proj_pair(("mg", hf, br, m))), ACT.Sigmoid
                                   ).then_inc(sem("proj_read_act"), 1)
                for k in range(KT):
                    act.wait_ge(sem("proj_read_dve"), dve_reads(("wo", k)))
                    square_tile(act, "ffn", k)

            @block.vector
            def _(dve):
                for i, (hf, br, m) in enumerate(mkeys):
                    key, j = ("mo", hf, br, m), 4 * hf + m
                    wait_proj(dve, key)
                    dve.wait_ge(sem("proj_read_act"), act_reads(("mg", hf, br, m)))
                    dst = MG[:, j, :] if br == 0 else TMP
                    if i >= 5 and br:
                        dve.wait_ge(sem("merged"), 8 * hf + 4 * (br - 1) + m)
                    dve.tensor_tensor(two(dst), both(proj_pair(key)), two(SG[i % 3]), ALU.mult
                                      ).then_inc(sem("proj_read_dve"), 1)
                    if br:
                        dve.wait_ge(sem("proj_read_dve"), dve_reads(key))
                        dve.tensor_tensor(MG[:, j, :], MG[:, j, :], TMP, ALU.add).then_inc(sem("merged"), 1)
                for j in range(KT):
                    wait_proj(dve, ("wo", j))
                    dve.tensor_tensor(two(xT[:, j, :]), both(proj_pair(("wo", j))), two(xT[:, j, :]), ALU.add
                                      ).then_inc(sem("proj_read_dve"), 1)

        with nc.Block() as block:
            @block.sync
            def _(sp):
                loads_of_phase(sp, 5, l)

            @block.tensor
            def _(pe):
                for i in range(FT):
                    if i % 4 == 0:
                        wg, wu = open_slab(pe, f"fg{i // 4}"), open_slab(pe, f"fu{i // 4}")
                    cs = slice((i % 4) * P, (i % 4 + 1) * P)
                    proj_T(pe, ("fg", i), lambda k: wg[:, k, cs], hT, made="ffn_h" if i == 0 else None)
                    proj_T(pe, ("fu", i), lambda k: wu[:, k, cs], hT)
                pe.wait_ge(sem("proj_read_dve"), dve_reads(("fu", FT - 1)))
                for hf in range(2):
                    for r in range(0, FT, 8):
                        w = open_slab(pe, f"fd{hf}{r}")
                        rt = min(8, FT - r)
                        for m in range(4):
                            j = 4 * hf + m
                            if r == 0:
                                wait_proj_bank(pe, ("fd", j))
                            for half in range(2):
                                for k in range(rt):
                                    last = pe.matmul(pair[m][:, half, 0:HA], w[:, k, m * P:(m + 1) * P],
                                                     FA[:, r + k, half * HA:(half + 1) * HA],
                                                     start=(r + k == 0), stop=(r + k == FT - 1))
                            if r == 16:
                                last.then_inc(sem("proj_done"), 1)
                        if r < 16:
                            last.then_inc(sem("ffn_down_slab"), 1)

            @block.scalar
            def _(act):
                norm_root(act, "ffn", ms8)
                for i in range(FT):
                    wait_proj(act, ("fg", i))
                    if i >= 2:
                        act.wait_ge(sem("proj_read_dve"), dve_reads(("fu", i - 2)))
                    act.activation(two(SGF[i % 2]), both(proj_pair(("fg", i))), ACT.Silu
                                   ).then_inc(sem("proj_read_act"), 1)

            @block.vector
            def _(dve):
                own = Own(dve, sem("dve_own"), own_counts["dve"])
                norm_mean(dve, "ffn", ms8)
                norm_dve(dve, own, "ffn", ms8, "ffn")
                for i in range(FT):
                    wait_proj(dve, ("fu", i))
                    dve.wait_ge(sem("proj_read_act"), act_reads(("fg", i)))
                    dve.tensor_tensor(two(FA[:, i, :]), both(proj_pair(("fu", i))), two(SGF[i % 2]), ALU.mult
                                      ).then_inc(sem("proj_read_dve"), 1)
                for j in range(KT):
                    wait_proj(dve, ("fd", j))
                    dve.tensor_tensor(two(xT[:, j, :]), both(proj_pair(("fd", j))), two(xT[:, j, :]), ALU.add
                                      ).then_inc(sem("proj_read_dve"), 1)

        with nc.Block() as block:
            @block.sync
            def _(sp):
                sp.wait_ge(sem("win_moved"), 16)
        nums = sorted(s.num for s in sems.values())
        assert nums == list(range(nums[0], nums[-1] + 1)), nums
        nc.gpsimd.dma_reset()
        nc.gpsimd.sem_clear(range(nums[0], nums[-1] + 1))
        nc.all_engine_barrier()

    yr = arena[:, 0:5 * DM].rearrange("p (t n) -> p t n", t=5)
    y_turned, y_copied, y_out = sem("io_turned"), sem("io_copied"), sem("io_moved")
    with nc.Block() as block:
        @block.tensor
        def _(pe):
            for tt in range(NT + 1):
                if tt >= 4:
                    pe.wait_ge(y_copied, tt - 3)
                n = P if tt < NT else NB
                for k in range(KT):
                    last = pe.transpose(bank[2 * (tt % 4) + k // 4][0:n, (k % 4) * P:(k % 4 + 1) * P],
                                        xT[:, k, tt * P:tt * P + n], ident)
                last.then_inc(y_turned, 1)

        @block.vector
        def _(dve):
            for tt in range(NT + 1):
                n = P if tt < NT else NB
                dve.wait_ge(y_turned, tt + 1)
                dve.tensor_copy(yr[0:n, tt, :].rearrange("p (a b) -> p a b", a=2), pair[tt % 4][0:n, :, :]
                                ).then_inc(y_copied, 1)

        @block.sync
        def _(sp):
            for tt in range(NT + 1):
                sp.wait_ge(y_copied, tt + 1)
                dst = O["y_prompt"][0, tt * P:(tt + 1) * P, :] if tt < NT else O["y_sample"][:, 0, :]
                sp.dma_start(dst, yr[0:(P if tt < NT else NB), tt, :]).then_inc(y_out, 16)
            sp.wait_ge(y_out, 16 * (NT + 1))


_INS = ['x_prompt', 'x_sample', 'cache_cmp_kv', 'cache_slc_kv', 'cache_win_kv', 'state_gla', 'state_rglru',
        'state_conv', 'page_table', 'norm_mix_g', 'w_in', 'rg_conv_w', 'rg_conv_b', 'rg_w_a', 'rg_b_a', 'rg_w_x',
        'rg_b_x', 'rg_lambda', 'gla_w_a', 'gla_b_a', 'gla_norm_g', 'nsa_q_norm_g', 'nsa_k_norm_g', 'nsa_phi_k',
        'nsa_phi_v', 'nsa_cmp_pe', 'w_rg_out', 'w_gla_out', 'w_nsa_out', 'w_out', 'norm_ffn_g', 'w_ffn_gate',
        'w_ffn_up', 'w_ffn_down']
_OUTS = [('y_prompt', (1, T, DM)), ('y_sample', (NB, 1, DM)),
         ('p_cmp_kv', (L, 1, T, 2, G, DH)), ('p_slc_kv', (L, 1, T, 2, G, DH)), ('p_win_kv', (L, 1, WIN, 2, G, DH)),
         ('p_gla', (L, 1, GH, DK, DV)), ('p_rglru', (L, 1, DM)), ('p_conv', (L, 1, 3, DM)),
         ('s_cmp_kv', (L, NB, 1, 2, G, DH)), ('s_slc_kv', (L, NB, 1, 2, G, DH)), ('s_win_kv', (L, NB, WIN, 2, G, DH)),
         ('s_gla', (L, NB, GH, DK, DV)), ('s_rglru', (L, NB, DM)), ('s_conv', (L, NB, 3, DM))]


def kernel(**inputs):
    import numpy as _np
    import concourse.bacc as _bacc
    from concourse import mybir as _mybir
    from concourse.bass_utils import run_bass_kernel_spmd as _run

    nc = _bacc.Bacc("TRN2", target_bir_lowering=False, num_devices=1)
    con, lmask = constants()
    arrays, args, consts, outs = {}, {}, {}, {}
    for name, a in [(n, inputs[n]) for n in _INS] + [("con", con), ("lmask", lmask)]:
        a = _np.ascontiguousarray(a)
        arrays[f"in_{name}_dram"] = a
        where = consts if name in ("con", "lmask") else args
        where[name] = nc.dram_tensor(f"in_{name}_dram", a.shape, _mybir.dt.from_np(a.dtype), kind="ExternalInput").ap()
    for name, shape in _OUTS:
        outs[name] = nc.dram_tensor(f"out_{name}_dram", shape, _mybir.dt.from_np(_np.dtype("float32")),
                                    kind="ExternalOutput").ap()
    build(nc, args, outs, consts)
    r = _run(nc, [arrays], core_ids=[0])
    return tuple(r.results[0][f"out_{name}_dram"] for name, _ in _OUTS)
```
